# Optimizing a Trainium2 kernel written in Bass

```python
import math
import jax, jax.numpy as jnp
from jax import lax
import numpy as np

D_MODEL = 1024
BATCH = 1
SEQ = 512
DEPTH = 1

D_MIX = D_MODEL
DN_WIDTH = D_MIX // 2
DN_HEAD_K = 128
DN_HEAD_V = 128
DN_HEADS = DN_WIDTH // DN_HEAD_V
CONV_WIDTH = 4
CHUNK = 64
DF_WIDTH = D_MIX - DN_WIDTH
DF_HEAD_QK = 64
DF_HEAD_V = 2 * DF_HEAD_QK
DF_HEADS = DF_WIDTH // DF_HEAD_V
Q_BLOCK = 128
EPS = 1e-6

DN_QK = DN_HEADS * DN_HEAD_K
DN_V = DN_HEADS * DN_HEAD_V
DF_QK = DF_HEADS * 2 * DF_HEAD_QK
DF_V = DF_HEADS * DF_HEAD_V
COL_SIZES = (DN_QK, DN_QK, DN_V, DN_V, DN_HEADS, DN_HEADS, DF_QK, DF_QK, DF_V, DF_V)
IN_COLS = sum(COL_SIZES)
COL_OFFSETS = tuple(int(o) for o in np.cumsum(COL_SIZES)[:-1])


def rmsnorm(x, gain):
    xf = x.astype(jnp.float32)
    y = xf * lax.rsqrt(jnp.mean(xf * xf, axis=-1, keepdims=True) + EPS)
    return (y * gain.astype(jnp.float32)).astype(x.dtype)

def l2norm(x):
    return x * lax.rsqrt(jnp.sum(x * x, axis=-1, keepdims=True) + EPS)

def causal_depthwise_conv(x, w):
    c = x.shape[-1]
    return lax.conv_general_dilated(
        x, w[:, None, :].astype(x.dtype), window_strides=(1,),
        padding=[(CONV_WIDTH - 1, 0)], dimension_numbers=("NWC", "WIO", "NWC"),
        feature_group_count=c)

def gated_delta_rule(q, k, v, g, beta):
    b, t, h, dk = q.shape
    dv = v.shape[-1]
    n = t // CHUNK

    def chunks(a):
        a = jnp.moveaxis(a, 2, 1)
        return a.reshape((b, h, n, CHUNK) + a.shape[3:])

    qc, kc, vc = chunks(q), chunks(k), chunks(v)
    gc = jnp.cumsum(chunks(g), axis=-1)
    bc = chunks(beta)
    k_beta = kc * bc[..., None]
    v_beta = vc * bc[..., None]

    tril = jnp.tril(jnp.ones((CHUNK, CHUNK), bool))
    strict = jnp.tril(jnp.ones((CHUNK, CHUNK), bool), -1)
    diff = gc[..., :, None] - gc[..., None, :]
    decay = jnp.exp(jnp.where(tril, diff, -jnp.inf))

    m = jnp.where(strict, jnp.einsum('bhncd,bhnsd->bhncs', k_beta, kc) * decay, 0.0)
    lmat = m + jnp.eye(CHUNK, dtype=m.dtype)
    rhs = jnp.concatenate([v_beta, k_beta * jnp.exp(gc)[..., None]], axis=-1)
    sol = lax.linalg.triangular_solve(lmat, rhs, left_side=True, lower=True,
                                      unit_diagonal=True)
    u, w = sol[..., :dv], sol[..., dv:]
    a_qk = jnp.einsum('bhncd,bhnsd->bhncs', qc, kc) * decay

    def step(state, inp):
        q_i, k_i, u_i, w_i, g_i, a_i = inp
        v_new = u_i - jnp.einsum('bhcd,bhdv->bhcv', w_i, state)
        o_i = (jnp.einsum('bhcd,bhdv->bhcv', q_i * jnp.exp(g_i)[..., None], state)
               + jnp.einsum('bhcs,bhsv->bhcv', a_i, v_new))
        g_last = g_i[..., -1]
        k_dec = k_i * jnp.exp(g_last[..., None] - g_i)[..., None]
        state = (state * jnp.exp(g_last)[..., None, None]
                 + jnp.einsum('bhcd,bhcv->bhdv', k_dec, v_new))
        return state, o_i

    xs = tuple(jnp.moveaxis(a, 2, 0) for a in (qc, kc, u, w, gc, a_qk))
    s0 = jnp.zeros((b, h, dk, dv), jnp.float32)
    _, o = lax.scan(step, s0, xs)
    o = jnp.transpose(o, (1, 0, 3, 2, 4))
    return o.reshape(b, t, h, dv)

def gated_deltanet_group(q, k, v, z, bb, aa, conv_w, a_log, dt_bias, out_gain):
    b, t, _ = q.shape
    qkv = jax.nn.silu(causal_depthwise_conv(jnp.concatenate([q, k, v], -1), conv_w))
    q, k, v = jnp.split(qkv, [DN_QK, 2 * DN_QK], axis=-1)
    q = l2norm(q.reshape(b, t, DN_HEADS, DN_HEAD_K).astype(jnp.float32)) * (DN_HEAD_K ** -0.5)
    k = l2norm(k.reshape(b, t, DN_HEADS, DN_HEAD_K).astype(jnp.float32))
    v = v.reshape(b, t, DN_HEADS, DN_HEAD_V).astype(jnp.float32)
    beta = jax.nn.sigmoid(bb.astype(jnp.float32))
    g = -jnp.exp(a_log.astype(jnp.float32)) * jax.nn.softplus(
        aa.astype(jnp.float32) + dt_bias.astype(jnp.float32))
    o = gated_delta_rule(q, k, v, g, beta)
    zf = z.reshape(b, t, DN_HEADS, DN_HEAD_V).astype(jnp.float32)
    o = rmsnorm(o, out_gain) * jax.nn.silu(zf)
    return o.reshape(b, t, DN_V).astype(z.dtype)

def diff_attention_group(q, k, v, z, q_gain, k_gain, lq1, lk1, lq2, lk2, out_gain, lambda_init):
    b, t, _ = q.shape
    q = rmsnorm(q.reshape(b, t, DF_HEADS, 2, DF_HEAD_QK), q_gain) * (DF_HEAD_QK ** -0.5)
    k = rmsnorm(k.reshape(b, t, DF_HEADS, 2, DF_HEAD_QK), k_gain)
    v = v.reshape(b, t, DF_HEADS, DF_HEAD_V)
    lam = (jnp.exp(jnp.sum(lq1.astype(jnp.float32) * lk1.astype(jnp.float32)))
           - jnp.exp(jnp.sum(lq2.astype(jnp.float32) * lk2.astype(jnp.float32)))
           + lambda_init)
    nb = t // Q_BLOCK
    qb = jnp.moveaxis(q.reshape(b, nb, Q_BLOCK, DF_HEADS, 2, DF_HEAD_QK), 1, 0)
    starts = jnp.arange(nb, dtype=jnp.int32) * Q_BLOCK
    key_pos = jnp.arange(t, dtype=jnp.int32)
    neg = jnp.finfo(jnp.float32).min

    def block(args):
        q_blk, start = args
        s = jnp.einsum('bqhcd,bkhcd->bhcqk', q_blk, k).astype(jnp.float32)
        q_pos = start + jnp.arange(Q_BLOCK, dtype=jnp.int32)
        mask = key_pos[None, :] <= q_pos[:, None]
        p = jax.nn.softmax(jnp.where(mask, s, neg), axis=-1)
        wts = p[:, :, 0] - lam * p[:, :, 1]
        return jnp.einsum('bhqk,bkhv->bqhv', wts.astype(v.dtype), v)

    o = lax.map(block, (qb, starts))
    o = jnp.moveaxis(o, 0, 1).reshape(b, t, DF_HEADS, DF_HEAD_V)
    o = rmsnorm(o, out_gain).astype(jnp.float32) * (1.0 - lambda_init)
    zf = z.reshape(b, t, DF_HEADS, DF_HEAD_V).astype(jnp.float32)
    o = o * jax.nn.silu(zf)
    return o.reshape(b, t, DF_V).astype(z.dtype)

def first_inputs(seed: int = 0) -> dict:
    key = jax.random.key(seed)
    ks = jax.random.split(key, 16)
    f32 = jnp.float32
    x = jax.random.normal(ks[0], (BATCH, SEQ, D_MODEL), f32)
    norm_gain = 1.0 + 0.05 * jax.random.normal(ks[1], (DEPTH, D_MODEL), f32)
    w_in = jax.random.normal(ks[2], (DEPTH, D_MODEL, IN_COLS), f32) * D_MODEL ** -0.5
    conv_w = jax.random.normal(ks[3], (DEPTH, CONV_WIDTH, DN_QK * 2 + DN_V), f32) * CONV_WIDTH ** -0.5
    a_log = jnp.log(jax.random.uniform(ks[4], (DEPTH, DN_HEADS), f32, 1.0, 16.0))
    dt = jnp.exp(jax.random.uniform(ks[5], (DEPTH, DN_HEADS), f32,
                                    math.log(1e-3), math.log(1e-1)))
    dt_bias = dt + jnp.log(-jnp.expm1(-dt))
    dn_out_gain = 1.0 + 0.05 * jax.random.normal(ks[6], (DEPTH, DN_HEAD_V), f32)
    q_gain = 1.0 + 0.05 * jax.random.normal(ks[7], (DEPTH, DF_HEAD_QK), f32)
    k_gain = 1.0 + 0.05 * jax.random.normal(ks[8], (DEPTH, DF_HEAD_QK), f32)
    lambda_q1 = 0.1 * jax.random.normal(ks[9], (DEPTH, DF_HEAD_QK), f32)
    lambda_k1 = 0.1 * jax.random.normal(ks[10], (DEPTH, DF_HEAD_QK), f32)
    lambda_q2 = 0.1 * jax.random.normal(ks[11], (DEPTH, DF_HEAD_QK), f32)
    lambda_k2 = 0.1 * jax.random.normal(ks[12], (DEPTH, DF_HEAD_QK), f32)
    df_out_gain = 1.0 + 0.05 * jax.random.normal(ks[13], (DEPTH, DF_HEAD_V), f32)
    w_out = jax.random.normal(ks[14], (DEPTH, D_MIX, D_MODEL), f32) * D_MIX ** -0.5
    return {"x": x, "norm_gain": norm_gain, "w_in": w_in, "conv_w": conv_w,
            "a_log": a_log, "dt_bias": dt_bias, "dn_out_gain": dn_out_gain,
            "q_gain": q_gain, "k_gain": k_gain, "lambda_q1": lambda_q1,
            "lambda_k1": lambda_k1, "lambda_q2": lambda_q2, "lambda_k2": lambda_k2,
            "df_out_gain": df_out_gain, "w_out": w_out}

def first_block(x, norm_gain, w_in, conv_w, a_log, dt_bias, dn_out_gain, q_gain, k_gain,
              lambda_q1, lambda_k1, lambda_q2, lambda_k2, df_out_gain, w_out):
    for l in range(DEPTH):
        lambda_init = 0.8 - 0.6 * math.exp(-0.3 * l)
        h = rmsnorm(x, norm_gain[l])
        proj = jnp.einsum('btd,dc->btc', h, w_in[l])
        (dn_q, dn_k, dn_v, dn_z, dn_b, dn_a,
         df_q, df_k, df_v, df_z) = jnp.split(proj, COL_OFFSETS, axis=-1)
        o_dn = gated_deltanet_group(dn_q, dn_k, dn_v, dn_z, dn_b, dn_a, conv_w[l],
                                    a_log[l], dt_bias[l], dn_out_gain[l])
        o_df = diff_attention_group(df_q, df_k, df_v, df_z, q_gain[l], k_gain[l],
                                    lambda_q1[l], lambda_k1[l], lambda_q2[l], lambda_k2[l],
                                    df_out_gain[l], lambda_init)
        mixed = jnp.concatenate([o_dn, o_df], axis=-1)
        x = x + jnp.einsum('btc,cd->btd', mixed, w_out[l])
    return x


N_META = 16
D_FF = 2816
RET_HEADS = 4
RET_DK = 256
RET_DV = 512
RET_CHUNK = 128
ATT_HEADS = 8
ATT_DH = 128
IDX_HEADS = 8
IDX_DH = 64
TOPK_MAX = 256
DSA_QBLOCK = 32
ROPE_THETA = 10000.0
RET_QK = RET_HEADS * RET_DK
RET_V = RET_HEADS * RET_DV
ATT_W = ATT_HEADS * ATT_DH
IDX_Q = IDX_HEADS * IDX_DH
IN_SPLITS = (RET_QK, RET_QK, RET_V, RET_V, ATT_W, ATT_W, ATT_W, IDX_Q, IDX_DH, IDX_HEADS, D_MODEL, D_MODEL)
D_IN = sum(IN_SPLITS)


def rmsnorm_2(x, g):
    xf = x.astype(jnp.float32)
    y = xf * lax.rsqrt(jnp.mean(xf * xf, axis=-1, keepdims=True) + EPS)
    return (y * g.astype(jnp.float32)).astype(x.dtype)

def rope(x, pos):
    d = x.shape[-1]
    inv_freq = ROPE_THETA ** (-jnp.arange(0, d, 2, dtype=jnp.float32) / d)
    ang = pos.astype(jnp.float32)[:, None] * inv_freq[None, :]
    cos = jnp.cos(ang)[:, None, :]
    sin = jnp.sin(ang)[:, None, :]
    xf = x.astype(jnp.float32)
    x1, x2 = xf[..., : d // 2], xf[..., d // 2:]
    return jnp.concatenate([x1 * cos - x2 * sin, x2 * cos + x1 * sin], axis=-1).astype(x.dtype)

def swiglu(u, w_gate, w_up, w_down):
    return (jax.nn.silu(u @ w_gate) * (u @ w_up)) @ w_down

def retention(q, k, v):
    out_dtype = v.dtype
    q, k, v = (a.astype(jnp.float32) for a in (q, k, v))
    B, H, T, _ = q.shape
    C = RET_CHUNK
    n = (T - N_META) // C
    log_g = jnp.log1p(-(2.0 ** (-5.0 - jnp.arange(H, dtype=jnp.float32))))

    def decay_matrix(c):
        i = jnp.arange(c, dtype=jnp.float32)
        diff = i[:, None] - i[None, :]
        return jnp.where(diff >= 0, jnp.exp(log_g[:, None, None] * jnp.maximum(diff, 0.0)), 0.0)

    qm, km, vm = q[:, :, :N_META], k[:, :, :N_META], v[:, :, :N_META]
    y_meta = jnp.einsum('bhqk,bhke->bhqe', jnp.einsum('bhqd,bhkd->bhqk', qm, km) * decay_matrix(N_META), vm)
    zeta_m = jnp.exp(log_g[:, None] * (N_META - 1.0 - jnp.arange(N_META, dtype=jnp.float32)))
    state0 = jnp.einsum('bhkd,bhke->bhde', km * zeta_m[..., None], vm)

    d_in = decay_matrix(C)
    pos_c = jnp.arange(C, dtype=jnp.float32)
    xi = jnp.exp(log_g[:, None] * (pos_c + 1.0))[..., None]
    zeta = jnp.exp(log_g[:, None] * (C - 1.0 - pos_c))[..., None]
    g_chunk = jnp.exp(log_g * C)[:, None, None]

    def to_chunks(a):
        return a[:, :, N_META:].reshape(B, H, n, C, a.shape[-1]).transpose(2, 0, 1, 3, 4)

    def step(state, qkv):
        qc, kc, vc = qkv
        inner = jnp.einsum('bhqk,bhke->bhqe', jnp.einsum('bhqd,bhkd->bhqk', qc, kc) * d_in, vc)
        cross = jnp.einsum('bhqd,bhde->bhqe', qc, state) * xi
        state = g_chunk * state + jnp.einsum('bhkd,bhke->bhde', kc * zeta, vc)
        return state, inner + cross

    _, y_chunks = lax.scan(step, state0, (to_chunks(q), to_chunks(k), to_chunks(v)))
    y_real = y_chunks.transpose(1, 2, 0, 3, 4).reshape(B, H, n * C, v.shape[-1])
    y = jnp.concatenate([y_meta, y_real], axis=2)
    y = y * lax.rsqrt(jnp.mean(y * y, axis=-1, keepdims=True) + EPS)
    return y.astype(out_dtype)

def dsa_attention(q, k, v, qi, ki, wi, k_top):
    B, T, H, dh = q.shape
    nb = -(-T // DSA_QBLOCK)
    t_pad = nb * DSA_QBLOCK
    pad = t_pad - T

    def blocks(a):
        a = jnp.pad(a, [(0, 0), (0, pad)] + [(0, 0)] * (a.ndim - 2))
        return a.reshape((B, nb, DSA_QBLOCK) + a.shape[2:]).swapaxes(0, 1)

    pos_blocks = jnp.arange(t_pad, dtype=jnp.int32).reshape(nb, DSA_QBLOCK)
    key_pos = jnp.arange(T, dtype=jnp.int32)
    meta_pos = jnp.arange(N_META, dtype=jnp.int32)
    k_meta, v_meta = k[:, :N_META], v[:, :N_META]
    scale = ATT_DH ** -0.5
    idx_scale = (IDX_DH ** -0.5) * (IDX_HEADS ** -0.5)
    gather = jax.vmap(lambda a, i: a[i])

    def one_block(args):
        qb, qib, wib, tq = args
        rel = jax.nn.relu(jnp.einsum('bqhd,bsd->bqhs', qib, ki))
        score = jnp.einsum('bqh,bqhs->bqs', wib, rel).astype(jnp.float32) * idx_scale
        admissible = (key_pos[None, :] >= N_META) & (key_pos[None, :] <= tq[:, None])
        score = jnp.where(admissible[None], score, -jnp.inf)
        _, sel = lax.top_k(score, k_top)
        sel_ok = (sel >= N_META) & (sel <= tq[None, :, None])
        k_sel = gather(k, sel)
        v_sel = gather(v, sel)
        s_meta = jnp.einsum('bqhd,bmhd->bhqm', qb, k_meta).astype(jnp.float32) * scale
        s_meta = jnp.where((meta_pos[None, :] <= tq[:, None])[None, None], s_meta, -jnp.inf)
        s_sel = jnp.einsum('bqhd,bqkhd->bhqk', qb, k_sel).astype(jnp.float32) * scale
        s_sel = jnp.where(sel_ok[:, None], s_sel, -jnp.inf)
        p = jax.nn.softmax(jnp.concatenate([s_meta, s_sel], axis=-1), axis=-1).astype(v.dtype)
        return (jnp.einsum('bhqm,bmhd->bqhd', p[..., :N_META], v_meta)
                + jnp.einsum('bhqk,bqkhd->bqhd', p[..., N_META:], v_sel))

    out = lax.map(one_block, (blocks(q), blocks(qi), blocks(wi), pos_blocks))
    return out.swapaxes(0, 1).reshape(B, t_pad, H, dh)[:, :T]

def hybrid_mixer(u, pos, k_top, w_in, w_ret_out, w_att_out, w_mix_out):
    B, T, _ = u.shape
    proj = u @ w_in
    offs = [int(o) for o in np.cumsum(IN_SPLITS)[:-1]]
    rq, rk, rv, rg, aq, ak, av, iq, ik, iw, g_ret, g_att = jnp.split(proj, offs, axis=-1)
    rq = rope(rq.reshape(B, T, RET_HEADS, RET_DK), pos)
    rk = rope(rk.reshape(B, T, RET_HEADS, RET_DK), pos) * (RET_DK ** -0.5)
    rv = rv.reshape(B, T, RET_HEADS, RET_DV)
    yr = retention(rq.transpose(0, 2, 1, 3), rk.transpose(0, 2, 1, 3), rv.transpose(0, 2, 1, 3))
    yr = yr.transpose(0, 2, 1, 3).reshape(B, T, RET_V)
    yr = (jax.nn.silu(rg) * yr) @ w_ret_out
    aq = rope(aq.reshape(B, T, ATT_HEADS, ATT_DH), pos)
    ak = rope(ak.reshape(B, T, ATT_HEADS, ATT_DH), pos)
    av = av.reshape(B, T, ATT_HEADS, ATT_DH)
    iq = rope(iq.reshape(B, T, IDX_HEADS, IDX_DH), pos)
    ik = rope(ik.reshape(B, T, 1, IDX_DH), pos)[:, :, 0]
    ya = dsa_attention(aq, ak, av, iq, ik, iw, k_top).reshape(B, T, ATT_W) @ w_att_out
    merged = jax.nn.sigmoid(g_ret) * yr + jax.nn.sigmoid(g_att) * ya
    return merged @ w_mix_out

def second_inputs(seed: int = 0) -> dict:
    key = jax.random.key(seed)
    ks = jax.random.split(key, 16)
    f32 = jnp.float32

    def dense(k, fan_in, fan_out):
        return jax.random.normal(k, (DEPTH, fan_in, fan_out), f32) * fan_in ** -0.5

    def gain(k, shape):
        return 1.0 + 0.02 * jax.random.normal(k, shape, f32)

    return {
        'x': jax.random.normal(ks[0], (BATCH, SEQ, D_MODEL), f32),
        'meta_tokens': jax.random.normal(ks[1], (N_META, D_MODEL), f32),
        'ffn1_norm': gain(ks[2], (DEPTH, D_MODEL)),
        'ffn1_w_gate': dense(ks[3], D_MODEL, D_FF),
        'ffn1_w_up': dense(ks[4], D_MODEL, D_FF),
        'ffn1_w_down': dense(ks[5], D_FF, D_MODEL),
        'mix_norm': gain(ks[6], (DEPTH, D_MODEL)),
        'w_in': dense(ks[7], D_MODEL, D_IN),
        'w_ret_out': dense(ks[8], RET_V, D_MODEL),
        'w_att_out': dense(ks[9], ATT_W, D_MODEL),
        'w_mix_out': dense(ks[10], D_MODEL, D_MODEL),
        'ffn2_norm': gain(ks[11], (DEPTH, D_MODEL)),
        'ffn2_w_gate': dense(ks[12], D_MODEL, D_FF),
        'ffn2_w_up': dense(ks[13], D_MODEL, D_FF),
        'ffn2_w_down': dense(ks[14], D_FF, D_MODEL),
        'final_norm': gain(ks[15], (D_MODEL,)),
    }

def second_block(x, meta_tokens, ffn1_norm, ffn1_w_gate, ffn1_w_up, ffn1_w_down, mix_norm, w_in, w_ret_out, w_att_out, w_mix_out, ffn2_norm, ffn2_w_gate, ffn2_w_up, ffn2_w_down, final_norm):
    B, L, D = x.shape
    k_top = min(TOPK_MAX, L // 4)
    meta = jnp.broadcast_to(meta_tokens.astype(x.dtype)[None], (B, N_META, D))
    h = jnp.concatenate([meta, x], axis=1)
    pos = jnp.arange(h.shape[1], dtype=jnp.int32)
    for l in range(DEPTH):
        h = h + 0.5 * swiglu(rmsnorm_2(h, ffn1_norm[l]), ffn1_w_gate[l], ffn1_w_up[l], ffn1_w_down[l])
        h = h + hybrid_mixer(rmsnorm_2(h, mix_norm[l]), pos, k_top, w_in[l], w_ret_out[l], w_att_out[l], w_mix_out[l])
        h = h + 0.5 * swiglu(rmsnorm_2(h, ffn2_norm[l]), ffn2_w_gate[l], ffn2_w_up[l], ffn2_w_down[l])
    y = rmsnorm_2(h, final_norm)
    return y[:, N_META:]


def setup_inputs(seed=0):
    out = dict(first_inputs(seed))
    for name, value in second_inputs(seed + 1).items():
        if name != "x":
            out[name + "_2"] = value
    return out


def reference(
    x, norm_gain, w_in, conv_w, a_log, dt_bias, dn_out_gain, q_gain, k_gain, lambda_q1,
    lambda_k1, lambda_q2, lambda_k2, df_out_gain, w_out, meta_tokens_2, ffn1_norm_2,
    ffn1_w_gate_2, ffn1_w_up_2, ffn1_w_down_2, mix_norm_2, w_in_2, w_ret_out_2, w_att_out_2,
    w_mix_out_2, ffn2_norm_2, ffn2_w_gate_2, ffn2_w_up_2, ffn2_w_down_2, final_norm_2,
):
    x = first_block(
        x, norm_gain, w_in, conv_w, a_log, dt_bias, dn_out_gain, q_gain, k_gain, lambda_q1,
        lambda_k1, lambda_q2, lambda_k2, df_out_gain, w_out,
    )
    return second_block(
        x, meta_tokens_2, ffn1_norm_2, ffn1_w_gate_2, ffn1_w_up_2, ffn1_w_down_2, mix_norm_2,
        w_in_2, w_ret_out_2, w_att_out_2, w_mix_out_2, ffn2_norm_2, ffn2_w_gate_2, ffn2_w_up_2,
        ffn2_w_down_2, final_norm_2,
    )


_drawn_inputs = setup_inputs


def setup_inputs(seed=0):
    import zlib

    import numpy as np

    out = dict(_drawn_inputs(seed))
    spreads = {}
    factors = {'q_gain': 2.765,
     'k_gain': 3.041,
     'lambda_q1': 8.0,
     'lambda_k1': 8.0,
     'lambda_k2': 21.64,
     'df_out_gain': 2.93,
     'ffn1_norm_2': 5.893,
     'mix_norm_2': 4.23,
     'ffn2_norm_2': 7.811,
     'final_norm_2': 8.269,
     'lambda_q2': 3.98}
    for name, (base, spread) in spreads.items():
        noise = np.random.default_rng([zlib.crc32(name.encode()), seed]).standard_normal(out[name].shape)
        drawn = base * np.exp(spread * noise) if base else spread * noise
        out[name] = __import__('jax').numpy.asarray(drawn.astype(out[name].dtype))
    for name, factor in factors.items():
        out[name] = (out[name] * factor).astype(out[name].dtype)
    return out
```

```python
from contextlib import ExitStack

import numpy as np
import concourse.bass as bass
from concourse import mybir

F32 = mybir.dt.float32
F32R = mybir.dt.float32r
ALU = mybir.AluOpType
ACT = mybir.ActivationFunctionType
AX = mybir.AxisListType

P = 128
D = 1024
KD = D // P
T = 512
M = 16
TT = M + T
HALF = TT // 2
TQ = slice(M, TT)
NQ = T // P
EPS = 1e-6
NEG = -1.0e30

DN_H = 4
LAMBDA_INIT = 0.8 - 0.6 * 1.0
DF_H = 4
DF_STEPS = DF_H * NQ
CH = 64
D_FF = 2816
KF = D_FF // P
RET_H = 4
RET_DK = 256
ROPE_THETA = 10000.0
ATT_SCALE = 128 ** -0.5
IDX_SCALE = (64 ** -0.5) * (8 ** -0.5)
TAKEN = -3.0e38
ATT_H = 8
IDX_H = 8
K_TOP = 128
SLOTS = 4
RING = 4



def results():
    r = []
    add = lambda key, blocks=0: r.append((key, blocks))
    add(("norm", 0))
    add(("ab",), 1)
    for j in range(12):
        add(("qkv", j), 1)
    for j in range(4):
        add(("z", j), 1)
    for j in range(4):
        add(("dz", j), 1)
    for j in range(8):
        add(("dqk", j), 1)
    add(("dv", 0))
    add(("dv", 1), 4)
    for i in range(16):
        add(("hn", i))
    for n in range(NQ):
        for k in ("gcb", "beb", "sm", "N0", "A0", "T1"):
            add((k, n))
        for l in range(5):
            add(("Y", n, l))
            if l < 4:
                add(("dT", n, l))
            add(("dU", n, l))
        for k in ("kt", "vt", "u", "wT"):
            add((k, n))
        for c in range(2):
            if (n, c) != (0, 0):
                add(("wS", n, c))
            add(("o", n, c))
            if (n, c) != (NQ - 1, 1):
                add(("dS", n, c))
    add(("lam",))
    for s in range(DF_STEPS + 2):
        if s < DF_STEPS:
            add(("S", s // NQ, s % NQ))
        if 1 <= s <= DF_STEPS:
            add(("PT", (s - 1) // NQ, (s - 1) % NQ))
        if s >= 2:
            add(("PV", (s - 2) // NQ, (s - 2) % NQ))
    for i in range(8):
        add(("ho", i))
    for j in range(KD):
        add(("wo", j), 1)
    ffn_results(add, 1)
    add(("norm", 2))
    add(("ik",), 1)
    add(("iw",), 1)
    for j in range(4):
        add(("iq", j), 1)
    for n in range(1, NQ):
        for j in range(4):
            add(("is", n, j))
    for hg in range(2):
        for j in range(4):
            add(("aq", hg, j), 1)
        for j in range(4):
            add(("ak", hg, j), 1)
        add(("av", hg, 0))
        add(("av", hg, 1))
        add(("av", hg, 2), 4)
        for s in range(16 + 2):
            if s < 16:
                add(("AS", hg, s))
            if 1 <= s <= 16:
                add(("AP", hg, s - 1))
            if s >= 2:
                add(("AV", hg, s - 2))
    for j in range(KD):
        add(("ao", j), 1)
    for j in range(KD):
        add(("ga", j), 1)
    for hd in range(RET_H):
        for j in range(2):
            add(("rq", hd, j), 1)
        for j in range(2):
            add(("rk", hd, j), 1)
        add(("rv", hd, 0))
        add(("rv", hd, 1))
        add(("rv", hd, 2), 4)
        for j in range(4):
            add(("rg", hd, j), 1)
        for kt in range(NQ + 1):
            add(("rs", hd, kt))
        for d in range(4):
            add(("ry", hd, d))
        add(("rn", hd))
        for j in range(KD):
            add(("wr", hd, j), j % 2)
    for j in range(KD):
        add(("gr", j), 1)
    for j in range(KD):
        add(("mx", j), 1)
    ffn_results(add, 2)
    add(("norm", 4))
    return r


def ffn_results(add, i):
    add(("norm", 2 * i - 1))
    for f in range(KF):
        add(("gate", i, f), 1)
        add(("up", i, f), 1)
    for d in range(KD):
        add(("down", i, d), 3)


RESULTS = results()
ROTATED = [k for k, _ in RESULTS if k[0] in ("ik", "iq", "aq", "ak")]
NUMBER = {key: c for c, (key, _) in enumerate(RESULTS)}
BLOCK = {}
READY = {}
_b = _g = 0
for _key, _n in RESULTS:
    BLOCK[_key] = _b
    _b += _n
    if _n:
        READY[_key] = ("used", _b)
    elif _key[0] in ("dv", "av", "rv"):
        READY[_key] = ("used", _b + 4)
    else:
        _g += 1
        READY[_key] = ("result", _g)
BLOCKS = _b
BLOCKS_PADDED = -(-BLOCKS // RING) * RING

CONST = {}


def constants():
    i = np.arange(P)
    s, c = i[:, None], i[None, :]
    same = (s // CH) == (c // CH)
    parts = {
        "ident": s == c,
        "ones": s == s + 0 * c,
        "ones64": (s // 64) == (c // 64),
        "tri": same & (s <= c),
        "suffix": same & (s > c),
        "chunk0": (s < CH) & (c == c),
        "chunk1": (s >= CH) & (c == c),
        "strict": same & (s < c),
    }
    for l in range(6):
        w = 2 ** l
        parts[f"join{l}"] = (s // (2 * w) == c // (2 * w)) & (s % (2 * w) < w) & (c % (2 * w) >= w)
    causal = np.zeros((P, T), np.float32)
    causal[:, T - P:] = np.where(c > s, np.float32(NEG), np.float32(0))
    parts = {"ident": parts.pop("ident"), "ones": parts.pop("ones"), "causal": causal, **parts}
    out, at = [], 0
    for name, m in parts.items():
        CONST[name] = (at, at + m.shape[1])
        at += m.shape[1]
        out.append(np.broadcast_to(m, (P, m.shape[1])).astype(np.float32))
    return np.ascontiguousarray(np.concatenate(out, 1))


N_CONST = constants().shape[1]
N_KEPT = CONST["causal"][1]


def rotations():
    pos = np.arange(TT, dtype=np.float32)

    def table(d, copies, signed):
        inv = np.float32(ROPE_THETA) ** (-np.arange(0, d, 2, dtype=np.float32) / np.float32(d))
        angle = (pos[:, None] * inv[None, :].astype(np.float32)).astype(np.float32).T
        cos, sin = np.cos(angle), np.sin(angle)
        cos = np.concatenate([cos] * copies)
        sin = np.concatenate([sin * (-1 if signed and k % 2 == 0 else 1) for k in range(copies)])
        return [cos, sin]
    t = table(128, 2, True) + table(64, 4, True) + table(256, 1, False)
    return np.ascontiguousarray(np.stack(t).transpose(1, 0, 2).astype(np.float32))


def retention_decay():
    out = np.zeros((P, RET_H, 2, T), np.float64)
    k, q = np.arange(P)[:, None], np.arange(T)[None, :]
    for hd in range(RET_H):
        log_g = float(np.log1p(-np.float32(2.0 ** (-5.0 - hd))))
        out[:, hd, 0] = np.where(q >= k, np.exp(log_g * np.maximum(q - k, 0)), 0.0)
        out[:M, hd, 1] = np.exp(log_g * (q + M - k[:M]))
    return (out * RET_DK ** -0.5).astype(np.float32)

SMALL = {}
_at = 0
for _name, _w in (("norm_gain", 8), ("conv", 48), ("dn_gain", 1), ("q_gain", 1), ("k_gain", 1), ("df_gain", 1),
                  ("a_log", 4), ("dt_bias", 4), ("lq1", 1), ("lk1", 1), ("lq2", 1), ("lk2", 1),
                  ("f1_gain", 8), ("mix_gain", 8), ("f2_gain", 8), ("final_gain", 8)):
    SMALL[_name] = (_at, _at + _w)
    _at += _w
N_SMALL = _at


class Own:

    def __init__(self, engine, sem):
        self.engine, self.sem, self.count, self.last = engine, sem, 0, None

    def own(self, ins):
        self.count += 1
        ins.then_inc(self.sem, 1)
        self.last = (self.sem, self.count)

    def sig(self, ins, sem, value):
        ins.then_inc(sem, 1)
        self.last = (sem, value)

    def sync(self):
        self.engine.wait_ge(*self.last)


def build(nc, w_dram, x_dram, meta_dram, const_dram, small_dram, rot_dram, dec_dram, out_dram, dump=None, dump_dram=None):
    with ExitStack() as ctx:
        def sb(name, shape, dt=F32, scope=ctx):
            return scope.enter_context(nc.sbuf_tensor(name, shape, dt))

        def sem(name):
            return ctx.enter_context(nc.semaphore(name))

        w_raw = [sb(f"w_raw{i}", [P, 1024]) for i in range(RING)]
        w_hi = [sb(f"w_hi{i}", [P, 1024], F32R) for i in range(RING)]
        w_lo = [sb(f"w_lo{i}", [P, 1024], F32R) for i in range(RING)]
        h = sb("h", [P, KD, TT])
        const = sb("const", [P, N_KEPT])
        small = sb("small", [P, N_SMALL])
        eps = sb("eps", [P, 1])
        square = [sb(f"square{i}", [P, TT]) for i in range(2)]
        rs = [sb(f"rs{i}", [P, TT]) for i in range(2)]
        xt = [sb(f"xt{i}", [P, TT]) for i in range(2)]
        psum = [ctx.enter_context(nc.psum_tensor(f"slot{i}", [P, 1024], F32)) for i in range(SLOTS)]

        with ExitStack() as scope:
            DT, EG, qg, kb, AT, N, U, Tm, Ns, Y, kdec, kbg, Sd, u, wT, vnew = [
                sb(f"dn_{name}", [P, 4, P], F32, scope) for name in
                "decay expg qg kb attn n inv_t inv join y kdec kbg sdec u w_t vnew".split()]
            vb, gB, bB = DT, Y, Ns
        x_hi = sb("x_hi", [P, KD, TT], F32R)
        x_lo = sb("x_lo", [P, KD, TT], F32R)

        with ExitStack() as scope:
            fb = lambda name, shape, dt=F32: sb(name, shape, dt, scope)
            qkv = fb("qkv", [P, 12, T])
            sz = fb("sz", [P, 4, T])
            dsz = fb("dsz", [P, 4, T])
            dqk = fb("dqk", [P, 8, T])
            dv = fb("dv", [P, NQ, T])
            St = [fb(f"state{i}", [P, 4, P]) for i in range(2)]
            Sx = [[fb(f"score{i}{c}", [P, T]) for c in range(2)] for i in range(2)]
            Pm = [fb(f"prob{i}", [P, T]) for i in range(2)]
            PTs = [fb(f"prob_t{i}", [P, T]) for i in range(2)]
            mx = [fb(f"mx{i}", [P, 2]) for i in range(2)]
            sums_ = [fb(f"sum{i}", [P, 2]) for i in range(2)]
            ab = fb("ab", [P, NQ, 8])
            tA = fb("tA", [P, NQ, 4])
            tB = fb("tB", [P, NQ, 4])
            beta = fb("beta", [P, NQ, 4])
            g = fb("g", [P, NQ, 4])
            nea = fb("nea", [P, 4])
            sm = fb("sm", [P, 16])
            esm = fb("esm", [P, 16])
            cb = fb("cb", [P, 4])
            lamt = fb("lamt", [P, 8])
            const1 = fb("const1", [P, N_CONST - N_KEPT])

        with ExitStack() as scope:
            f_hi = sb("f_hi", [P, KF, TT], F32R, scope)
            f_lo = sb("f_lo", [P, KF, TT], F32R, scope)

        with ExitStack() as mix:
            mb = lambda name, shape, dt=F32, scope=mix: sb(name, shape, dt, scope)
            with ExitStack() as scope:
                aq = mb("aq", [P, 4, T], F32, scope)
                av = mb("av", [P, NQ, T], F32, scope)
            ya = mb("ya", [P, KD, T])
            with ExitStack() as att:
                bias = mb("bias", [P, NQ, TT], F32, att)
                at_rot = mb("at_rot", [P, 2, TT], F32, att)
                with ExitStack() as scope:
                    ix_rot = mb("ix_rot", [P, 2, TT], F32, scope)
                    iq = mb("iq", [P, 4, T], F32, scope)
                    ik = mb("ik", [P, T], F32, scope)
                    relu = [mb(f"relu{i}", [P, 2, T], F32, scope) for i in range(2)]
                    iw = mb("iw", [P, NQ, 8], F32, scope)
                with ExitStack() as scope:
                    att_hi = mb("att_hi", [P, ATT_H, T], F32R, scope)
                    att_lo = mb("att_lo", [P, ATT_H, T], F32R, scope)
                    avm = mb("av_meta", [P, T], F32, scope)
                    ak = mb("ak", [P, 4, TT], F32, scope)
                    Ax = [mb(f"att_score{i}", [P, TT], F32, scope) for i in range(2)]
                    Ap = Ax
                    At = [mb(f"att_prob_t{i}", [P, 5 * P], F32, scope) for i in range(2)]
                    amx = [mb(f"att_mx{i}", [P, 1], F32, scope) for i in range(2)]
                    asum = [mb(f"att_sum{i}", [P, 1], F32, scope) for i in range(2)]
                    score = [mb(f"ix_score{i}", [P, T], F32, scope) for i in range(3)]
                    top8 = mb("top8", [P, 3, 8], F32, scope)
            yr = mb("yr", [P, KD, T])
            rqk = mb("rqk", [P, 4, TT])
            rv = mb("rv", [P, NQ, T])
            rvm = mb("rv_meta", [P, T])
            rg = mb("rg", [P, 4, T])
            rst = mb("ret_score_t", [P, NQ, T])
            rstm = mb("ret_score_meta", [P, T])
            y_hi = mb("y_hi", [P, 4, T], F32R)
            y_lo = mb("y_lo", [P, 4, T], F32R)
            rt_rot = mb("rt_rot", [P, 2, TT])
            dec = mb("dec", [P, 2, T])

        s_small = sem("small_loaded")
        s_x = sem("x_loaded")
        s_raw = [sem(f"w_raw_loaded{i}") for i in range(RING)]
        s_hi = sem("w_hi_made")
        s_lo = sem("w_lo_made")
        s_used = sem("w_block_used")
        s_res = sem("result_ready")
        s_evac = [sem(f"evac{i}") for i in range(SLOTS)]
        s_eps = sem("eps_set")
        s_sq = sem("square_made")
        s_sqd = sem("square_used")
        s_rs = sem("rs_made")
        s_rsd = sem("rs_used")
        s_xt = sem("xt_made")
        s_xhi = sem("x_hi_made")
        s_xlo = sem("x_lo_made")
        s_v = sem("vector_order")
        s_a = sem("scalar_order")
        s_conv = sem("conv_made")
        s_silu = sem("silu_made")
        s_hn = sem("head_norm_applied")
        s_g = sem("g_beta")
        s_dn = sem("delta_vector")
        s_da = sem("delta_scalar")
        s_df = sem("diff_vector")
        s_dfp = sem("diff_prob")
        s_dfa = sem("diff_scalar")
        s_sg = sem("silu_gate")
        s_rot = sem("rotated_copy")
        s_ixt = sem("indexer_tables")
        s_relu = sem("relu_made")
        s_relud = sem("relu_used")
        s_af = sem("att_vector")
        s_afp = sem("att_prob")
        s_afa = sem("att_scalar")
        s_gate = sem("gate_made")
        s_ry = sem("ret_y_copied")
        s_dec = sem("decay_loaded")
        s_rst = sem("ret_score_decayed")
        s_y = sem("y_made")
        s_rotd = sem("ret_rotated")
        s_rtt = sem("ret_rotation_loaded")
        s_dump = sem("dumped")
        s_out = sem("out_stored")

        C = NUMBER

        def halves(ap):
            return ap.rearrange("p (a c) -> p a c", a=2)

        def ps_all(key):
            return halves(slot(key)[:])[:, :, 0:HALF]

        def evac_in(key, g):
            s_, v = evac_at(key)
            return s_, v + g

        def K(name):
            a, b = CONST[name]
            return const[:, a:b] if b <= N_KEPT else const1[:, a - N_KEPT:b - N_KEPT]

        def sml(name, j=0, w=1):
            a = SMALL[name][0] + j
            return small[:, a:a + w]

        def wait_result(eng, key):
            kind, value = READY[key]
            eng.wait_ge(s_used if kind == "used" else s_res, value)

        def wait_evac(eng, key):
            c = NUMBER[key]
            eng.wait_ge(s_evac[c % SLOTS], c // SLOTS + 1)

        def evac_at(key):
            c = NUMBER[key]
            return s_evac[c % SLOTS], c // SLOTS + 1

        def slot(key):
            return psum[NUMBER[key] % SLOTS]

        def heads(ap):
            return ap.rearrange("p (h c) -> p h c", h=4)

        DNV = ["gB", "dt", "qg", "U", "Ns0", "Ns1", "Ns2", "Ns3", "Ns4"]
        dnv = lambda name, n: n * len(DNV) + DNV.index(name) + 1

        block = ctx.enter_context(nc.Block())
        owners = []

        @block.sync
        def _(sp):
            for j in range(RING):
                sp.dma_start(w_raw[j][:], w_dram[0, j]).then_inc(s_raw[j], 16)
            with sp.Fori(1, BLOCKS_PADDED // RING) as i:
                for j in range(RING):
                    sp.wait_ge(s_lo, i * RING + (j + 1 - RING))
                    sp.dma_start(w_raw[j][:], w_dram[i, j]).then_inc(s_raw[j], 16)

        @block.scalar
        def _(act):
            A = Own(act, s_a)
            owners.append(A)
            made = {"w": 0, "sq": 0, "rs": 0, "x": 0}

            def w_split(upto):
                while made["w"] < min(upto + 1, BLOCKS_PADDED):
                    b = made["w"]
                    act.wait_ge(s_raw[b % RING], 16 * (b // RING + 1))
                    if b >= RING:
                        act.wait_ge(s_used, b - RING + 1)
                    nc.scalar.activation(w_hi[b % RING][:], w_raw[b % RING][:], ACT.Copy).then_inc(s_hi, 1)
                    made["w"] += 1

            def ahead(key, blocks=1):
                w_split(BLOCK[key] + blocks - 1 + RING - 1)

            def squares(srcs):
                for src in srcs:
                    q = made["sq"]
                    if q >= 2:
                        act.wait_ge(s_sqd, q - 1)
                    w = src.shape[-1]
                    nc.scalar.activation(square[q % 2][:, 0:w], src, ACT.Square).then_inc(s_sq, 1)
                    made["sq"] += 1

            def rsqrt(key, scale, w):
                r = made["rs"]
                if r >= 2:
                    act.wait_ge(s_rsd, r - 1)
                wait_result(act, key)
                if w == T:
                    src, dst = slot(key)[:, 0:T], rs[r % 2][:, 0:T]
                else:
                    src = slot(key)[:].rearrange("p (a c) -> p a c", a=2)[:, :, 0:HALF]
                    dst = rs[r % 2][:].rearrange("p (a c) -> p a c", a=2)
                A.sig(nc.scalar.activation(dst, src, ACT.Ln, bias=eps[:, 0:1], scale=scale), *evac_at(key))
                A.sync()
                A.sig(nc.scalar.activation(dst, dst, ACT.Exp, scale=-0.5), s_rs, r + 1)
                made["rs"] += 1

            def x_high(n, k0=0, c0=0, dst=x_hi):
                for k in range(k0, k0 + n):
                    m = made["x"]
                    act.wait_ge(s_xt, m + 1)
                    o = dst[:, k, c0:TT] if dst is x_hi else dst[:, k, :]
                    A.sig(nc.scalar.activation(o, xt[m % 2][:, c0:TT], ACT.Copy), s_xhi, m + 1)
                    made["x"] += 1

            def copy_out(key, dst, func=ACT.Copy, w=T):
                wait_result(act, key)
                src = slot(key)[:, 0:w] if w != TT else ps_all(key)
                A.sig(nc.scalar.activation(halves(dst) if w == TT else dst, src, func), *evac_at(key))

            def ffn(i, c0):
                width = TT if c0 == 0 else T
                squares([h[:, k, c0:TT] for k in range(KD)])
                rsqrt(("norm", 2 * i - 1), 1.0 / D, width)
                x_high(KD, c0=c0)
                b0, m0 = BLOCK[("gate", i, 0)], made["x"]
                w_split(b0 + RING - 2)
                act.wait_ge(s_sqd, made["sq"])

                def w_next(b, g, per):
                    b += RING - 1
                    act.wait_ge(s_raw[b % RING], g * (16 * per // RING) + 16 * (b // RING + 1))
                    act.wait_ge(s_used, g * per + (b - RING + 1))
                    nc.scalar.activation(w_hi[b % RING][:], w_raw[b % RING][:], ACT.Copy).then_inc(s_hi, 1)
                with act.Fori(0, KF // 2) as g:
                    for j in range(2):
                        gk = ("gate", i, j)
                        w_next(b0 + 2 * j, g, 4)
                        act.wait_ge(s_used, g * 4 + (b0 + 2 * j + 1))
                        if c0 == 0:
                            ins = nc.scalar.activation(halves(square[j][:]), ps_all(gk), ACT.Silu)
                        else:
                            ins = nc.scalar.activation(square[j][:, 0:T], slot(gk)[:, 0:T], ACT.Silu)
                        s_, v = evac_in(gk, g)
                        ins.then_inc(s_, 1)
                        w_next(b0 + 2 * j + 1, g, 4)
                        act.wait_ge(s_xt, g * 2 + (m0 + j + 1))
                        nc.scalar.activation(f_hi[:, g * 2 + j, c0:TT], xt[j][:, c0:TT], ACT.Copy).then_inc(s_xhi, 1)
                made["x"] += KF
                made["w"] += 2 * KF
                b1 = BLOCK[("down", i, 0)]
                assert made["w"] == b1 + RING - 1
                if i == 1:
                    with act.Fori(0, 2) as g:
                        for j in range(12):
                            w_next(b1 + j, g, 12)
                    made["w"] += 24
                else:
                    w_split(BLOCKS_PADDED - 1)
                act.wait_ge(s_xhi, made["x"])
                wait_evac(act, ("down", i, 7))
                act.wait_ge(s_evac[C[("down", i, 6)] % SLOTS], C[("down", i, 6)] // SLOTS + 1)

            act.dma_start(const[:], const_dram[:, 0:N_KEPT]).then_inc(s_small, 16)
            act.dma_start(const1[:], const_dram[:, N_KEPT:N_CONST]).then_inc(s_small, 16)
            act.dma_start(small[:], small_dram).then_inc(s_small, 16)
            act.dma_start(h[:, :, TQ], x_dram).then_inc(s_x, 16)
            act.dma_start(h[:, :, 0:M], meta_dram).then_inc(s_x, 16)
            w_split(RING - 2)
            act.wait_ge(s_x, 32)
            act.wait_ge(s_eps, 1)
            squares([h[:, k, TQ] for k in range(KD)])
            rsqrt(("norm", 0), 1.0 / D, T)
            x_high(KD, c0=M)
            ahead(("ab",))
            for j in range(12):
                key = ("qkv", j)
                ahead(key)
                wait_evac(act, key)
                nc.scalar.activation(qkv[:, j, :], qkv[:, j, :], ACT.Silu).then_inc(s_silu, 1)
            for j in range(4):
                ahead(("z", j))
                wait_result(act, ("z", j))
                nc.scalar.activation(sz[:, j, :], slot(("z", j))[:, 0:T], ACT.Silu).then_inc(evac_at(("z", j))[0], 1)
            for j in range(4):
                ahead(("dz", j))
                wait_result(act, ("dz", j))
                nc.scalar.activation(dsz[:, j, :], slot(("dz", j))[:, 0:T], ACT.Silu).then_inc(evac_at(("dz", j))[0], 1)
            for j in range(8):
                ahead(("dqk", j))
                wait_result(act, ("dqk", j))
                nc.scalar.activation(dqk[:, j, :], slot(("dqk", j))[:, 0:T], ACT.Copy).then_inc(evac_at(("dqk", j))[0], 1)
            w_split(BLOCK[("dv", 1)] + 3 + RING - 1 - 1)
            for i in range(2):
                wait_result(act, ("dv", i))
                A.sig(nc.scalar.activation(dv[:, 2 * i:2 * i + 2, :].rearrange("p a c -> p (a c)"), slot(("dv", i))[:, :], ACT.Copy), *evac_at(("dv", i)))
            w_split(BLOCK[("dv", 1)] + 3 + RING)
            A.sync()
            act.wait_ge(s_silu, 12)
            srcs = [qkv[:, j, :] for j in range(8)] + [dqk[:, j, :] for j in range(8)]
            squares(srcs[:1])
            for i in range(16):
                if i + 1 < 16:
                    squares(srcs[i + 1:i + 2])
                rsqrt(("hn", i), 1.0 if i < 8 else 1.0 / 64, T)
            act.wait_ge(s_g, 1)
            A.own(nc.scalar.activation(tA[:], tA[:], ACT.Exp, scale=-1.0))
            A.own(nc.scalar.activation(beta[:], ab[:, :, 0:4], ACT.Exp, scale=-1.0))
            A.sync()
            A.own(nc.scalar.activation(tA[:], tA[:], ACT.Ln, bias=1.0))
            A.sig(nc.scalar.activation(nea[:], sml("a_log", 0, 4), ACT.Exp), s_da, 1)
            da = [1]

            def dsig(ins):
                da[0] += 1
                A.sig(ins, s_da, da[0])
            for n in range(NQ):
                act.wait_ge(s_dn, dnv("dt", n))
                dsig(nc.scalar.activation(DT[:], DT[:], ACT.Exp))
                A.sig(nc.scalar.activation(EG[:].rearrange("p h c -> p (h c)"), slot(("gcb", n))[:, 0:T], ACT.Exp), *evac_at(("gcb", n)))
                wait_evac(act, ("sm", n))
                dsig(nc.scalar.activation(esm[:], sm[:], ACT.Exp))
                for l in range(5):
                    wait_result(act, ("Y", n, l))
                    A.sig(nc.scalar.activation(Y[:].rearrange("p h c -> p (h c)"), slot(("Y", n, l))[:, 0:T], ACT.Copy), *evac_at(("Y", n, l)))
                wait_result(act, ("u", n))
                A.sig(nc.scalar.activation(u[:].rearrange("p h c -> p (h c)"), slot(("u", n))[:, 0:T], ACT.Copy), *evac_at(("u", n)))
                for c in range(2):
                    wait_result(act, ("o", n, c))
                    A.sig(nc.scalar.activation(qkv[:, 0:4, n * P + c * CH:n * P + c * CH + CH],
                                         slot(("o", n, c))[:, 0:4 * CH].rearrange("p (h c) -> p h c", h=4), ACT.Copy), *evac_at(("o", n, c)))

            act.wait_ge(s_df, 1)
            wait_result(act, ("lam",))
            A.sig(nc.scalar.activation(lamt[:, 2:4], slot(("lam",))[:, 0:2], ACT.Exp), *evac_at(("lam",)))
            for s in range(DF_STEPS + 1):
                if s < DF_STEPS:
                    n, i = s % NQ, s % 2
                    w = (n + 1) * P
                    act.wait_ge(s_df, 2 + s)
                    for c in range(2):
                        A.sig(nc.scalar.activation(Sx[i][c][:, 0:w], Sx[i][c][:, 0:w], ACT.Exp, bias=mx[i][:, c:c + 1],
                                                   accum_out=sums_[i][:, c:c + 1]), s_dfa, 2 * s + c + 1)
                if s >= 1:
                    e = s - 1
                    j, n, i = e // NQ, e % NQ, e % 2
                    w = (n + 1) * P
                    if e >= 2:
                        wait_result(act, ("PV", (e - 2) // NQ, (e - 2) % NQ))
                    key = ("PT", j, n)
                    wait_result(act, key)
                    A.sig(nc.scalar.activation(PTs[i][:, 0:w], slot(key)[:, 0:w], ACT.Copy), *evac_at(key))
            wait_evac(act, ("PV", DF_H - 1, NQ - 1))
            A.sync()
            srcs = [qkv[:, j, :] for j in range(4)] + [dqk[:, j, :] for j in range(4)]
            squares(srcs[:1])
            for i in range(8):
                if i + 1 < 8:
                    squares(srcs[i + 1:i + 2])
                rsqrt(("ho", i), 1.0 / P, T)
                if i:
                    x_high(1, i - 1, M)
            x_high(1, 7, M)
            for j in range(8):
                ahead(("wo", j))
            wait_evac(act, ("wo", 7))
            ffn(1, 0)
            act.dma_start(at_rot[:], rot_dram[:, 0:2]).then_inc(s_ixt, 16)
            act.dma_start(ix_rot[:], rot_dram[:, 2:4]).then_inc(s_ixt, 16)
            squares([h[:, k, :] for k in range(KD)])
            rsqrt(("norm", 2), 1.0 / D, TT)
            x_high(KD)
            rot = [0]

            def rotate(key, half, w):
                i = rot[0]
                wait_result(act, key)
                if i >= 2:
                    wait_evac(act, ROTATED[i - 2])
                else:
                    act.wait_ge(s_sqd, made["sq"])
                for p in range(0, P, 2 * half):
                    for a, b in ((p, p + half), (p + half, p)):
                        if w == T:
                            ins = nc.scalar.activation(square[i % 2][a:a + half, 0:T], slot(key)[b:b + half, 0:T], ACT.Copy)
                        else:
                            ins = nc.scalar.activation(halves(square[i % 2][:])[a:a + half], ps_all(key)[b:b + half], ACT.Copy)
                        A.own(ins) if (p, a) != (P - 2 * half, P - half) else A.sig(ins, s_rot, i + 1)
                rot[0] += 1
            ahead(("ik",))
            rotate(("ik",), 32, T)
            ahead(("iw",))
            for j in range(4):
                ahead(("iq", j))
                rotate(("iq", j), 32, T)
            for s in range(12):
                key = ("is", 1 + s // 4, s % 4)
                w = (1 + s // 4 + 1) * P
                if s >= 2:
                    act.wait_ge(s_relud, s - 1)
                wait_result(act, key)
                A.sig(nc.scalar.activation(relu[s % 2][:, :, 0:w], slot(key)[:].rearrange("p (a c) -> p a c", a=2)[:, :, 0:w],
                                           ACT.Relu), *evac_at(key))
            for hg in range(2):
                for j in range(4):
                    ahead(("aq", hg, j))
                    rotate(("aq", hg, j), 64, T)
                for j in range(4):
                    ahead(("ak", hg, j))
                    rotate(("ak", hg, j), 64, TT)
                w_split(BLOCK[("av", hg, 2)] + 3 + 2)
                for i in range(2):
                    wait_result(act, ("av", hg, i))
                    A.sig(nc.scalar.activation(av[:, 2 * i:2 * i + 2, :].rearrange("p a c -> p (a c)"),
                                               slot(("av", hg, i))[:, :], ACT.Copy), *evac_at(("av", hg, i)))
                A.sig(nc.scalar.activation(avm[0:M, :], slot(("av", hg, 2))[0:M, 0:T], ACT.Copy), *evac_at(("av", hg, 2)))
                w_split(BLOCK[("av", hg, 2)] + 3 + 3)
                for s in range(17):
                    if s < 16:
                        n, i = s % NQ, s % 2
                        w = M + (n + 1) * P
                        act.wait_ge(s_af, 16 * hg + s + 1)
                        A.sig(nc.scalar.activation(Ax[i][:, 0:w], Ax[i][:, 0:w], ACT.Exp, bias=amx[i][:, 0:1], scale=ATT_SCALE,
                                                   accum_out=asum[i][:, 0:1]), s_afa, 16 * hg + s + 1)
                    if s >= 1:
                        e = s - 1
                        n, i = e % NQ, e % 2
                        if e >= 2:
                            wait_result(act, ("AV", hg, e - 2))
                        key = ("AP", hg, e)
                        wait_result(act, key)
                        A.own(nc.scalar.activation(At[i][0:M, 0:P], slot(key)[0:M, 0:P], ACT.Copy))
                        A.sig(nc.scalar.activation(At[i][:, P:P + (n + 1) * P], slot(key)[:, P:P + (n + 1) * P], ACT.Copy), *evac_at(key))
                x_high(4, 4 * hg, M, att_hi)
            for j in range(KD):
                ahead(("ao", j))
                copy_out(("ao", j), ya[:, j, :])
            def sigmoid(key, i):
                if i >= 2:
                    act.wait_ge(s_gate, i - 1)
                wait_result(act, key)
                A.sig(nc.scalar.activation(square[i % 2][:, 0:T], slot(key)[:, 0:T], ACT.Sigmoid), *evac_at(key))
            for j in range(KD):
                ahead(("ga", j))
                sigmoid(("ga", j), j)
            act.wait_ge(s_gate, KD)
            act.dma_start(rt_rot[:], rot_dram[:, 4:6]).then_inc(s_rtt, 16)
            for hd in range(RET_H):
                if hd:
                    act.wait_ge(s_rst, 5 * hd)
                act.dma_start(dec[:], dec_dram[:, hd]).then_inc(s_dec, 16)
                for j in range(4):
                    key = ("rq", hd, j) if j < 2 else ("rk", hd, j - 2)
                    ahead(key)
                    if j % 2 == 0 and (hd or j):
                        act.wait_ge(s_rotd, (2 * hd + j // 2))
                    dst = square[j % 2][:, 0:T] if j < 2 else square[j % 2][:]
                    copy_out(key, dst, w=T if j < 2 else TT)
                w_split(BLOCK[("rv", hd, 2)] + 3 + 2)
                for i in range(2):
                    wait_result(act, ("rv", hd, i))
                    A.sig(nc.scalar.activation(rv[:, 2 * i:2 * i + 2, :].rearrange("p a c -> p (a c)"),
                                               slot(("rv", hd, i))[:, :], ACT.Copy), *evac_at(("rv", hd, i)))
                A.sig(nc.scalar.activation(rvm[0:M, :], slot(("rv", hd, 2))[0:M, 0:T], ACT.Copy), *evac_at(("rv", hd, 2)))
                for j in range(4):
                    ahead(("rg", hd, j))
                    copy_out(("rg", hd, j), rg[:, j, :], ACT.Silu)
                w_split(BLOCK[("rg", hd, 3)] + 1 + 3)
                act.wait_ge(s_rst, 5 * hd + 5)
                for d in range(4):
                    copy_out(("ry", hd, d), rqk[:, d, 0:T])
                    A.sync()
                    squares([rqk[:, d, 0:T]])
                rsqrt(("rn", hd), 1.0 / T, T)
                x_high(4, 0, M, y_hi)
                for j in range(KD):
                    ahead(("wr", hd, j))
            for j in range(KD):
                ahead(("gr", j))
                sigmoid(("gr", j), KD + j)
            x_high(KD, c0=M)
            for j in range(KD):
                ahead(("mx", j))
            wait_evac(act, ("mx", KD - 1))
            ffn(2, M)
            squares([h[:, k, TQ] for k in range(KD)])
            rsqrt(("norm", 4), 1.0 / D, T)
            act.wait_ge(s_y, KD)
            act.dma_start(out_dram, h[:, :, TQ]).then_inc(s_out, 16)
            act.wait_ge(s_out, 16)

        @block.vector
        def _(dve):
            V = Own(dve, s_v)
            owners.append(V)
            made = {"rs": 0, "x": 0}

            def split(makers, c0=0, k0=0, hi=x_hi, lo=x_lo):
                d0 = c0 if hi is x_hi else 0

                def low(m, k):
                    dve.wait_ge(s_xhi, m + 1)
                    V.sig(nc.vector.tensor_tensor(lo[:, k, d0:], xt[m % 2][:, c0:TT],
                                                  hi[:, k, d0:].bitcast(F32), ALU.subtract), s_xlo, m + 1)
                for i, maker in enumerate(makers):
                    m = made["x"]
                    if i >= 2:
                        V.sync()
                    maker(xt[m % 2][:, c0:TT], m)
                    made["x"] += 1
                    if i:
                        low(m - 1, k0 + i - 1)
                low(made["x"] - 1, k0 + len(makers) - 1)

            def model_norm(gain, c0):
                r = made["rs"]
                dve.wait_ge(s_rs, r + 1)
                split([lambda dst, m, k=k: V.sig(nc.vector.scalar_tensor_tensor(
                    dst, h[:, k, c0:TT], sml(gain, k), rs[r % 2][:, 0:TT - c0], ALU.mult, ALU.mult), s_xt, m + 1)
                    for k in range(KD)], c0)
                V.sync()
                dve.sem_inc(s_rsd, 1)
                made["rs"] += 1

            V.sig(nc.vector.memset(eps[:], EPS), s_eps, 1)
            dve.wait_ge(s_small, 48)
            dve.wait_ge(s_x, 32)
            model_norm("norm_gain", M)
            key = ("ab",)
            wait_result(dve, key)
            V.sig(nc.vector.tensor_copy(ab[:].rearrange("p n c -> p (n c)"), slot(key)[:, 0:NQ * 8]), *evac_at(key))
            V.sync()
            dtb = sml("dt_bias", 0, 4).unsqueeze(1).broadcast_to([P, NQ, 4])
            V.own(nc.vector.tensor_tensor(g[:], ab[:, :, 4:8], dtb, ALU.add))
            V.sync()
            V.own(nc.vector.tensor_scalar(tA[:], g[:], -1.0, None, ALU.mult))
            V.sync()
            V.own(nc.vector.tensor_tensor(tA[:], tA[:], g[:], ALU.max))
            V.sync()
            V.sig(nc.vector.tensor_scalar(tB[:], g[:], 0.0, None, ALU.max), s_g, 1)
            for j in range(12):
                key = ("qkv", j)
                wait_result(dve, key)
                ps = slot(key)
                cw = lambda i: sml("conv", 4 * j + i)
                V.own(nc.vector.tensor_scalar(qkv[:, j, :], ps[:, 0:T], cw(3), None, ALU.mult))
                for i in (1, 2, 3):
                    V.sync()
                    ins = nc.vector.scalar_tensor_tensor(qkv[:, j, i:T], ps[:, 0:T - i], cw(3 - i), qkv[:, j, i:T],
                                                         ALU.mult, ALU.add)
                    if i < 3:
                        V.own(ins)
                    else:
                        V.sig(ins, *evac_at(key))
            for i in range(16):
                r = made["rs"]
                dve.wait_ge(s_rs, r + 1)
                if i < 8:
                    t, gain, const_s = qkv[:, i, :], (P ** -0.5 if i < 4 else 1.0), None
                    V.sig(nc.vector.scalar_tensor_tensor(t, t, gain, rs[r % 2][:, 0:T], ALU.mult, ALU.mult), s_rsd, r + 1)
                else:
                    t = dqk[:, i - 8, :]
                    gain = sml("q_gain" if i < 12 else "k_gain")
                    V.sig(nc.vector.scalar_tensor_tensor(t, t, gain, rs[r % 2][:, 0:T], ALU.mult, ALU.mult), s_rsd, r + 1)
                    if i < 12:
                        V.sync()
                        V.own(nc.vector.tensor_scalar(t, t, 64 ** -0.5, None, ALU.mult))
                made["rs"] += 1
            dve.wait_ge(s_da, 1)
            V.own(nc.vector.tensor_tensor(tB[:], tB[:], tA[:], ALU.add))
            V.own(nc.vector.tensor_scalar(beta[:], beta[:], 1.0, None, ALU.add))
            V.sync()
            V.own(nc.vector.reciprocal(beta[:], beta[:]))
            V.own(nc.vector.scalar_tensor_tensor(g[:], tB[:], -1.0, nea[:].unsqueeze(1).broadcast_to([P, NQ, 4]), ALU.mult, ALU.mult))
            V.sync()
            dn = [0]

            def dsig(ins, name, n):
                dn[0] += 1
                assert dn[0] == dnv(name, n), (name, n)
                V.sig(ins, s_dn, dn[0])

            def per_token(ap):
                return ap.unsqueeze(2).broadcast_to([P, 4, P])

            def per_head(name):
                return K(name).unsqueeze(1).broadcast_to([P, 4, P])
            for n in range(NQ):
                tok = slice(n * P, n * P + P)
                V.sync()
                if n:
                    wait_result(dve, ("beb", n - 1))
                V.own(nc.vector.tensor_copy(bB[:], per_token(beta[:, n, :])))
                dsig(nc.vector.tensor_copy(gB[:], per_token(g[:, n, :])), "gB", n)
                wait_result(dve, ("sm", n))
                V.sig(nc.vector.tensor_copy(sm[:], slot(("sm", n))[:, 0:16]), *evac_at(("sm", n)))
                V.sync()
                for hd in range(4):
                    ins = nc.vector.tensor_scalar(DT[:, hd, :], slot(("gcb", n))[:, hd * P:hd * P + P], sm[:, hd:hd + 1], 0.0,
                                                  ALU.subtract, ALU.min)
                    if hd < 3:
                        V.own(ins)
                    else:
                        dsig(ins, "dt", n)
                V.sig(nc.vector.tensor_tensor(kb[:], qkv[:, 4:8, tok], heads(slot(("beb", n))[:, 0:T]), ALU.mult), *evac_at(("beb", n)))
                wait_evac(dve, ("gcb", n))
                V.own(nc.vector.tensor_tensor(DT[:], DT[:], per_head("tri"), ALU.mult))
                dsig(nc.vector.tensor_tensor(qg[:], qkv[:, 0:4, tok], EG[:], ALU.mult), "qg", n)
                wait_result(dve, ("N0", n))
                V.sync()
                V.sig(nc.vector.tensor_tensor(N[:], heads(slot(("N0", n))[:, 0:T]), DT[:], ALU.mult), *evac_at(("N0", n)))
                V.sync()
                V.own(nc.vector.tensor_tensor(N[:], N[:], per_head("strict"), ALU.mult))
                V.sync()
                V.own(nc.vector.tensor_tensor(U[:], N[:], per_head("join0"), ALU.mult))
                V.sync()
                dsig(nc.vector.scalar_tensor_tensor(U[:].rearrange("p h c -> p h c"), U[:], -1.0, per_head("ident"), ALU.mult, ALU.add), "U", n)
                wait_result(dve, ("A0", n))
                V.sig(nc.vector.tensor_tensor(AT[:], heads(slot(("A0", n))[:, 0:T]), DT[:], ALU.mult), *evac_at(("A0", n)))
                wait_result(dve, ("T1", n))
                V.sig(nc.vector.tensor_copy(Tm[:].rearrange("p h c -> p (h c)"), slot(("T1", n))[:, 0:T]), *evac_at(("T1", n)))
                V.sync()
                for l in range(5):
                    dsig(nc.vector.tensor_tensor(Ns[:], N[:], per_head(f"join{l + 1}"), ALU.mult), f"Ns{l}", n)
                    wait_result(dve, ("dU", n, l))
                    if l < 4:
                        V.sig(nc.vector.tensor_tensor(Tm[:], Tm[:], heads(slot(("dT", n, l))[:, 0:T]), ALU.subtract), *evac_at(("dT", n, l)))
                    V.sig(nc.vector.tensor_tensor(U[:], U[:], heads(slot(("dU", n, l))[:, 0:T]), ALU.subtract), *evac_at(("dU", n, l)))
                    V.sync()
                dve.wait_ge(s_da, 1 + 2 * n + 2)
                V.own(nc.vector.tensor_tensor(cb[:], esm[:, 0:4], beta[:, n, :], ALU.mult))
                wait_result(dve, ("kt", n))
                V.sync()
                V.own(nc.vector.tensor_tensor(kdec[:], heads(slot(("kt", n))[:, 0:T]), per_token(esm[:, 4:8]), ALU.mult))
                V.sig(nc.vector.tensor_tensor(kbg[:], heads(slot(("kt", n))[:, 0:T]), per_token(cb[:]), ALU.mult), *evac_at(("kt", n)))
                wait_result(dve, ("vt", n))
                V.sig(nc.vector.tensor_tensor(vb[:], heads(slot(("vt", n))[:, 0:T]), per_token(beta[:, n, :]), ALU.mult), *evac_at(("vt", n)))
                wait_result(dve, ("wT", n))
                V.sig(nc.vector.tensor_copy(wT[:].rearrange("p h c -> p (h c)"), slot(("wT", n))[:, 0:T]), *evac_at(("wT", n)))
                wait_evac(dve, ("u", n))
                for c in range(2):
                    rr = slice(c * CH, c * CH + CH)
                    i = 2 * n + c
                    old, new = St[i % 2], St[(i + 1) % 2]
                    if i:
                        wait_result(dve, ("wS", n, c))
                        V.sig(nc.vector.tensor_tensor(vnew[rr], u[rr], heads(slot(("wS", n, c))[rr, 0:T]), ALU.subtract), *evac_at(("wS", n, c)))
                    if i == 2 * NQ - 1:
                        continue
                    if i:
                        V.own(nc.vector.tensor_tensor(Sd[:], old[:], per_token(esm[:, 8 + 4 * c:12 + 4 * c]), ALU.mult))
                        V.sync()
                    wait_result(dve, ("dS", n, c))
                    if i:
                        V.sig(nc.vector.tensor_tensor(new[:], Sd[:], heads(slot(("dS", n, c))[:, 0:T]), ALU.add), *evac_at(("dS", n, c)))
                    else:
                        V.sig(nc.vector.tensor_copy(new[:].rearrange("p h c -> p (h c)"), slot(("dS", n, c))[:, 0:T]), *evac_at(("dS", n, c)))
                    V.sync()
            V.own(nc.vector.tensor_tensor(lamt[0:64, 0:1], sml("lq1")[0:64], sml("lk1")[0:64], ALU.mult))
            V.sig(nc.vector.tensor_tensor(lamt[0:64, 1:2], sml("lq2")[0:64], sml("lk2")[0:64], ALU.mult), s_df, 1)
            wait_evac(dve, ("lam",))
            V.own(nc.vector.scalar_tensor_tensor(lamt[:, 4:5], lamt[:, 2:3], LAMBDA_INIT, lamt[:, 3:4], ALU.add, ALU.subtract))
            V.sync()
            V.own(nc.vector.tensor_scalar(lamt[:, 5:6], lamt[:, 4:5], -1.0, None, ALU.mult))
            for s in range(DF_STEPS + 2):
                if s < DF_STEPS:
                    j, n, i = s // NQ, s % NQ, s % 2
                    w = (n + 1) * P
                    key = ("S", j, n)
                    wait_result(dve, key)
                    for c in range(2):
                        ins = nc.vector.tensor_tensor_reduce(Sx[i][c][:, 0:w], slot(key)[:, c * 512:c * 512 + w],
                                                             K("causal")[:, T - w:T], 1.0, NEG, ALU.add, ALU.max, mx[i][:, c:c + 1])
                        V.own(ins) if c == 0 else V.sig(ins, *evac_at(key))
                    V.sync()
                    V.sig(nc.vector.tensor_scalar(mx[i][:], mx[i][:], -1.0, None, ALU.mult), s_df, 2 + s)
                if 1 <= s <= DF_STEPS:
                    e = s - 1
                    j, n, i = e // NQ, e % NQ, e % 2
                    w = (n + 1) * P
                    dve.wait_ge(s_dfa, 2 * e + 2)
                    V.own(nc.vector.reciprocal(sums_[i][:], sums_[i][:]))
                    V.sync()
                    V.own(nc.vector.tensor_scalar(sums_[i][:, 1:2], sums_[i][:, 1:2], lamt[:, 5:6], None, ALU.mult))
                    V.sync()
                    V.own(nc.vector.tensor_scalar(Sx[i][1][:, 0:w], Sx[i][1][:, 0:w], sums_[i][:, 1:2], None, ALU.mult))
                    V.sync()
                    if e >= 2:
                        wait_result(dve, ("PT", (e - 2) // NQ, (e - 2) % NQ))
                    V.sig(nc.vector.scalar_tensor_tensor(Pm[i][:, 0:w], Sx[i][0][:, 0:w], sums_[i][:, 0:1], Sx[i][1][:, 0:w],
                                                         ALU.mult, ALU.add), s_dfp, e + 1)
                if s >= 2:
                    e = s - 2
                    j, n = e // NQ, e % NQ
                    key = ("PV", j, n)
                    wait_result(dve, key)
                    V.sig(nc.vector.tensor_copy(dqk[:, j, n * P:n * P + P], slot(key)[:, 0:P]), *evac_at(key))
            def head_out(i):
                t = qkv[:, i, :] if i < 4 else dqk[:, i - 4, :]

                def maker(dst, m):
                    r = made["rs"]
                    dve.wait_ge(s_rs, r + 1)
                    V.own(nc.vector.scalar_tensor_tensor(dst, t, sml("dn_gain" if i < 4 else "df_gain"), rs[r % 2][:, 0:T],
                                                         ALU.mult, ALU.mult))
                    V.sync()
                    dve.sem_inc(s_rsd, 1)
                    made["rs"] += 1
                    z = sz[:, i, :] if i < 4 else dsz[:, i - 4, :]
                    V.sig(nc.vector.scalar_tensor_tensor(dst, dst, 1.0 if i < 4 else 1.0 - LAMBDA_INIT, z, ALU.mult, ALU.mult), s_xt, m + 1)
                return maker
            split([head_out(i) for i in range(8)], c0=M)

            def add_to_h(key):
                wait_result(dve, key)
                V.sig(nc.vector.tensor_tensor(h[:, key[-1], TQ], h[:, key[-1], TQ], slot(key)[:, 0:T], ALU.add), *evac_at(key))
            for j in range(KD):
                add_to_h(("wo", j))

            def ffn(i, c0):
                V.sync()
                model_norm(f"f{i}_gain", c0)
                b0, m0 = BLOCK[("gate", i, 0)], made["x"]
                wide = c0 == 0
                with dve.Fori(0, KF // 2) as g:
                    for j in range(2):
                        up = ("up", i, j)
                        dve.wait_ge(s_used, g * 4 + (b0 + 2 * j + 2))
                        s_, v = evac_in(("gate", i, j), g)
                        dve.wait_ge(s_, v)
                        dve.wait_ge(s_xlo, g * 2 + (m0 + j))
                        s_, v = evac_in(up, g)
                        a, b, o = square[j][:, 0:TT - c0], slot(up)[:, 0:T], xt[j][:, c0:TT]
                        if wide:
                            a, b, o = halves(a), ps_all(up), halves(o)
                        ins = nc.vector.tensor_tensor(o, a, b, ALU.mult)
                        ins.then_inc(s_, 1)
                        dve.wait_ge(s_, v)
                        dve.sem_inc(s_xt, 1)
                        dve.wait_ge(s_xhi, g * 2 + (m0 + j + 1))
                        nc.vector.tensor_tensor(f_lo[:, g * 2 + j, c0:TT], xt[j][:, c0:TT],
                                                f_hi[:, g * 2 + j, c0:TT].bitcast(F32), ALU.subtract).then_inc(s_xlo, 1)
                made["x"] += KF
                b1 = BLOCK[("down", i, 0)]
                with dve.Fori(0, 2) as g:
                    for j in range(4):
                        key = ("down", i, j)
                        dve.wait_ge(s_used, g * 12 + (b1 + 3 * j + 3))
                        hh = h[:, g * 4 + j, c0:TT]
                        src = slot(key)[:, 0:T]
                        if wide:
                            hh, src = halves(hh), ps_all(key)
                        s_, v = evac_in(key, g)
                        nc.vector.scalar_tensor_tensor(hh, src, 0.5, hh, ALU.mult, ALU.add).then_inc(s_, 1)
                V.last = evac_at(("down", i, KD - 1))
                V.sync()
            ffn(1, 0)
            model_norm("mix_gain", 0)
            rot = [0]
            dve.wait_ge(s_ixt, 32)

            def rotated(key, table, dst, w):
                i = rot[0]
                c0 = TT - w
                dve.wait_ge(s_rot, i + 1)
                src = slot(key)[:, 0:T] if w == T else ps_all(key)
                tab = lambda k: table[:, k, c0:TT] if w == T else halves(table[:, k, :])
                d = dst if w == T else halves(dst)
                other = square[i % 2][:, 0:T] if w == T else halves(square[i % 2][:])
                V.own(nc.vector.tensor_tensor(other, other, tab(1), ALU.mult))
                V.own(nc.vector.tensor_tensor(d, src, tab(0), ALU.mult))
                V.sync()
                V.sig(nc.vector.tensor_tensor(d, d, other, ALU.add), *evac_at(key))
                rot[0] += 1
            rotated(("ik",), ix_rot, ik[:], T)
            wait_result(dve, ("iw",))
            V.sig(nc.vector.tensor_scalar(iw[:].rearrange("p n c -> p (n c)"), slot(("iw",))[:, 0:NQ * 8], IDX_SCALE, None, ALU.mult),
                  *evac_at(("iw",)))
            for j in range(4):
                rotated(("iq", j), ix_rot, iq[:, j, :], T)
            V.own(nc.vector.memset(bias[:, :, 0:M], 0.0))
            V.own(nc.vector.tensor_copy(bias[:, 0, M:M + P], K("causal")[:, T - P:T]))
            for s in range(12):
                n, j = 1 + s // 4, s % 4
                w = (n + 1) * P
                key = ("is", n, j)
                wait_evac(dve, key)
                for a in range(2):
                    V.sync()
                    before = K("causal")[:, T - w:T] if (j, a) == (0, 0) else score[n - 1][:, 0:w]
                    ins = nc.vector.scalar_tensor_tensor(score[n - 1][:, 0:w], relu[s % 2][:, a, 0:w], iw[:, n, 2 * j + a:2 * j + a + 1],
                                                         before, ALU.mult, ALU.add)
                    V.own(ins) if a == 0 else V.sig(ins, s_relud, s + 1)
            rounds = [(n, r) for n in range(1, NQ) for r in range(K_TOP // 8)]

            def top(k):
                for _ in range(k):
                    n, r = rounds.pop(0)
                    w = (n + 1) * P
                    V.sync()
                    V.own(nc.vector.max(top8[:, n - 1, :], score[n - 1][:, 0:w]))
                    V.sync()
                    V.own(nc.vector.match_replace(score[n - 1][:, 0:w], top8[:, n - 1, :], score[n - 1][:, 0:w], TAKEN))
                    if r == K_TOP // 8 - 1:
                        V.sync()
                        V.own(nc.vector.tensor_scalar(score[n - 1][:, 0:w], score[n - 1][:, 0:w], TAKEN, NEG, ALU.not_equal, ALU.mult))
                        V.sync()
                        V.own(nc.vector.tensor_tensor(bias[:, n, M:M + w], score[n - 1][:, 0:w], K("causal")[:, T - w:T], ALU.add))
            for hg in range(2):
                for j in range(4):
                    rotated(("aq", hg, j), at_rot, aq[:, j, :], T)
                    if hg == 0:
                        top(6)
                for j in range(4):
                    rotated(("ak", hg, j), at_rot, ak[:, j, :], TT)
                    if hg == 0:
                        top(6)
                V.sync()
                for s in range(18):
                    if s < 16:
                        n, i = s % NQ, s % 2
                        w = M + (n + 1) * P
                        key = ("AS", hg, s)
                        if s >= 2:
                            wait_result(dve, ("AP", hg, s - 2))
                        wait_result(dve, key)
                        V.sig(nc.vector.tensor_tensor_reduce(Ax[i][:, 0:w], slot(key)[:, 0:w], bias[:, n, 0:w], 1.0, NEG,
                                                             ALU.add, ALU.max, amx[i][:, 0:1]), *evac_at(key))
                        V.sync()
                        V.sig(nc.vector.tensor_scalar(amx[i][:], amx[i][:], -ATT_SCALE, None, ALU.mult), s_af, 16 * hg + s + 1)
                    if 1 <= s <= 16:
                        e = s - 1
                        n, i = e % NQ, e % 2
                        w = M + (n + 1) * P
                        dve.wait_ge(s_afa, 16 * hg + e + 1)
                        V.own(nc.vector.reciprocal(asum[i][:], asum[i][:]))
                        V.sync()
                        V.sig(nc.vector.tensor_scalar(Ax[i][:, 0:w], Ax[i][:, 0:w], asum[i][:, 0:1], None, ALU.mult), s_afp, 16 * hg + e + 1)
                    if s >= 2:
                        e = s - 2
                        j, n = e // NQ, e % NQ
                        key = ("AV", hg, e)
                        wait_result(dve, key)
                        V.sig(nc.vector.tensor_copy(aq[:, j, n * P:n * P + P], slot(key)[:, 0:P]), *evac_at(key))
                V.sync()
                split([lambda dst, m, j=j: V.sig(nc.vector.tensor_copy(dst, aq[:, j, :]), s_xt, m + 1) for j in range(4)],
                      M, 4 * hg, att_hi, att_lo)
            for j in range(KD):
                wait_evac(dve, ("ga", j))
                V.sig(nc.vector.tensor_tensor(ya[:, j, :], ya[:, j, :], square[j % 2][:, 0:T], ALU.mult), s_gate, j + 1)
            dve.wait_ge(s_rtt, 16)
            for hd in range(RET_H):
                for a, (name, w) in enumerate((("rq", T), ("rk", TT))):
                    for j in range(2):
                        wait_evac(dve, (name, hd, j))
                    x1, x2 = square[0][:, 0:w], square[1][:, 0:w]
                    o1, o2 = rqk[:, 2 * a, 0:w], rqk[:, 2 * a + 1, 0:w]
                    cos, sin = rt_rot[:, 0, TT - w:TT], rt_rot[:, 1, TT - w:TT]
                    V.sync()
                    V.own(nc.vector.tensor_tensor(o1, x1, cos, ALU.mult))
                    V.own(nc.vector.tensor_tensor(o2, x2, cos, ALU.mult))
                    V.own(nc.vector.tensor_tensor(x2, x2, sin, ALU.mult))
                    V.own(nc.vector.tensor_tensor(x1, x1, sin, ALU.mult))
                    V.sync()
                    V.own(nc.vector.tensor_tensor(o1, o1, x2, ALU.subtract))
                    V.sig(nc.vector.tensor_tensor(o2, o2, x1, ALU.add), s_rotd, 2 * hd + a + 1)
                dve.wait_ge(s_dec, 16 * (hd + 1))
                for kt in range(NQ + 1):
                    key = ("rs", hd, kt)
                    wait_result(dve, key)
                    if kt < NQ:
                        w = T - kt * P
                        ins = nc.vector.tensor_tensor(rst[:, kt, kt * P:T], slot(key)[:, 0:w], dec[:, 0, 0:w], ALU.mult)
                    else:
                        ins = nc.vector.tensor_tensor(rstm[0:M, :], slot(key)[0:M, 0:T], dec[0:M, 1, :], ALU.mult)
                    V.sig(ins, *evac_at(key))
                    V.sync()
                    dve.sem_inc(s_rst, 1)

                def ret_out(d):
                    def maker(dst, m):
                        r = made["rs"]
                        if d == 0:
                            dve.wait_ge(s_rs, r + 1)
                        V.own(nc.vector.tensor_tensor(dst, rqk[:, d, 0:T], rs[r % 2][:, 0:T], ALU.mult))
                        V.sync()
                        V.sig(nc.vector.tensor_tensor(dst, dst, rg[:, d, :], ALU.mult), s_xt, m + 1)
                    return maker
                split([ret_out(d) for d in range(4)], M, 0, y_hi, y_lo)
                V.sync()
                dve.sem_inc(s_rsd, 1)
                made["rs"] += 1
                for j in range(KD):
                    key = ("wr", hd, j)
                    wait_result(dve, key)
                    if hd == 0:
                        V.sig(nc.vector.tensor_copy(yr[:, j, :], slot(key)[:, 0:T]), *evac_at(key))
                    else:
                        V.sig(nc.vector.tensor_tensor(yr[:, j, :], yr[:, j, :], slot(key)[:, 0:T], ALU.add), *evac_at(key))
            for j in range(KD):
                wait_evac(dve, ("gr", j))
                V.sync()
                V.sig(nc.vector.tensor_tensor(yr[:, j, :], yr[:, j, :], square[j % 2][:, 0:T], ALU.mult), s_gate, KD + j + 1)
            V.sync()
            wait_result(dve, ("gr", KD - 1))
            split([lambda dst, m, j=j: V.sig(nc.vector.tensor_tensor(dst, yr[:, j, :], ya[:, j, :], ALU.add), s_xt, m + 1)
                   for j in range(KD)], M)
            for j in range(KD):
                add_to_h(("mx", j))
            ffn(2, M)
            r = made["rs"]
            dve.wait_ge(s_rs, r + 1)
            for k in range(KD):
                V.sig(nc.vector.scalar_tensor_tensor(h[:, k, TQ], h[:, k, TQ], sml("final_gain", k), rs[r % 2][:, 0:T],
                                                     ALU.mult, ALU.mult), s_y, k + 1)

        @block.tensor
        def _(pe):
            done = {"sq": 0, "c": 0}

            def begin(key):
                c = NUMBER[key]
                assert c == done["c"], key
                done["c"] += 1
                if c >= SLOTS:
                    pe.wait_ge(s_evac[c % SLOTS], c // SLOTS)
                return psum[c % SLOTS]

            def mm(out, lhsT, rhs, start, stop):
                return nc.tensor.matmul(out, lhsT, rhs, start=start, stop=stop)

            def mm3(out, a, b, start, stop):
                mm(out, a[0], b[0], start, False)
                mm(out, a[1], b[0], False, False)
                return mm(out, a[0], b[1], False, stop)

            def sums(key, n, w, ones="ones"):
                ps = begin(key)
                for i in range(n):
                    q = done["sq"]
                    pe.wait_ge(s_sq, q + 1)
                    if w == T:
                        m = mm(ps[:, 0:T], K(ones), square[q % 2][:, 0:T], i == 0, i == n - 1)
                    else:
                        for a in range(2):
                            m = mm(ps[:, a * 512:a * 512 + HALF], K(ones), square[q % 2][:, a * HALF:a * HALF + HALF], i == 0, i == n - 1)
                    m.then_inc(s_sqd, 1)
                    done["sq"] += 1
                pe.wait_ge(s_sqd, done["sq"])
                pe.sem_inc(s_res, 1)

            def dense(key, parts, ktiles=KD, x=(x_hi, x_lo), per=8):
                ps = begin(key)
                b = BLOCK[key]
                k = 0
                for i in range(-(-ktiles // per)):
                    pe.wait_ge(s_lo, b + i + 1)
                    w = (w_hi[(b + i) % RING], w_lo[(b + i) % RING])
                    for j in range(min(per, ktiles - k)):
                        for o0, c0, c1 in parts:
                            m = mm3(ps[:, o0:o0 + c1 - c0], (w[0][:, j * P:j * P + P], w[1][:, j * P:j * P + P]),
                                    (x[0][:, k, c0:c1], x[1][:, k, c0:c1]), k == 0, k == ktiles - 1)
                        k += 1
                    m.then_inc(s_used, 1)

            SEQ = [(0, M, TT)]
            ALL = [(0, 0, HALF), (512, HALF, TT)]

            pe.wait_ge(s_small, 48)
            sums(("norm", 0), KD, T)
            ps = begin(("ab",))
            b = BLOCK[("ab",)]
            pe.wait_ge(s_lo, b + 1)
            pe.wait_ge(s_xlo, KD)
            for n in range(NQ):
                tk = slice(M + n * P, M + n * P + P)
                for k in range(KD):
                    m = mm3(ps[:, n * 8:n * 8 + 8], (x_hi[:, k, tk], x_lo[:, k, tk]),
                            (w_hi[b % RING][:, k * P:k * P + 8], w_lo[b % RING][:, k * P:k * P + 8]), k == 0, k == KD - 1)
            m.then_inc(s_used, 1)
            for j in range(12):
                dense(("qkv", j), SEQ)
            for j in range(4):
                dense(("z", j), SEQ)
            for j in range(4):
                dense(("dz", j), SEQ)
            for j in range(8):
                dense(("dqk", j), SEQ)
            sl = [begin(("dv", 0)), begin(("dv", 1))]
            b = BLOCK[("dv", 1)]
            for i in range(4):
                pe.wait_ge(s_lo, b + i + 1)
                w = (w_hi[(b + i) % RING], w_lo[(b + i) % RING])
                for kk in range(2):
                    k = 2 * i + kk
                    for n in range(NQ):
                        tk = slice(M + n * P, M + n * P + P)
                        m = mm3(sl[n // 2][:, (n % 2) * 512:(n % 2) * 512 + 512], (x_hi[:, k, tk], x_lo[:, k, tk]),
                                (w[0][:, kk * 512:kk * 512 + 512], w[1][:, kk * 512:kk * 512 + 512]), k == 0, k == KD - 1)
                m.then_inc(s_used, 1)
            for i in range(16):
                sums(("hn", i), 1, T, "ones" if i < 8 else "ones64")

            def four(key, f):
                ps = begin(key)
                for hd in range(4):
                    m = f(ps[:, hd * P:hd * P + P], hd)
                m.then_inc(s_res, 1)
            for n in range(NQ):
                tok = slice(n * P, n * P + P)
                pe.wait_ge(s_dn, dnv("gB", n))
                four(("gcb", n), lambda o, hd: mm(o, gB[:, hd, :], K("tri"), True, True))
                four(("beb", n), lambda o, hd: mm(o, bB[:, hd, :], K("ident"), True, True))
                ps = begin(("sm", n))
                for i, name in enumerate(("tri", "suffix", "chunk0", "chunk1")):
                    m = mm(ps[:, 4 * i:4 * i + 4], K(name), g[:, n, :], True, True)
                m.then_inc(s_res, 1)
                pe.wait_ge(s_dn, dnv("qg", n))
                four(("N0", n), lambda o, hd: mm(o, qkv[:, 4 + hd, tok], kb[:, hd, :], True, True))
                four(("A0", n), lambda o, hd: mm(o, qkv[:, 4 + hd, tok], qkv[:, hd, tok], True, True))
                pe.wait_ge(s_dn, dnv("U", n))
                four(("T1", n), lambda o, hd: nc.tensor.transpose(o, U[:, hd, :], K("ident")))
                for l in range(5):
                    pe.wait_ge(s_dn, dnv(f"Ns{l}", n))
                    four(("Y", n, l), lambda o, hd: mm(o, Ns[:, hd, :], Tm[:, hd, :], True, True))
                    wait_evac(pe, ("Y", n, l))
                    if l < 4:
                        four(("dT", n, l), lambda o, hd: mm(o, U[:, hd, :], Y[:, hd, :], True, True))
                    four(("dU", n, l), lambda o, hd: mm(o, Y[:, hd, :], U[:, hd, :], True, True))
                four(("kt", n), lambda o, hd: nc.tensor.transpose(o, qkv[:, 4 + hd, tok], K("ident")))
                four(("vt", n), lambda o, hd: nc.tensor.transpose(o, qkv[:, 8 + hd, tok], K("ident")))
                wait_evac(pe, ("vt", n))
                four(("u", n), lambda o, hd: mm(o, U[:, hd, :], vb[:, hd, :], True, True))
                four(("wT", n), lambda o, hd: mm(o, kbg[:, hd, :], U[:, hd, :], True, True))
                for c in range(2):
                    rr = slice(c * CH, c * CH + CH)
                    i = 2 * n + c
                    old = St[i % 2]
                    if i:
                        wait_evac(pe, ("dS", (i - 1) // 2, (i - 1) % 2))
                        wait_evac(pe, ("wT", n))
                        ps = begin(("wS", n, c))
                        for hd in range(4):
                            m = mm(ps[rr, hd * P:hd * P + P], wT[:, hd, rr], old[:, hd, :], True, True)
                        m.then_inc(s_res, 1)
                        wait_evac(pe, ("wS", n, c))
                    else:
                        wait_evac(pe, ("u", n))
                    vn = vnew if i else u
                    ps = begin(("o", n, c))
                    for hd in range(4):
                        if i:
                            mm(ps[:, hd * CH:hd * CH + CH], old[:, hd, :], qg[:, hd, rr], True, False)
                        m = mm(ps[:, hd * CH:hd * CH + CH], vn[rr, hd, :], AT[rr, hd, rr], i == 0, True)
                    m.then_inc(s_res, 1)
                    if i < 2 * NQ - 1:
                        four(("dS", n, c), lambda o, hd: mm(o, kdec[rr, hd, :], vn[rr, hd, :], True, True))
            pe.wait_ge(s_df, 1)
            ps = begin(("lam",))
            mm(ps[:, 0:2], K("ones")[0:64], lamt[0:64, 0:2], True, True).then_inc(s_res, 1)
            for s in range(DF_STEPS + 2):
                if s < DF_STEPS:
                    j, n = s // NQ, s % NQ
                    ps = begin(("S", j, n))
                    for c in range(2):
                        r = slice(64 * c, 64 * c + 64)
                        m = mm(ps[:, c * 512:c * 512 + (n + 1) * P], dqk[r, j, n * P:n * P + P], dqk[r, 4 + j, 0:(n + 1) * P], True, True)
                    m.then_inc(s_res, 1)
                if 1 <= s <= DF_STEPS:
                    e = s - 1
                    j, n, i = e // NQ, e % NQ, e % 2
                    pe.wait_ge(s_dfp, e + 1)
                    ps = begin(("PT", j, n))
                    for kt in range(n + 1):
                        m = nc.tensor.transpose(ps[:, kt * P:kt * P + P], Pm[i][:, kt * P:kt * P + P], K("ident"))
                    m.then_inc(s_res, 1)
                if s >= 2:
                    e = s - 2
                    j, n, i = e // NQ, e % NQ, e % 2
                    wait_evac(pe, ("PT", j, n))
                    ps = begin(("PV", j, n))
                    for kt in range(n + 1):
                        m = mm(ps[:, 0:P], dv[:, kt, j * P:j * P + P], PTs[i][:, kt * P:kt * P + P], kt == 0, kt == n)
                    m.then_inc(s_res, 1)
            for i in range(8):
                sums(("ho", i), 1, T)
            pe.wait_ge(s_xlo, 16)
            for j in range(KD):
                dense(("wo", j), SEQ)

            def ffn(i, parts):
                wide = len(parts) == 2
                sums(("norm", 2 * i - 1), KD, TT if wide else T)
                b0, c0 = BLOCK[("gate", i, 0)], C[("gate", i, 0)]
                pe.wait_ge(s_xlo, xlo[0] + KD)
                xlo[0] += KD + KF
                assert done["c"] == c0
                with pe.Fori(0, KF // 2) as g:
                    for j in range(4):
                        c, b = c0 + j, b0 + j
                        pe.wait_ge(s_evac[c % SLOTS], g + c // SLOTS)
                        pe.wait_ge(s_lo, g * 4 + (b + 1))
                        for k in range(KD):
                            w = (w_hi[b % RING][:, k * P:k * P + P], w_lo[b % RING][:, k * P:k * P + P])
                            for o, a0, a1 in parts:
                                m = mm3(psum[c % SLOTS][:, o:o + a1 - a0], w, (x_hi[:, k, a0:a1], x_lo[:, k, a0:a1]), k == 0, k == KD - 1)
                        m.then_inc(s_used, 1)
                pe.wait_ge(s_xlo, xlo[0])
                b1, c1 = BLOCK[("down", i, 0)], C[("down", i, 0)]
                with pe.Fori(0, 2) as g:
                    for j in range(4):
                        c = c1 + j
                        pe.wait_ge(s_evac[c % SLOTS], g + c // SLOTS)
                        for q in range(3):
                            b = b1 + 3 * j + q
                            pe.wait_ge(s_lo, g * 12 + (b + 1))
                            for kk in range(min(8, KF - 8 * q)):
                                k = 8 * q + kk
                                w = (w_hi[b % RING][:, kk * P:kk * P + P], w_lo[b % RING][:, kk * P:kk * P + P])
                                for o, a0, a1 in parts:
                                    m = mm3(psum[c % SLOTS][:, o:o + a1 - a0], w, (f_hi[:, k, a0:a1], f_lo[:, k, a0:a1]), k == 0, k == KF - 1)
                            m.then_inc(s_used, 1)
                done["c"] = c1 + KD

            def wide(keys, meta):
                sl = [begin(k) for k in keys]
                b = BLOCK[keys[-1]]
                for i in range(4):
                    pe.wait_ge(s_lo, b + i + 1)
                    w = (w_hi[(b + i) % RING], w_lo[(b + i) % RING])
                    for kk in range(2):
                        k = 2 * i + kk
                        for n in range(NQ + meta):
                            tk = slice(M + n * P, M + n * P + P) if n < NQ else slice(0, M)
                            out = sl[n // 2][:, (n % 2) * 512:(n % 2) * 512 + 512] if n < NQ else sl[2][0:M, 0:512]
                            m = mm3(out, (x_hi[:, k, tk], x_lo[:, k, tk]),
                                    (w[0][:, kk * 512:kk * 512 + 512], w[1][:, kk * 512:kk * 512 + 512]), k == 0, k == KD - 1)
                    m.then_inc(s_used, 1)
            xlo = [16]
            ffn(1, ALL)
            sums(("norm", 2), KD, TT)
            xlo[0] += KD
            pe.wait_ge(s_xlo, xlo[0])
            dense(("ik",), SEQ)
            ps = begin(("iw",))
            b = BLOCK[("iw",)]
            pe.wait_ge(s_lo, b + 1)
            for n in range(NQ):
                tk = slice(M + n * P, M + n * P + P)
                for k in range(KD):
                    m = mm3(ps[:, n * 8:n * 8 + 8], (x_hi[:, k, tk], x_lo[:, k, tk]),
                            (w_hi[b % RING][:, k * P:k * P + 8], w_lo[b % RING][:, k * P:k * P + 8]), k == 0, k == KD - 1)
            m.then_inc(s_used, 1)
            for j in range(4):
                dense(("iq", j), SEQ)
            wait_evac(pe, ("ik",))
            for n in range(1, NQ):
                for j in range(4):
                    wait_evac(pe, ("iq", j))
                    ps = begin(("is", n, j))
                    for a in range(2):
                        r = slice(64 * a, 64 * a + 64)
                        m = mm(ps[:, a * 512:a * 512 + (n + 1) * P], iq[r, j, n * P:n * P + P], ik[r, 0:(n + 1) * P], True, True)
                    m.then_inc(s_res, 1)
            for hg in range(2):
                for j in range(4):
                    dense(("aq", hg, j), SEQ)
                for j in range(4):
                    dense(("ak", hg, j), ALL)
                wide([("av", hg, i) for i in range(3)], 1)
                for i in range(3):
                    wait_evac(pe, ("av", hg, i))
                for s in range(18):
                    if s < 16:
                        j, n = s // NQ, s % NQ
                        if n == 0:
                            wait_evac(pe, ("aq", hg, j))
                            wait_evac(pe, ("ak", hg, j))
                        w = M + (n + 1) * P
                        ps = begin(("AS", hg, s))
                        for a0, a1 in ((0, min(w, 512)), (512, w)):
                            if a1 > a0:
                                m = mm(ps[:, a0:a1], aq[:, j, n * P:n * P + P], ak[:, j, a0:a1], True, True)
                        m.then_inc(s_res, 1)
                    if 1 <= s <= 16:
                        e = s - 1
                        n, i = e % NQ, e % 2
                        pe.wait_ge(s_afp, 16 * hg + e + 1)
                        ps = begin(("AP", hg, e))
                        nc.tensor.transpose(ps[0:M, 0:P], Ax[i][:, 0:M], K("ident"))
                        for kt in range(n + 1):
                            m = nc.tensor.transpose(ps[:, (kt + 1) * P:(kt + 2) * P], Ax[i][:, M + kt * P:M + kt * P + P], K("ident"))
                        m.then_inc(s_res, 1)
                    if s >= 2:
                        e = s - 2
                        j, n, i = e // NQ, e % NQ, e % 2
                        wait_evac(pe, ("AP", hg, e))
                        ps = begin(("AV", hg, e))
                        mm(ps[:, 0:P], avm[0:M, j * P:j * P + P], At[i][0:M, 0:P], True, False)
                        for kt in range(n + 1):
                            m = mm(ps[:, 0:P], av[:, kt, j * P:j * P + P], At[i][:, (kt + 1) * P:(kt + 2) * P], False, kt == n)
                        m.then_inc(s_res, 1)
            xlo[0] += ATT_H
            pe.wait_ge(s_xlo, xlo[0])
            for j in range(KD):
                dense(("ao", j), [(0, 0, T)], ATT_H, (att_hi, att_lo))
            for j in range(KD):
                dense(("ga", j), SEQ)
            for hd in range(RET_H):
                for j in range(2):
                    dense(("rq", hd, j), SEQ)
                for j in range(2):
                    dense(("rk", hd, j), ALL)
                wide([("rv", hd, i) for i in range(3)], 1)
                for j in range(4):
                    dense(("rg", hd, j), SEQ)
                pe.wait_ge(s_rotd, 2 * hd + 2)
                for kt in range(NQ + 1):
                    ps = begin(("rs", hd, kt))
                    keys = slice(M + kt * P, M + kt * P + P) if kt < NQ else slice(0, M)
                    q0 = kt * P if kt < NQ else 0
                    out = ps[:, 0:T - q0] if kt < NQ else ps[0:M, 0:T]
                    for d in range(2):
                        m = mm(out, rqk[:, 2 + d, keys], rqk[:, d, q0:T], d == 0, d == 1)
                    m.then_inc(s_res, 1)
                for i in range(3):
                    wait_evac(pe, ("rv", hd, i))
                pe.wait_ge(s_rst, 5 * hd + 5)
                for d in range(4):
                    ps = begin(("ry", hd, d))
                    mm(ps[:, 0:T], rvm[0:M, d * P:d * P + P], rstm[0:M, :], True, False)
                    for kt in range(NQ):
                        m = mm(ps[:, kt * P:T], rv[:, kt, d * P:d * P + P], rst[:, kt, kt * P:T], False, kt == NQ - 1)
                    m.then_inc(s_res, 1)
                sums(("rn", hd), 4, T)
                xlo[0] += 4
                pe.wait_ge(s_xlo, xlo[0])
                for j in range(KD):
                    key = ("wr", hd, j)
                    ps = begin(key)
                    b = BLOCK[key]
                    pe.wait_ge(s_lo, b + 1)
                    w = (w_hi[b % RING], w_lo[b % RING])
                    for k in range(4):
                        a = (j % 2) * 512 + k * P
                        m = mm3(ps[:, 0:T], (w[0][:, a:a + P], w[1][:, a:a + P]), (y_hi[:, k, :], y_lo[:, k, :]), k == 0, k == 3)
                    m.then_inc(s_used if j % 2 else s_res, 1)
            for j in range(KD):
                dense(("gr", j), SEQ)
            xlo[0] += KD
            pe.wait_ge(s_xlo, xlo[0])
            for j in range(KD):
                dense(("mx", j), SEQ)
            ffn(2, SEQ)
            sums(("norm", 4), KD, T)

        @block.gpsimd
        def _(pool):
            with pool.Fori(0, BLOCKS_PADDED // RING) as i:
                for j in range(RING):
                    pool.wait_ge(s_hi, i * RING + (j + 1))
                    nc.gpsimd.tensor_tensor(w_lo[j][:], w_raw[j][:], w_hi[j][:].bitcast(F32),
                                            ALU.subtract).then_inc(s_lo, 1)
            if dump is not None:
                for o in owners:
                    pool.wait_ge(*o.last)
                src = {"h": h, "qkv": qkv, "dqk": dqk, "g": g, "beta": beta, "x_hi": x_hi}[dump]
                pool.dma_start(dump_dram, src[:].bitcast(F32) if dump == "x_hi" else src[:]).then_inc(s_dump, 16)
                pool.wait_ge(s_dump, 16)


def tiles_of(w, cols):
    k, n = w.shape
    return w


def stream(inp):
    z = np.zeros
    w_in, w_out = inp["w_in"][0], inp["w_out"][0]
    blocks = []

    def cols(w):
        k = w.shape[0]
        w = w.reshape(k // P, P, w.shape[1]).transpose(1, 0, 2)
        blocks.append(np.ascontiguousarray(w.reshape(P, -1)))

    def wide(w):
        w = w.reshape(4, 2, P, 512).transpose(0, 2, 1, 3).reshape(4, P, 1024)
        blocks.extend(np.ascontiguousarray(w))
    o = np.cumsum([0, 512, 512, 512, 512, 4, 4, 512, 512, 512, 512])
    gates = z((D, P), np.float32)
    gates[:, 0:8] = w_in[:, o[4]:o[6]]
    cols(gates)
    for a in (o[0], o[1], o[2], o[3], o[9], o[6], o[7]):
        for j in range(4):
            cols(w_in[:, a + j * P:a + j * P + P])
    wide(w_in[:, o[8]:o[9]])
    for j in range(8):
        cols(w_out[:, j * P:j * P + P])
    fit = lambda w: np.concatenate([w, z((w.shape[0], P - w.shape[1]), np.float32)], 1)

    def ffn(i):
        gate, up, down = (inp[f"ffn{i}_w_{n}_2"][0] for n in ("gate", "up", "down"))
        for f in range(KF):
            cols(gate[:, f * P:f * P + P])
            cols(up[:, f * P:f * P + P])
        for d in range(KD):
            w = np.concatenate([down[:, d * P:d * P + P], z((24 * P - D_FF, P), np.float32)])
            for q in range(3):
                cols(w[q * 1024:q * 1024 + 1024])
    ffn(1)
    w2 = inp["w_in_2"][0]
    names = ("rq", "rk", "rv", "rg", "aq", "ak", "av", "iq", "ik", "iw", "gr", "ga")
    sizes = (1024, 1024, 2048, 2048, 1024, 1024, 1024, 512, 64, 8, 1024, 1024)
    start = dict(zip(names, np.cumsum([0, *sizes])))
    part = lambda name, c, n: w2[:, start[name] + c:start[name] + c + n]
    cols(np.concatenate([part("ik", 0, 64)] * 2, 1))
    cols(fit(part("iw", 0, 8)))
    for j in range(4):
        cols(part("iq", j * P, P))
    for hg in range(2):
        for name in ("aq", "ak"):
            for j in range(4):
                cols(part(name, hg * 512 + j * P, P))
        wide(part("av", hg * 512, 512))
    for j in range(KD):
        cols(inp["w_att_out_2"][0][:, j * P:j * P + P])
    for j in range(KD):
        cols(part("ga", j * P, P))
    for hd in range(RET_H):
        for name in ("rq", "rk"):
            for j in range(2):
                cols(part(name, hd * 256 + j * P, P))
        wide(part("rv", hd * 512, 512))
        for j in range(4):
            cols(part("rg", hd * 512 + j * P, P))
        w = inp["w_ret_out_2"][0][hd * 512:hd * 512 + 512]
        for j in range(0, KD, 2):
            blocks.append(np.ascontiguousarray(
                w.reshape(4, P, KD, P)[:, :, j:j + 2].transpose(1, 2, 0, 3).reshape(P, 1024)))
    for j in range(KD):
        cols(part("gr", j * P, P))
    for j in range(KD):
        cols(inp["w_mix_out_2"][0][:, j * P:j * P + P])
    ffn(2)
    assert len(blocks) == BLOCKS, (len(blocks), BLOCKS)
    while len(blocks) < BLOCKS_PADDED:
        blocks.append(z((P, 1024), np.float32))
    return np.stack(blocks).reshape(BLOCKS_PADDED // RING, RING, P, 1024)


def small_inputs(inp):
    a = np.zeros((P, N_SMALL), np.float32)

    def put(name, v):
        v = np.asarray(v)
        a[:v.shape[0], SMALL[name][0]:SMALL[name][0] + v.shape[1]] = v
    col = lambda v: v.reshape(-1, P).T
    put("norm_gain", col(inp["norm_gain"][0]))
    put("conv", inp["conv_w"][0].reshape(4, 12, P).transpose(2, 1, 0).reshape(P, 48))
    put("dn_gain", col(inp["dn_out_gain"][0]))
    put("q_gain", np.concatenate([inp["q_gain"][0]] * 2)[:, None])
    put("k_gain", np.concatenate([inp["k_gain"][0]] * 2)[:, None])
    put("df_gain", col(inp["df_out_gain"][0]))
    put("a_log", np.broadcast_to(inp["a_log"][0], (P, 4)))
    put("dt_bias", np.broadcast_to(inp["dt_bias"][0], (P, 4)))
    for n, m in (("lq1", "lambda_q1"), ("lk1", "lambda_k1"), ("lq2", "lambda_q2"), ("lk2", "lambda_k2")):
        put(n, inp[m][0][:, None])
    put("f1_gain", col(inp["ffn1_norm_2"][0]))
    put("mix_gain", col(inp["mix_norm_2"][0]))
    put("f2_gain", col(inp["ffn2_norm_2"][0]))
    put("final_gain", col(inp["final_norm_2"]))
    return a


def kernel(_dump=None, **inputs):
    import concourse.bacc as bacc
    from concourse.bass_utils import run_bass_kernel_spmd as run

    inp = {k: np.asarray(v) for k, v in inputs.items()}
    feature_major = lambda a: np.ascontiguousarray(a.T.reshape(KD, P, -1).transpose(1, 0, 2))
    arrays = {
        "weights": stream(inp),
        "x_t": feature_major(inp["x"][0]),
        "meta_t": feature_major(inp["meta_tokens_2"]),
        "consts": constants(),
        "small_in": small_inputs(inp),
        "rotations": rotations(),
        "decays": retention_decay(),
    }
    nc = bacc.Bacc("TRN2", target_bir_lowering=False, num_devices=1)
    args = [nc.dram_tensor(n, a.shape, F32, kind="ExternalInput").ap() for n, a in arrays.items()]
    out = nc.dram_tensor("out", (P, KD, T), F32, kind="ExternalOutput").ap()
    dd = None
    if _dump:
        dd = nc.dram_tensor("dumped", _dump[1], F32, kind="ExternalOutput").ap()
    build(nc, *args, out, _dump and _dump[0], dd)
    r = run(nc, [arrays], core_ids=[0])
    y = r.results[0]["out"]
    return np.ascontiguousarray(y.transpose(1, 0, 2).reshape(D, T).T)[None]
```

```python
from contextlib import ExitStack

import numpy as np
import concourse.bass as bass
from concourse import mybir

F32 = mybir.dt.float32
F32R = mybir.dt.float32r
ALU = mybir.AluOpType
ACT = mybir.ActivationFunctionType
AX = mybir.AxisListType

P = 128
D = 1024
KD = D // P
T = 512
M = 16
TT = M + T
HALF = TT // 2
TQ = slice(M, TT)
NQ = T // P
EPS = 1e-6
LN_EXP = "natural_log_exp_and_others"
NEG = -1.0e30
DN_WORK = "decay qg attn n inv_t inv join join_b y kdec kbg u".split()

DN_H = 4
LAMBDA_INIT = 0.8 - 0.6 * 1.0
DF_H = 4
DF_STEPS = DF_H * NQ
CH = 64
D_FF = 2816
KF = D_FF // P
RET_H = 4
RET_DK = 256
ROPE_THETA = 10000.0
ATT_SCALE = 128 ** -0.5
IDX_SCALE = (64 ** -0.5) * (8 ** -0.5)
TAKEN = -3.0e38
ATT_H = 8
IDX_H = 8
K_TOP = 128
SLOTS = 4
RING = 4



def results():
    r = []
    add = lambda key, blocks=0: r.append((key, blocks))
    add(("norm", 0))
    for j in range(12):
        add(("qkv", j), 1)
    add(("ab",), 1)
    add(("dv", 0))
    for i in range(8):
        add(("hn", i))
    add(("dv", 1), 4)
    add(("lam",))
    point = 0

    def aside():
        nonlocal point
        for key in aside_results(point):
            add(key, 1 if key in ASIDE_DENSE else 0)
        point += 1
    for n in range(NQ):
        for k in ("gcb", "beb", "sm"):
            add((k, n))
        aside()
        for k in ("N0", "A0"):
            add((k, n))
        aside()
        for k in ("T1", "kt", "vt"):
            add((k, n))
        aside()
        for l in range(5):
            add(("Y", n, l))
            aside()
            if l < 4:
                add(("dT", n, l))
            add(("dU", n, l))
            aside()
        for k in ("u", "wT"):
            add((k, n))
        aside()
        for c in range(2):
            if (n, c) != (0, 0):
                add(("wS", n, c))
            aside()
            add(("o", n, c))
            if (n, c) != (NQ - 1, 1):
                add(("dS", n, c))
            aside()
    assert point == POINTS * NQ
    while point < LAST_POINT:
        aside()
    for i in range(8):
        add(("ho", i))
    for j in range(KD):
        add(("wo", j), 1)
    ffn_results(add, 1)
    add(("norm", 2))
    add(("ik",), 1)
    add(("iw",), 1)
    for j in range(4):
        add(("iq", j), 1)
    for n in range(1, NQ):
        for j in range(4):
            add(("is", n, j))
    for key, blocks in projection_keys(0):
        add(key, blocks)
    for j in range(4):
        add(("ga", j), 1)
    for s in range(ATT_STEPS + 2):
        if s < ATT_STEPS:
            add(("AS", s))
        for key, blocks in filled(2 * s):
            add(key, blocks)
        if 1 <= s <= ATT_STEPS:
            add(("AP", s - 1))
        for key, blocks in filled(2 * s + 1):
            add(key, blocks)
        if s >= 2:
            add(("AV", s - 2))
    for j in range(KD):
        add(("ao", j), 1)
    for hd in range(RET_H):
        for j in range(2):
            add(("rq", hd, j), 1)
        for j in range(2):
            add(("rk", hd, j), 1)
        add(("rv", hd, 0))
        add(("rv", hd, 1))
        add(("rv", hd, 2), 4)
        add(("rg", hd, 0), 1)
        for kt in range(NQ + 1):
            add(("rs", hd, kt))
        add(("rg", hd, 1), 1)
        for d in range(4):
            add(("ry", hd, d))
        add(("rg", hd, 2), 1)
        add(("rn", hd))
        add(("rg", hd, 3), 1)
        for j in range(KD):
            add(("wr", hd, j), j % 2)
    for j in range(KD):
        add(("gr", j), 1)
    for j in range(KD):
        add(("mx", j), 1)
    ffn_results(add, 2)
    add(("norm", 4))
    return r


def ffn_results(add, i):
    add(("norm", 2 * i - 1))
    for f in range(KF):
        add(("gate", i, f), 1)
        add(("up", i, f), 1)
    for d in range(KD):
        add(("down", i, d), 3)


POINTS = 18
PIECE = 5
ASIDE_DENSE = [("z", j) for j in range(4)] + [("dz", j) for j in range(4)] + [("dqk", j) for j in range(8)]
DF_START = 2 * POINTS
LAST_POINT = DF_START + 2 * (DF_STEPS - 1) + 8


def dense_done(f):
    return (8 * f + 7) // PIECE


def norm_at(p, stage):
    return [i for i in range(8) if dense_done(8 + i) + 2 + stage == p]


def df_at(p, late):
    s, odd = divmod(p - DF_START, 2)
    s -= late
    return s if 0 <= s < DF_STEPS else None


def aside_results(p):
    keys = [key for f, key in enumerate(ASIDE_DENSE) if dense_done(f) == p]
    keys += [("hn", 8 + i) for i in norm_at(p, 1)]
    if p >= DF_START and (p - DF_START) % 2 == 0:
        for name, late in (("S", 0), ("PT", 2), ("PV", 3)):
            s = df_at(p, late)
            if s is not None:
                keys.append((name, s // NQ, s % NQ))
    return keys


ATT_STEPS = ATT_H * NQ
PAIR_STEPS = 2 * NQ


def projection_keys(g):
    if g == ATT_H // 2:
        return [(("ga", 4 + j), 1) for j in range(4)]
    return [((name, g, j), 1) for j in range(2) for name in ("ak", "aq")] + [(("av", g, 0), 0), (("av", g, 1), 2)]


def projection_units(g):
    units = []
    for key, _ in projection_keys(g):
        if key[0] == "av":
            units += [(key, n, k, 1) for n in (range(NQ) if key[2] == 0 else [NQ]) for k in range(KD)]
        else:
            units += [(key, None, k, 2) for k in range(KD)]
    return units


def fill_places():
    units, complete = {}, {}
    for g in range(ATT_H // 2):
        todo = projection_units(g + 1)
        cost, places, before = sum(u[3] for u in todo), 2 * PAIR_STEPS, 0
        for u in todo:
            at = 2 * PAIR_STEPS * g + before * places // cost
            units.setdefault(at, []).append(u)
            before += u[3]
            if u is todo[-1] or todo[todo.index(u) + 1][0] != u[0]:
                complete.setdefault(at, []).append(u[0])
    return units, complete


FILL, FILLED = fill_places()


def filled(at):
    return [(key, dict(projection_keys(key[1] if key[0] != "ga" else ATT_H // 2))[key]) for key in FILLED.get(at, [])]


RESULTS = results()
ROTATED = [k for k, _ in RESULTS if k[0] in ("ik", "iq", "aq", "ak")]
PLACE = {}
FREE = {}
_bank, _count, _main, _half = {}, {}, 0, 0
for _key, _ in RESULTS:
    if _key[0] in ("gcb", "beb", "sm", "N0", "A0", "T1", "Y", "dT", "dU", "kt", "vt", "u", "wT", "wS", "o", "dS") or \
            _key[0] == "hn" and _key[1] < 8:
        _p = (4 + _half % 4, 1)
        _half += 1
    elif _key in ASIDE_DENSE:
        _p = (2 * (ASIDE_DENSE.index(_key) % 2), 1)
    elif _key[0] == "hn":
        _p = (3 - 2 * (_key[1] % 2), 1)
    elif _key[0] in ("S", "dv"):
        _p = (2 * _key[1] if _key[0] == "dv" else 0, 2)
    elif _key[0] in ("aq", "ak", "av", "AS", "AP", "AV") or _key[0] == "ga" and _key[1] >= 4:
        _p = {"aq": (2, 1), "ak": (0, 2), "AV": (3, 1), "AS": (4, 2), "AP": (6, 2),
              "av": ((0, 2), (2, 1))[_key[-1] % 2], "ga": ((0, 2), (2, 1))[_key[-1] % 2]}[_key[0]]
    elif _key[0] in ("PT", "PV"):
        _p = (2 + (_key[0] == "PV"), 1)
    else:
        _p = (2 * (_main % SLOTS), 2)
        _main += 1
    _count[_p] = _count.get(_p, 0) + 1
    PLACE[_key] = (*_p, _count[_p])
    FREE[_key] = sorted({_bank[b] for b in range(_p[0], _p[0] + _p[1]) if b in _bank}, key=str)
    for b in range(_p[0], _p[0] + _p[1]):
        _bank[b] = _key
BLOCK = {}
READY = {}
_b = _g = 0
for _key, _n in RESULTS:
    BLOCK[_key] = _b
    _b += _n
    if _n:
        READY[_key] = ("used", _b)
    elif _key[0] in ("dv", "rv"):
        READY[_key] = ("used", _b + 4)
    else:
        _g += 1
        READY[_key] = ("result", _g)
BLOCKS = _b
BLOCKS_PADDED = -(-BLOCKS // RING) * RING

CONST = {}


def constants():
    i = np.arange(P)
    s, c = i[:, None], i[None, :]
    same = (s // CH) == (c // CH)
    parts = {
        "ident": s == c,
        "ones": s == s + 0 * c,
        "ones64": (s // 64) == (c // 64),
        "tri": same & (s <= c),
        "suffix": same & (s > c),
        "chunk0": (s < CH) & (c == c),
        "chunk1": (s >= CH) & (c == c),
    }
    for l in range(6):
        w = 2 ** l
        parts[f"join{l}"] = (s // (2 * w) == c // (2 * w)) & (s % (2 * w) < w) & (c % (2 * w) >= w)
    causal = np.zeros((P, T), np.float32)
    causal[:, T - P:] = np.where(c > s, np.float32(NEG), np.float32(0))
    parts = {"ident": parts.pop("ident"), "ones": parts.pop("ones"), "causal": causal, **parts}
    out, at = [], 0
    for name, m in parts.items():
        CONST[name] = (at, at + m.shape[1])
        at += m.shape[1]
        out.append(np.broadcast_to(m, (P, m.shape[1])).astype(np.float32))
    return np.ascontiguousarray(np.concatenate(out, 1))


N_CONST = constants().shape[1]
N_KEPT = CONST["causal"][1]


def rotations():
    pos = np.arange(TT, dtype=np.float32)

    def table(d, copies, signed):
        inv = np.float32(ROPE_THETA) ** (-np.arange(0, d, 2, dtype=np.float32) / np.float32(d))
        angle = (pos[:, None] * inv[None, :].astype(np.float32)).astype(np.float32).T
        cos, sin = np.cos(angle), np.sin(angle)
        cos = np.concatenate([cos] * copies)
        sin = np.concatenate([sin * (-1 if signed and k % 2 == 0 else 1) for k in range(copies)])
        return [cos, sin]
    t = table(128, 2, True) + table(64, 4, True) + table(256, 1, False)
    return np.ascontiguousarray(np.stack(t).transpose(1, 0, 2).astype(np.float32))


def retention_decay():
    out = np.zeros((P, RET_H, 2, T), np.float64)
    k, q = np.arange(P)[:, None], np.arange(T)[None, :]
    for hd in range(RET_H):
        log_g = float(np.log1p(-np.float32(2.0 ** (-5.0 - hd))))
        out[:, hd, 0] = np.where(q >= k, np.exp(log_g * np.maximum(q - k, 0)), 0.0)
        out[:M, hd, 1] = np.exp(log_g * (q + M - k[:M]))
    return (out * RET_DK ** -0.5).astype(np.float32)

SMALL = {}
_at = 0
for _name, _w in (("norm_gain", 8), ("conv", 48), ("dn_gain", 1), ("q_gain", 1), ("k_gain", 1), ("df_gain", 1),
                  ("a_log", 4), ("dt_bias", 4), ("lq1", 1), ("lk1", 1), ("lq2", 1), ("lk2", 1),
                  ("f1_gain", 8), ("mix_gain", 8), ("f2_gain", 8), ("final_gain", 8)):
    SMALL[_name] = (_at, _at + _w)
    _at += _w
N_SMALL = _at


class Own:

    def __init__(self, engine, sem):
        self.engine, self.sem, self.count, self.last = engine, sem, 0, None

    def own(self, ins):
        self.count += 1
        ins.then_inc(self.sem, 1)
        self.last = (self.sem, self.count)

    def sig(self, ins, sem, value):
        ins.then_inc(sem, 1)
        self.last = (sem, value)

    def sync(self):
        self.engine.wait_ge(*self.last)


def build(nc, w_dram, x_dram, meta_dram, const_dram, small_dram, rot_dram, dec_dram, out_dram, dump=None, dump_dram=None):
    with ExitStack() as ctx:
        def sb(name, shape, dt=F32, scope=ctx):
            return scope.enter_context(nc.sbuf_tensor(name, shape, dt))

        def sem(name):
            return ctx.enter_context(nc.semaphore(name))

        w_raw = [sb(f"w_raw{i}", [P, 1024]) for i in range(RING)]
        w_hi = [sb(f"w_hi{i}", [P, 1024], F32R) for i in range(RING)]
        w_lo = [sb(f"w_lo{i}", [P, 1024], F32R) for i in range(RING)]
        h = sb("h", [P, KD, TT])
        const = sb("const", [P, N_KEPT])
        small = sb("small", [P, N_SMALL])
        eps = sb("eps", [P, 1])
        square = [sb(f"square{i}", [P, TT]) for i in range(2)]
        rs = [sb(f"rs{i}", [P, TT]) for i in range(2)]
        xt = [sb(f"xt{i}", [P, TT]) for i in range(2)]
        psum = [ctx.enter_context(nc.psum_tensor(f"slot{i}", [P, 1024], F32)) for i in range(SLOTS)]

        with ExitStack() as scope:
            work_late = [sb(f"dn_{name}", [P, 4, P], F32, scope) for name in DN_WORK]
        x_hi = sb("x_hi", [P, KD, TT], F32R)
        x_lo = sb("x_lo", [P, KD, TT], F32R)

        with ExitStack() as scope:
            fb = lambda name, shape, dt=F32, scope=scope: sb(name, shape, dt, scope)
            qkv = fb("qkv", [P, 12, T])
            sz = fb("sz", [P, 4, T])
            dsz = fb("dsz", [P, 4, T])
            dqk = fb("dqk", [P, 8, T])
            dv = fb("dv", [P, NQ, T])
            St = [fb(f"state{i}", [P, 4, P]) for i in range(2)]
            with ExitStack() as early:
                work_early = [fb(f"dn_early_{name}", [P, 4, P], F32, early) for name in DN_WORK[:-2]]
                work_early += [x[:, 0:T].rearrange("p (h c) -> p h c", h=4) for x in xt]
            with ExitStack() as late:
                Sx = [[fb(f"score{i}{c}", [P, T], F32, late) for c in range(2)] for i in range(2)]
                Pm = [fb(f"prob{i}", [P, T], F32, late) for i in range(2)]
                PTs = [fb(f"prob_t{i}", [P, T], F32, late) for i in range(2)]
            fb("dn_early_place", [P, (len(DN_WORK) - 2) * T])
            mx = [fb(f"mx{i}", [P, 2]) for i in range(2)]
            sums_ = [fb(f"sum{i}", [P, 2]) for i in range(2)]
            ab = fb("ab", [P, NQ, 8])
            tA = fb("tA", [P, NQ, 4])
            tB = fb("tB", [P, NQ, 4])
            beta = fb("beta", [P, NQ, 4])
            g = fb("g", [P, NQ, 4])
            nea = fb("nea", [P, 4])
            sm = fb("sm", [P, 16])
            esm = fb("esm", [P, 16])
            cb = fb("cb", [P, 4])
            lamt = fb("lamt", [P, 8])
            const1 = fb("const1", [P, N_CONST - N_KEPT])

        with ExitStack() as scope:
            f_hi = sb("f_hi", [P, KF, TT], F32R, scope)
            f_lo = sb("f_lo", [P, KF, TT], F32R, scope)

        with ExitStack() as mix:
            mb = lambda name, shape, dt=F32, scope=mix: sb(name, shape, dt, scope)
            with ExitStack() as scope:
                aq = [mb(f"aq{i}", [P, 2, T], F32, scope) for i in range(1)]
                av = [mb(f"av{i}", [P, NQ, 2 * P], F32, scope) for i in range(1)]
            ya_late = mb("ya_late", [P, 4, T])
            ya_early = mb("ya_early", [P, 4, T])
            ya = [(ya_early if j < 4 else ya_late)[:, j % 4, :] for j in range(KD)]
            with ExitStack() as att:
                aq += [mb("aq1", [P, 2, T], F32, att)]
                av += [mb("av1", [P, NQ, 2 * P], F32, att)]
                ak = [mb(f"ak{i}", [P, 2, TT], F32, att) for i in range(2)]
                avm = [mb(f"av_meta{i}", [P, 2 * P], F32, att) for i in range(2)]
                bias = mb("bias", [P, NQ, TT], F32, att)
                at_rot = mb("at_rot", [P, 2, TT], F32, att)
                with ExitStack() as scope:
                    ix_rot = mb("ix_rot", [P, 2, TT], F32, scope)
                    iq = mb("iq", [P, 4, T], F32, scope)
                    ik = mb("ik", [P, T], F32, scope)
                    relu = [mb(f"relu{i}", [P, 2, T], F32, scope) for i in range(2)]
                    iw = mb("iw", [P, NQ, 8], F32, scope)
                with ExitStack() as scope:
                    att_hi = mb("att_hi", [P, ATT_H, T], F32R, scope)
                    att_lo = mb("att_lo", [P, ATT_H, T], F32R, scope)
                    Ax = [mb(f"att_score{i}", [P, TT], F32, scope) for i in range(2)]
                    At = [mb(f"att_prob_t{i}", [P, 5 * P], F32, scope) for i in range(2)]
                    amx = [mb(f"att_mx{i}", [P, 1], F32, scope) for i in range(2)]
                    asum = [mb(f"att_sum{i}", [P, 1], F32, scope) for i in range(2)]
                    score = [mb(f"ix_score{i}", [P, T], F32, scope) for i in range(3)]
                    top8 = mb("top8", [P, 3, 8], F32, scope)
            yr = mb("yr", [P, KD, T])
            with ExitStack() as scope:
                merged_hi = mb("merged_hi", [P, KD, T], F32R, scope)
                merged_lo = mb("merged_lo", [P, KD, T], F32R, scope)
            rqk = mb("rqk", [P, 4, TT])
            rv = mb("rv", [P, NQ, T])
            rvm = mb("rv_meta", [P, T])
            rg = mb("rg", [P, 4, T])
            rst = mb("ret_score_t", [P, NQ, T])
            rstm = mb("ret_score_meta", [P, T])
            y_hi = mb("y_hi", [P, 4, T], F32R)
            y_lo = mb("y_lo", [P, 4, T], F32R)
            rt_rot = mb("rt_rot", [P, 2, TT])
            dec = mb("dec", [P, 2, T])

        s_small = sem("small_loaded")
        s_const = sem("const_loaded")
        s_x = [sem(f"x_loaded{i}") for i in range(4)]
        s_raw = [sem(f"w_raw_loaded{i}") for i in range(RING)]
        s_hi = sem("w_hi_made")
        s_lo = sem("w_lo_made")
        s_used = sem("w_block_used")
        s_res = sem("result_ready")
        s_evac = {p: sem(f"evac_bank{p[0]}_{p[1]}") for p in sorted({(a, b) for a, b, _ in PLACE.values()})}
        s_eps = sem("eps_set")
        s_sq = sem("square_made")
        s_sqd = sem("square_used")
        s_acc = sem("squares_added")
        s_rs = sem("rs_made")
        s_rsd = sem("rs_used")
        s_xt = sem("xt_made")
        s_xhi = sem("x_hi_made")
        s_xlo = sem("x_lo_made")
        s_v = sem("vector_order")
        s_a = sem("scalar_order")
        s_conv = sem("conv_made")
        s_silu = sem("silu_made")
        s_hn = sem("head_norm_applied")
        s_g = sem("g_beta")
        s_dn = sem("delta_vector")
        s_da = sem("delta_scalar")
        s_df = sem("diff_vector")
        s_dfp = sem("diff_prob")
        s_dfa = sem("diff_scalar")
        s_sg = sem("silu_gate")
        s_rot = sem("rotated_copy")
        s_ixt = sem("indexer_tables")
        s_relu = sem("relu_made")
        s_relud = sem("relu_used")
        s_af = sem("att_vector")
        s_afp = sem("att_prob")
        s_afa = sem("att_scalar")
        s_athi = sem("att_hi_made")
        s_gate = sem("gate_used")
        s_sigm = sem("att_gate_made")
        s_ry = sem("ret_y_copied")
        s_dec = sem("decay_loaded")
        s_rst = sem("ret_score_decayed")
        s_y = sem("y_made")
        s_rotd = sem("ret_rotated")
        s_rtt = sem("ret_rotation_loaded")
        s_dump = sem("dumped")
        s_out = sem("out_stored")

        def halves(ap):
            return ap.rearrange("p (a c) -> p a c", a=2)

        def ps_all(key):
            return halves(slot(key)[:])[:, :, 0:HALF]

        def evac_in(key, g):
            s_, v = evac_at(key)
            return s_, v + g

        def K(name):
            a, b = CONST[name]
            return const[:, a:b] if b <= N_KEPT else const1[:, a - N_KEPT:b - N_KEPT]

        def sml(name, j=0, w=1):
            a = SMALL[name][0] + j
            return small[:, a:a + w]

        def wait_result(eng, key):
            kind, value = READY[key]
            eng.wait_ge(s_used if kind == "used" else s_res, value)

        def evac_at(key):
            bank, n, count = PLACE[key]
            return s_evac[bank, n], count

        def wait_evac(eng, key):
            eng.wait_ge(*evac_at(key))

        def slot(key):
            bank, n, _ = PLACE[key]
            return psum[bank // 2][:, bank % 2 * 512:(bank % 2 + n) * 512]

        def work(n):
            DT, qg, AT, N, U, Tm, Ns, Ns_b, Y, kdec, kbg, u = work_early if n < 2 else work_late
            return DT, qg, qg, Ns, AT, N, U, Tm, (Ns, Ns_b), Y, kdec, kbg, kbg, u, Tm, u, DT, Y, Ns

        def heads(ap):
            return ap.rearrange("p (h c) -> p h c", h=4)

        DNV = ["gB", "dt", "qg", "U", "Ns0", "Ns1", "Ns2", "Ns3", "Ns4"]
        dnv = lambda name, n: n * len(DNV) + DNV.index(name) + 1

        block = ctx.enter_context(nc.Block())
        owners = []

        @block.sync
        def _(sp):
            for j in range(RING):
                sp.dma_start(w_raw[j][:], w_dram[0, j]).then_inc(s_raw[j], 16)
            with sp.Fori(1, BLOCKS_PADDED // RING) as i:
                for j in range(RING):
                    sp.wait_ge(s_lo, i * RING + (j + 1 - RING))
                    sp.dma_start(w_raw[j][:], w_dram[i, j]).then_inc(s_raw[j], 16)

        @block.scalar
        def _(act):
            A = Own(act, s_a)
            owners.append(A)
            made = {"w": 0, "sq": 0, "rs": 0, "x": 0, "table": None}

            def w_split(upto):
                while made["w"] < min(upto + 1, BLOCKS_PADDED):
                    b = made["w"]
                    act.wait_ge(s_raw[b % RING], 16 * (b // RING + 1))
                    if b >= RING:
                        act.wait_ge(s_used, b - RING + 1)
                    nc.scalar.activation(w_hi[b % RING][:], w_raw[b % RING][:], ACT.Copy).then_inc(s_hi, 1)
                    made["w"] += 1

            def ahead(key, blocks=1):
                w_split(BLOCK[key] + blocks - 1 + RING - 1)

            def squares(srcs):
                for src in srcs:
                    q = made["sq"]
                    if q >= 2:
                        act.wait_ge(s_sqd, q - 1)
                    w = src.shape[-1]
                    nc.scalar.activation(square[q % 2][:, 0:w], src, ACT.Square).then_inc(s_sq, 1)
                    made["sq"] += 1

            def rsqrt(key, scale, w):
                r = made["rs"]
                if r >= 2:
                    act.wait_ge(s_rsd, r - 1)
                wait_result(act, key)
                if w == T:
                    src, dst = slot(key)[:, 0:T], rs[r % 2][:, 0:T]
                else:
                    src = slot(key)[:].rearrange("p (a c) -> p a c", a=2)[:, :, 0:HALF]
                    dst = rs[r % 2][:].rearrange("p (a c) -> p a c", a=2)
                if made["table"] != LN_EXP:
                    nc.scalar.preload_act_table_set(LN_EXP)
                    made["table"] = LN_EXP
                A.sig(nc.scalar.activation(dst, src, ACT.Ln, bias=eps[:, 0:1], scale=scale), *evac_at(key))
                A.sync()
                A.sig(nc.scalar.activation(dst, dst, ACT.Exp, scale=-0.5), s_rs, r + 1)
                made["rs"] += 1

            def x_high(n, k0=0, c0=0, dst=x_hi):
                for k in range(k0, k0 + n):
                    m = made["x"]
                    act.wait_ge(s_xt, m + 1)
                    o = dst[:, k, c0:TT] if dst is x_hi else dst[:, k, :]
                    A.sig(nc.scalar.activation(o, xt[m % 2][:, c0:TT], ACT.Copy), s_xhi, m + 1)
                    made["x"] += 1

            def copy_out(key, dst, func=ACT.Copy, w=T):
                wait_result(act, key)
                src = slot(key)[:, 0:w] if w != TT else ps_all(key)
                A.sig(nc.scalar.activation(halves(dst) if w == TT else dst, src, func), *evac_at(key))

            def ffn(i, c0):
                width = TT if c0 == 0 else T
                rsqrt(("norm", 2 * i - 1), 1.0 / D, width)
                x_high(KD, c0=c0)
                b0, m0 = BLOCK[("gate", i, 0)], made["x"]
                w_split(b0 + RING - 2)
                act.wait_ge(s_sqd, made["sq"])

                def w_next(b, g, per):
                    b += RING - 1
                    act.wait_ge(s_raw[b % RING], g * (16 * per // RING) + 16 * (b // RING + 1))
                    act.wait_ge(s_used, g * per + (b - RING + 1))
                    nc.scalar.activation(w_hi[b % RING][:], w_raw[b % RING][:], ACT.Copy).then_inc(s_hi, 1)
                made["table"] = None
                with act.Fori(0, KF // 2) as g:
                    for j in range(2):
                        gk = ("gate", i, j)
                        w_next(b0 + 2 * j, g, 4)
                        act.wait_ge(s_used, g * 4 + (b0 + 2 * j + 1))
                        if c0 == 0:
                            ins = nc.scalar.activation(halves(square[j][:]), ps_all(gk), ACT.Silu)
                        else:
                            ins = nc.scalar.activation(square[j][:, 0:T], slot(gk)[:, 0:T], ACT.Silu)
                        s_, v = evac_in(gk, g)
                        ins.then_inc(s_, 1)
                        w_next(b0 + 2 * j + 1, g, 4)
                        act.wait_ge(s_xt, g * 2 + (m0 + j + 1))
                        nc.scalar.activation(f_hi[:, g * 2 + j, c0:TT], xt[j][:, c0:TT], ACT.Copy).then_inc(s_xhi, 1)
                made["x"] += KF
                made["w"] += 2 * KF
                b1 = BLOCK[("down", i, 0)]
                assert made["w"] == b1 + RING - 1
                if i == 1:
                    with act.Fori(0, 2) as g:
                        for j in range(12):
                            w_next(b1 + j, g, 12)
                    made["w"] += 24
                else:
                    w_split(BLOCKS_PADDED - 1)
                act.wait_ge(s_xhi, made["x"])
                wait_evac(act, ("down", i, 7))
                wait_evac(act, ("down", i, 6))

            for i in range(4):
                act.dma_start(h[:, 2 * i:2 * i + 2, TQ], x_dram[:, 2 * i:2 * i + 2]).then_inc(s_x[i], 16)
                if i == 0:
                    act.dma_start(const[:], const_dram[:, 0:N_KEPT]).then_inc(s_const, 16)
            act.dma_start(small[:], small_dram).then_inc(s_small, 16)
            act.dma_start(const1[:], const_dram[:, N_KEPT:N_CONST]).then_inc(s_small, 16)
            act.dma_start(h[:, :, 0:M], meta_dram).then_inc(s_small, 16)
            for i in range(4):
                act.wait_ge(s_x[i], 16)
                squares([h[:, k, TQ] for k in (2 * i, 2 * i + 1)])
            act.wait_ge(s_eps, 1)
            rsqrt(("norm", 0), 1.0 / D, T)
            x_high(KD, c0=M)
            made["table"] = None
            for j in range(12):
                key = ("qkv", j)
                ahead(key)
                wait_evac(act, key)
                nc.scalar.activation(qkv[:, j, :], qkv[:, j, :], ACT.Silu).then_inc(s_silu, 1)
            ahead(("ab",))
            srcs = [qkv[:, j, :] for j in range(8)]
            act.wait_ge(s_silu, 8)
            w_split(BLOCK[("dv", 1)] + RING - 2)
            squares(srcs[:1])
            for i in range(8):
                if i + 1 < 8:
                    squares(srcs[i + 1:i + 2])
                rsqrt(("hn", i), 1.0, T)
                if i % 2:
                    w_split(BLOCK[("dv", 1)] + RING - 2 + (i + 1) // 2)
            for i in range(2):
                wait_result(act, ("dv", i))
                A.sig(nc.scalar.activation(dv[:, 2 * i:2 * i + 2, :].rearrange("p a c -> p (a c)"), slot(("dv", i))[:, :], ACT.Copy), *evac_at(("dv", i)))
            w_split(BLOCK[("dv", 1)] + 3 + RING - 1)
            act.wait_ge(s_df, 1)
            wait_result(act, ("lam",))
            A.sig(nc.scalar.activation(lamt[:, 2:4], slot(("lam",))[:, 0:2], ACT.Exp), *evac_at(("lam",)))
            act.wait_ge(s_g, 1)
            A.own(nc.scalar.activation(tA[:], tA[:], ACT.Exp, scale=-1.0))
            A.own(nc.scalar.activation(beta[:], ab[:, :, 0:4], ACT.Exp, scale=-1.0))
            A.sync()
            A.own(nc.scalar.activation(tA[:], tA[:], ACT.Ln, bias=1.0))
            A.sig(nc.scalar.activation(nea[:], sml("a_log", 0, 4), ACT.Exp), s_da, 1)
            da = [1]

            def dsig(ins):
                da[0] += 1
                A.sig(ins, s_da, da[0])
            point = [0]

            def aside():
                p = point[0]
                point[0] += 1
                for f, key in enumerate(ASIDE_DENSE):
                    if dense_done(f) + 1 == p:
                        wait_result(act, key)
                        name, j = key
                        dst = {"z": sz, "dz": dsz, "dqk": dqk}[name][:, j, :]
                        if name != "dqk":
                            made["table"] = None
                        A.sig(nc.scalar.activation(dst, slot(key)[:, 0:T], ACT.Copy if name == "dqk" else ACT.Silu), *evac_at(key))
                        w_split(BLOCK[key] + RING)
                for i in norm_at(p, 0):
                    A.sync()
                    squares([dqk[:, i, :]])
                for i in norm_at(p, 2):
                    rsqrt(("hn", 8 + i), 1.0 / 64, T)
                if p < DF_START or (p - DF_START) % 2 == 0:
                    return
                s = df_at(p, 0)
                if s is not None:
                    n, i = s % NQ, s % 2
                    w = (n + 1) * P
                    act.wait_ge(s_df, 2 + s)
                    for c in range(2):
                        A.sig(nc.scalar.activation(Sx[i][c][:, 0:w], Sx[i][c][:, 0:w], ACT.Exp, bias=mx[i][:, c:c + 1],
                                                   accum_out=sums_[i][:, c:c + 1]), s_dfa, 2 * s + c + 1)
                e = df_at(p, 2)
                if e is not None:
                    w = (e % NQ + 1) * P
                    key = ("PT", e // NQ, e % NQ)
                    wait_result(act, key)
                    A.sig(nc.scalar.activation(PTs[e % 2][:, 0:w], slot(key)[:, 0:w], ACT.Copy), *evac_at(key))
            for n in range(NQ):
                DT, EG, qg, kb, AT, N, U, Tm, Ns, Y, kdec, kbg, Sd, u, wT, vnew, vb, gB, bB = work(n)
                act.wait_ge(s_dn, dnv("dt", n))
                dsig(nc.scalar.activation(DT[:], DT[:], ACT.Exp))
                A.sig(nc.scalar.activation(EG[:].rearrange("p h c -> p (h c)"), slot(("gcb", n))[:, 0:T], ACT.Exp), *evac_at(("gcb", n)))
                wait_evac(act, ("sm", n))
                dsig(nc.scalar.activation(esm[:], sm[:], ACT.Exp))
                for _ in range(3):
                    aside()
                for l in range(5):
                    wait_result(act, ("Y", n, l))
                    A.sig(nc.scalar.activation(Y[:].rearrange("p h c -> p (h c)"), slot(("Y", n, l))[:, 0:T], ACT.Copy), *evac_at(("Y", n, l)))
                    aside()
                    aside()
                wait_result(act, ("u", n))
                A.sig(nc.scalar.activation(u[:].rearrange("p h c -> p (h c)"), slot(("u", n))[:, 0:T], ACT.Copy), *evac_at(("u", n)))
                aside()
                for c in range(2):
                    aside()
                    wait_result(act, ("o", n, c))
                    A.sig(nc.scalar.activation(qkv[:, 0:4, n * P + c * CH:n * P + c * CH + CH],
                                         slot(("o", n, c))[:, 0:4 * CH].rearrange("p (h c) -> p h c", h=4), ACT.Copy), *evac_at(("o", n, c)))
                    aside()
            while point[0] < LAST_POINT:
                aside()
            wait_evac(act, ("PV", DF_H - 1, NQ - 1))
            A.sync()
            srcs = [qkv[:, j, :] for j in range(4)] + [dqk[:, j, :] for j in range(4)]
            squares(srcs[:1])
            for i in range(8):
                if i + 1 < 8:
                    squares(srcs[i + 1:i + 2])
                rsqrt(("ho", i), 1.0 / P, T)
                if i:
                    x_high(1, i - 1, M)
            x_high(1, 7, M)
            for j in range(8):
                ahead(("wo", j))
            wait_evac(act, ("wo", 7))
            ffn(1, 0)
            act.dma_start(at_rot[:], rot_dram[:, 0:2]).then_inc(s_ixt, 16)
            act.dma_start(ix_rot[:], rot_dram[:, 2:4]).then_inc(s_ixt, 16)
            rsqrt(("norm", 2), 1.0 / D, TT)
            x_high(KD)
            rot = [0]

            def rotate(key, half, w):
                i = rot[0]
                wait_result(act, key)
                if i >= 2:
                    wait_evac(act, ROTATED[i - 2])
                else:
                    act.wait_ge(s_sqd, made["sq"])
                for p in range(0, P, 2 * half):
                    for a, b in ((p, p + half), (p + half, p)):
                        if w == T:
                            ins = nc.scalar.activation(square[i % 2][a:a + half, 0:T], slot(key)[b:b + half, 0:T], ACT.Copy)
                        else:
                            ins = nc.scalar.activation(halves(square[i % 2][:])[a:a + half], ps_all(key)[b:b + half], ACT.Copy)
                        A.own(ins) if (p, a) != (P - 2 * half, P - half) else A.sig(ins, s_rot, i + 1)
                rot[0] += 1
            ahead(("ik",))
            rotate(("ik",), 32, T)
            ahead(("iw",))
            for j in range(4):
                ahead(("iq", j))
                rotate(("iq", j), 32, T)
            for s in range(12):
                key = ("is", 1 + s // 4, s % 4)
                w = (1 + s // 4 + 1) * P
                if s >= 2:
                    act.wait_ge(s_relud, s - 1)
                wait_result(act, key)
                A.sig(nc.scalar.activation(relu[s % 2][:, :, 0:w], slot(key)[:].rearrange("p (a c) -> p a c", a=2)[:, :, 0:w],
                                           ACT.Relu), *evac_at(key))

            def projected(key, blocks):
                name, g = key[0], key[1]
                if name in ("aq", "ak"):
                    rotate(key, 64, T if name == "aq" else TT)
                elif key == ("av", g, 0):
                    copy_out(key, av[g % 2][:].rearrange("p a c -> p (a c)"), w=2 * T)
                elif key == ("av", g, 1):
                    wait_result(act, key)
                    A.sig(nc.scalar.activation(avm[g % 2][0:M, :], slot(key)[0:M, 0:2 * P], ACT.Copy), *evac_at(key))
                else:
                    copy_out(key, ya[g])
                if blocks:
                    w_split(BLOCK[key] + blocks - 1 + RING)
            for key, blocks in projection_keys(0):
                projected(key, blocks)
            for j in range(4):
                copy_out(("ga", j), ya[j], ACT.Sigmoid)
                w_split(BLOCK[("ga", j)] + RING)
            for s in range(ATT_STEPS + 3):
                if s >= 3:
                    e = s - 3
                    n, key = e % NQ, ("AV", e)
                    wait_result(act, key)
                    A.sig(nc.scalar.activation(att_hi[:, e // NQ, n * P:n * P + P], slot(key)[:, 0:P], ACT.Copy), s_athi, e + 1)
                if s < ATT_STEPS:
                    n, i = s % NQ, s % 2
                    w = M + (n + 1) * P
                    act.wait_ge(s_af, s + 1)
                    A.sig(nc.scalar.activation(Ax[i][:, 0:w], Ax[i][:, 0:w], ACT.Exp, bias=amx[i][:, 0:1], scale=ATT_SCALE,
                                               accum_out=asum[i][:, 0:1]), s_afa, s + 1)
                for key, blocks in filled(2 * s - 1):
                    projected(key, blocks)
                if 1 <= s <= ATT_STEPS:
                    e = s - 1
                    n, i = e % NQ, e % 2
                    if e >= 2:
                        wait_result(act, ("AV", e - 2))
                    key = ("AP", e)
                    wait_result(act, key)
                    A.own(nc.scalar.activation(At[i][0:M, 0:P], slot(key)[0:M, 0:P], ACT.Copy))
                    A.sig(nc.scalar.activation(At[i][:, P:P + (n + 1) * P], slot(key)[:, P:P + (n + 1) * P], ACT.Copy), *evac_at(key))
                for key, blocks in filled(2 * s):
                    projected(key, blocks)
            A.sync()
            for j in range(4, KD):
                A.own(nc.scalar.activation(ya[j], ya[j], ACT.Sigmoid))
            A.sync()
            act.sem_inc(s_sigm, 1)
            for j in range(KD):
                ahead(("ao", j))
            def sigmoid(key, i):
                if i >= 2:
                    act.wait_ge(s_gate, i - 1)
                wait_result(act, key)
                A.sig(nc.scalar.activation(square[i % 2][:, 0:T], slot(key)[:, 0:T], ACT.Sigmoid), *evac_at(key))
            for j in range(4):
                wait_evac(act, ("ao", KD - 1 - j))
            act.dma_start(rt_rot[:], rot_dram[:, 4:6]).then_inc(s_rtt, 16)
            for hd in range(RET_H):
                if hd:
                    act.wait_ge(s_rst, 5 * hd)
                act.dma_start(dec[:], dec_dram[:, hd]).then_inc(s_dec, 16)
                for j in range(4):
                    key = ("rq", hd, j) if j < 2 else ("rk", hd, j - 2)
                    ahead(key)
                    if j % 2 == 0 and (hd or j):
                        act.wait_ge(s_rotd, (2 * hd + j // 2))
                    dst = square[j % 2][:, 0:T] if j < 2 else square[j % 2][:]
                    copy_out(key, dst, w=T if j < 2 else TT)
                w_split(BLOCK[("rv", hd, 2)] + 3 + 2)
                for i in range(2):
                    wait_result(act, ("rv", hd, i))
                    A.sig(nc.scalar.activation(rv[:, 2 * i:2 * i + 2, :].rearrange("p a c -> p (a c)"),
                                               slot(("rv", hd, i))[:, :], ACT.Copy), *evac_at(("rv", hd, i)))
                A.sig(nc.scalar.activation(rvm[0:M, :], slot(("rv", hd, 2))[0:M, 0:T], ACT.Copy), *evac_at(("rv", hd, 2)))
                for j in range(2):
                    ahead(("rg", hd, j))
                    made["table"] = None
                    copy_out(("rg", hd, j), rg[:, j, :], ACT.Silu)
                ahead(("rg", hd, 2))
                act.wait_ge(s_rst, 5 * hd + 5)
                for d in range(4):
                    wait_result(act, ("ry", hd, d))
                    squares([slot(("ry", hd, d))[:, 0:T]])
                    copy_out(("ry", hd, d), rqk[:, d, 0:T])
                copy_out(("rg", hd, 2), rg[:, 2, :], ACT.Silu)
                ahead(("rg", hd, 3))
                rsqrt(("rn", hd), 1.0 / T, T)
                x_high(3, 0, M, y_hi)
                made["table"] = None
                copy_out(("rg", hd, 3), rg[:, 3, :], ACT.Silu)
                w_split(BLOCK[("rg", hd, 3)] + 1 + 3)
                x_high(1, 3, M, y_hi)
                for j in range(KD):
                    ahead(("wr", hd, j))
            for j in range(KD):
                ahead(("gr", j))
                sigmoid(("gr", j), j)
                if j:
                    x_high(1, j - 1, M, merged_hi)
            x_high(1, KD - 1, M, merged_hi)
            for j in range(KD):
                ahead(("mx", j))
            wait_evac(act, ("mx", KD - 1))
            ffn(2, M)
            rsqrt(("norm", 4), 1.0 / D, T)
            act.wait_ge(s_y, KD)
            act.dma_start(out_dram, h[:, :, TQ]).then_inc(s_out, 16)
            act.wait_ge(s_out, 16)

        @block.vector
        def _(dve):
            V = Own(dve, s_v)
            owners.append(V)
            made = {"rs": 0, "x": 0, "acc": 0}

            def split(makers, c0=0, k0=0, hi=x_hi, lo=x_lo):
                d0 = c0 if hi is x_hi else 0

                def low(m, k):
                    dve.wait_ge(s_xhi, m + 1)
                    V.sig(nc.vector.tensor_tensor(lo[:, k, d0:], xt[m % 2][:, c0:TT],
                                                  hi[:, k, d0:].bitcast(F32), ALU.subtract), s_xlo, m + 1)
                for i, maker in enumerate(makers):
                    m = made["x"]
                    if i >= 2:
                        V.sync()
                    maker(xt[m % 2][:, c0:TT], m)
                    made["x"] += 1
                    if i:
                        low(m - 1, k0 + i - 1)
                low(made["x"] - 1, k0 + len(makers) - 1)

            def model_norm(gain, c0):
                r = made["rs"]
                dve.wait_ge(s_rs, r + 1)
                split([lambda dst, m, k=k: V.sig(nc.vector.scalar_tensor_tensor(
                    dst, h[:, k, c0:TT], sml(gain, k), rs[r % 2][:, 0:TT - c0], ALU.mult, ALU.mult), s_xt, m + 1)
                    for k in range(KD)], c0)
                V.sync()
                dve.sem_inc(s_rsd, 1)
                made["rs"] += 1

            V.sig(nc.vector.memset(eps[:], EPS), s_eps, 1)
            dve.wait_ge(s_small, 48)
            for i in range(4):
                dve.wait_ge(s_x[i], 16)
            model_norm("norm_gain", M)
            for j in range(12):
                key = ("qkv", j)
                wait_result(dve, key)
                ps = slot(key)
                cw = lambda i: sml("conv", 4 * j + i)
                V.own(nc.vector.tensor_scalar(qkv[:, j, :], ps[:, 0:T], cw(3), None, ALU.mult))
                for i in (1, 2, 3):
                    V.sync()
                    ins = nc.vector.scalar_tensor_tensor(qkv[:, j, i:T], ps[:, 0:T - i], cw(3 - i), qkv[:, j, i:T],
                                                         ALU.mult, ALU.add)
                    if i < 3:
                        V.own(ins)
                    else:
                        V.sig(ins, *evac_at(key))
            key = ("ab",)
            wait_result(dve, key)
            V.sig(nc.vector.tensor_copy(ab[:].rearrange("p n c -> p (n c)"), slot(key)[:, 0:NQ * 8]), *evac_at(key))
            V.sync()
            dtb = sml("dt_bias", 0, 4).unsqueeze(1).broadcast_to([P, NQ, 4])
            V.own(nc.vector.tensor_tensor(g[:], ab[:, :, 4:8], dtb, ALU.add))
            V.sync()
            V.own(nc.vector.tensor_scalar(tA[:], g[:], -1.0, None, ALU.mult))
            V.sync()
            V.own(nc.vector.tensor_tensor(tA[:], tA[:], g[:], ALU.max))
            V.sync()
            V.sig(nc.vector.tensor_scalar(tB[:], g[:], 0.0, None, ALU.max), s_g, 1)
            def head_norm(i):
                r = made["rs"]
                dve.wait_ge(s_rs, r + 1)
                if i < 8:
                    t, gain, const_s = qkv[:, i, :], (P ** -0.5 if i < 4 else 1.0), None
                    V.sig(nc.vector.scalar_tensor_tensor(t, t, gain, rs[r % 2][:, 0:T], ALU.mult, ALU.mult), s_rsd, r + 1)
                else:
                    t = dqk[:, i - 8, :]
                    gain = sml("q_gain" if i < 12 else "k_gain")
                    V.sig(nc.vector.scalar_tensor_tensor(t, t, gain, rs[r % 2][:, 0:T], ALU.mult, ALU.mult), s_rsd, r + 1)
                    if i < 12:
                        V.sync()
                        V.own(nc.vector.tensor_scalar(t, t, 64 ** -0.5, None, ALU.mult))
                made["rs"] += 1
            V.own(nc.vector.tensor_tensor(lamt[0:64, 0:1], sml("lq1")[0:64], sml("lk1")[0:64], ALU.mult))
            V.sig(nc.vector.tensor_tensor(lamt[0:64, 1:2], sml("lq2")[0:64], sml("lk2")[0:64], ALU.mult), s_df, 1)
            for i in range(8):
                head_norm(i)
            wait_evac(dve, ("lam",))
            V.own(nc.vector.scalar_tensor_tensor(lamt[:, 4:5], lamt[:, 2:3], LAMBDA_INIT, lamt[:, 3:4], ALU.add, ALU.subtract))
            V.sync()
            V.own(nc.vector.tensor_scalar(lamt[:, 5:6], lamt[:, 4:5], -1.0, None, ALU.mult))
            dve.wait_ge(s_da, 1)
            V.own(nc.vector.tensor_tensor(tB[:], tB[:], tA[:], ALU.add))
            V.own(nc.vector.tensor_scalar(beta[:], beta[:], 1.0, None, ALU.add))
            V.sync()
            V.own(nc.vector.reciprocal(beta[:], beta[:]))
            V.own(nc.vector.scalar_tensor_tensor(g[:], tB[:], -1.0, nea[:].unsqueeze(1).broadcast_to([P, NQ, 4]), ALU.mult, ALU.mult))
            V.sync()
            dn = [0]

            def dsig(ins, name, n):
                dn[0] += 1
                assert dn[0] == dnv(name, n), (name, n)
                V.sig(ins, s_dn, dn[0])

            def per_token(ap):
                return ap.unsqueeze(2).broadcast_to([P, 4, P])

            def per_head(name):
                return K(name).unsqueeze(1).broadcast_to([P, 4, P])
            point = [0]

            def aside():
                p = point[0]
                point[0] += 1
                for i in norm_at(p, 3):
                    head_norm(8 + i)
                if p < DF_START or (p - DF_START) % 2 == 0:
                    return
                e = df_at(p, 1)
                if e is not None:
                    j, n, i = e // NQ, e % NQ, e % 2
                    w = (n + 1) * P
                    dve.wait_ge(s_dfa, 2 * e + 2)
                    V.own(nc.vector.reciprocal(sums_[i][:], sums_[i][:]))
                    V.sync()
                    V.own(nc.vector.tensor_scalar(sums_[i][:, 1:2], sums_[i][:, 1:2], lamt[:, 5:6], None, ALU.mult))
                    V.sync()
                    V.own(nc.vector.tensor_scalar(Sx[i][1][:, 0:w], Sx[i][1][:, 0:w], sums_[i][:, 1:2], None, ALU.mult))
                    V.sync()
                    if e >= 2:
                        wait_result(dve, ("PT", (e - 2) // NQ, (e - 2) % NQ))
                    V.sig(nc.vector.scalar_tensor_tensor(Pm[i][:, 0:w], Sx[i][0][:, 0:w], sums_[i][:, 0:1], Sx[i][1][:, 0:w],
                                                         ALU.mult, ALU.add), s_dfp, e + 1)
                s = df_at(p, 0)
                if s is not None:
                    j, n, i = s // NQ, s % NQ, s % 2
                    w = (n + 1) * P
                    key = ("S", j, n)
                    wait_result(dve, key)
                    for c in range(2):
                        ins = nc.vector.tensor_tensor_reduce(Sx[i][c][:, 0:w], slot(key)[:, c * 512:c * 512 + w],
                                                             K("causal")[:, T - w:T], 1.0, NEG, ALU.add, ALU.max, mx[i][:, c:c + 1])
                        V.own(ins) if c == 0 else V.sig(ins, *evac_at(key))
                    V.sync()
                    V.sig(nc.vector.tensor_scalar(mx[i][:], mx[i][:], -1.0, None, ALU.mult), s_df, 2 + s)
                e = df_at(p, 3)
                if e is not None:
                    j, n = e // NQ, e % NQ
                    key = ("PV", j, n)
                    wait_result(dve, key)
                    V.sig(nc.vector.tensor_copy(dqk[:, j, n * P:n * P + P], slot(key)[:, 0:P]), *evac_at(key))
            for n in range(NQ):
                tok = slice(n * P, n * P + P)
                DT, EG, qg, kb, AT, N, U, Tm, Ns, Y, kdec, kbg, Sd, u, wT, vnew, vb, gB, bB = work(n)
                V.sync()
                if n == 2:
                    wait_result(dve, ASIDE_DENSE[-1])
                if n:
                    wait_result(dve, ("beb", n - 1))
                V.own(nc.vector.tensor_copy(bB[:], per_token(beta[:, n, :])))
                dsig(nc.vector.tensor_copy(gB[:], per_token(g[:, n, :])), "gB", n)
                wait_result(dve, ("sm", n))
                V.sig(nc.vector.tensor_copy(sm[:], slot(("sm", n))[:, 0:16]), *evac_at(("sm", n)))
                V.sync()
                for hd in range(4):
                    ins = nc.vector.tensor_scalar(DT[:, hd, :], slot(("gcb", n))[:, hd * P:hd * P + P], sm[:, hd:hd + 1], 0.0,
                                                  ALU.subtract, ALU.min)
                    if hd < 3:
                        V.own(ins)
                    else:
                        dsig(ins, "dt", n)
                V.sig(nc.vector.tensor_tensor(kb[:], qkv[:, 4:8, tok], heads(slot(("beb", n))[:, 0:T]), ALU.mult), *evac_at(("beb", n)))
                wait_evac(dve, ("gcb", n))
                V.own(nc.vector.tensor_tensor(DT[:], DT[:], per_head("tri"), ALU.mult))
                dsig(nc.vector.tensor_tensor(qg[:], qkv[:, 0:4, tok], EG[:], ALU.mult), "qg", n)
                aside()
                aside()
                wait_result(dve, ("N0", n))
                V.sync()
                V.sig(nc.vector.tensor_tensor(N[:], heads(slot(("N0", n))[:, 0:T]), DT[:], ALU.mult), *evac_at(("N0", n)))
                V.sync()
                V.own(nc.vector.tensor_tensor(U[:], N[:], per_head("join0"), ALU.mult))
                V.sync()
                dsig(nc.vector.scalar_tensor_tensor(U[:].rearrange("p h c -> p h c"), U[:], -1.0, per_head("ident"), ALU.mult, ALU.add), "U", n)
                wait_result(dve, ("A0", n))
                V.sig(nc.vector.tensor_tensor(AT[:], heads(slot(("A0", n))[:, 0:T]), DT[:], ALU.mult), *evac_at(("A0", n)))
                wait_result(dve, ("T1", n))
                V.sig(nc.vector.tensor_copy(Tm[:].rearrange("p h c -> p (h c)"), slot(("T1", n))[:, 0:T]), *evac_at(("T1", n)))
                V.sync()
                aside()
                dsig(nc.vector.tensor_tensor(Ns[0][:], N[:], per_head("join1"), ALU.mult), "Ns0", n)
                for l in range(5):
                    if l < 4:
                        dsig(nc.vector.tensor_tensor(Ns[(l + 1) % 2][:], N[:], per_head(f"join{l + 2}"), ALU.mult), f"Ns{l + 1}", n)
                    if l == 0:
                        dve.wait_ge(s_da, 1 + 2 * n + 2)
                        V.own(nc.vector.tensor_tensor(cb[:], esm[:, 0:4], beta[:, n, :], ALU.mult))
                        wait_result(dve, ("kt", n))
                        V.sync()
                        V.own(nc.vector.tensor_tensor(kdec[:], heads(slot(("kt", n))[:, 0:T]), per_token(esm[:, 4:8]), ALU.mult))
                        V.sig(nc.vector.tensor_tensor(kbg[:], heads(slot(("kt", n))[:, 0:T]), per_token(cb[:]), ALU.mult), *evac_at(("kt", n)))
                        wait_result(dve, ("vt", n))
                        V.sig(nc.vector.tensor_tensor(vb[:], heads(slot(("vt", n))[:, 0:T]), per_token(beta[:, n, :]), ALU.mult), *evac_at(("vt", n)))
                    aside()
                    aside()
                    if l < 4:
                        wait_result(dve, ("dT", n, l))
                        V.sig(nc.vector.tensor_tensor(Tm[:], Tm[:], heads(slot(("dT", n, l))[:, 0:T]), ALU.subtract), *evac_at(("dT", n, l)))
                    wait_result(dve, ("dU", n, l))
                    V.sig(nc.vector.tensor_tensor(U[:], U[:], heads(slot(("dU", n, l))[:, 0:T]), ALU.subtract), *evac_at(("dU", n, l)))
                    V.sync()
                wait_result(dve, ("wT", n))
                V.sig(nc.vector.tensor_copy(wT[:].rearrange("p h c -> p (h c)"), slot(("wT", n))[:, 0:T]), *evac_at(("wT", n)))
                aside()
                wait_evac(dve, ("u", n))
                for c in range(2):
                    rr = slice(c * CH, c * CH + CH)
                    i = 2 * n + c
                    old, new = St[i % 2], St[(i + 1) % 2]
                    if i:
                        wait_result(dve, ("wS", n, c))
                        V.sig(nc.vector.tensor_tensor(vnew[rr], u[rr], heads(slot(("wS", n, c))[rr, 0:T]), ALU.subtract), *evac_at(("wS", n, c)))
                    aside()
                    if i == 2 * NQ - 1:
                        aside()
                        continue
                    if i:
                        V.own(nc.vector.tensor_tensor(Sd[:], old[:], per_token(esm[:, 8 + 4 * c:12 + 4 * c]), ALU.mult))
                        V.sync()
                    wait_result(dve, ("dS", n, c))
                    if i:
                        V.sig(nc.vector.tensor_tensor(new[:], Sd[:], heads(slot(("dS", n, c))[:, 0:T]), ALU.add), *evac_at(("dS", n, c)))
                    else:
                        V.sig(nc.vector.tensor_copy(new[:].rearrange("p h c -> p (h c)"), slot(("dS", n, c))[:, 0:T]), *evac_at(("dS", n, c)))
                    V.sync()
                    aside()
            while point[0] < LAST_POINT:
                aside()
            def head_out(i):
                t = qkv[:, i, :] if i < 4 else dqk[:, i - 4, :]

                def maker(dst, m):
                    r = made["rs"]
                    dve.wait_ge(s_rs, r + 1)
                    V.own(nc.vector.scalar_tensor_tensor(dst, t, sml("dn_gain" if i < 4 else "df_gain"), rs[r % 2][:, 0:T],
                                                         ALU.mult, ALU.mult))
                    V.sync()
                    dve.sem_inc(s_rsd, 1)
                    made["rs"] += 1
                    z = sz[:, i, :] if i < 4 else dsz[:, i - 4, :]
                    V.sig(nc.vector.scalar_tensor_tensor(dst, dst, 1.0 if i < 4 else 1.0 - LAMBDA_INIT, z, ALU.mult, ALU.mult), s_xt, m + 1)
                return maker
            split([head_out(i) for i in range(8)], c0=M)

            def add_to_h(key, c0):
                j = key[-1]
                if j == 0:
                    V.own(nc.vector.memset(square[1][:], 0.0))
                wait_result(dve, key)
                V.sig(nc.vector.tensor_tensor(h[:, j, TQ], h[:, j, TQ], slot(key)[:, 0:T], ALU.add), *evac_at(key))
                V.sync()
                w = TT - c0
                V.sig(nc.vector.tensor_tensor(square[0][:, 0:w], h[:, j, c0:TT], h[:, j, c0:TT], ALU.mult), s_acc, made["acc"] + 1)
                V.sync()
                V.sig(nc.vector.tensor_tensor(square[1][:, 0:w], square[1][:, 0:w], square[0][:, 0:w], ALU.add), s_acc, made["acc"] + 2)
                made["acc"] += 2
            for j in range(KD):
                add_to_h(("wo", j), 0)

            def ffn(i, c0):
                V.sync()
                model_norm(f"f{i}_gain", c0)
                b0, m0 = BLOCK[("gate", i, 0)], made["x"]
                wide = c0 == 0
                with dve.Fori(0, KF // 2) as g:
                    for j in range(2):
                        up = ("up", i, j)
                        dve.wait_ge(s_used, g * 4 + (b0 + 2 * j + 2))
                        s_, v = evac_in(("gate", i, j), g)
                        dve.wait_ge(s_, v)
                        dve.wait_ge(s_xlo, g * 2 + (m0 + j))
                        s_, v = evac_in(up, g)
                        a, b, o = square[j][:, 0:TT - c0], slot(up)[:, 0:T], xt[j][:, c0:TT]
                        if wide:
                            a, b, o = halves(a), ps_all(up), halves(o)
                        ins = nc.vector.tensor_tensor(o, a, b, ALU.mult)
                        ins.then_inc(s_, 1)
                        dve.wait_ge(s_, v)
                        dve.sem_inc(s_xt, 1)
                        dve.wait_ge(s_xhi, g * 2 + (m0 + j + 1))
                        nc.vector.tensor_tensor(f_lo[:, g * 2 + j, c0:TT], xt[j][:, c0:TT],
                                                f_hi[:, g * 2 + j, c0:TT].bitcast(F32), ALU.subtract).then_inc(s_xlo, 1)
                made["x"] += KF
                b1, a0, w = BLOCK[("down", i, 0)], made["acc"], TT - c0
                V.last = (s_xlo, made["x"])
                V.sync()
                V.own(nc.vector.memset(square[1][:], 0.0))
                V.sync()
                with dve.Fori(0, 2) as g:
                    for j in range(4):
                        key = ("down", i, j)
                        dve.wait_ge(s_used, g * 12 + (b1 + 3 * j + 3))
                        hh = h[:, g * 4 + j, c0:TT]
                        src = slot(key)[:, 0:T]
                        if wide:
                            hh, src = halves(hh), ps_all(key)
                        s_, v = evac_in(key, g)
                        nc.vector.scalar_tensor_tensor(hh, src, 0.5, hh, ALU.mult, ALU.add).then_inc(s_, 1)
                        dve.wait_ge(s_, v)
                        hh = h[:, g * 4 + j, c0:TT]
                        nc.vector.tensor_tensor(square[0][:, 0:w], hh, hh, ALU.mult).then_inc(s_acc, 1)
                        dve.wait_ge(s_acc, g * 8 + (a0 + 2 * j + 1))
                        nc.vector.tensor_tensor(square[1][:, 0:w], square[1][:, 0:w], square[0][:, 0:w],
                                                ALU.add).then_inc(s_acc, 1)
                        dve.wait_ge(s_acc, g * 8 + (a0 + 2 * j + 2))
                made["acc"] += 16
                V.last = (s_acc, made["acc"])
                V.sync()
            ffn(1, 0)
            model_norm("mix_gain", 0)
            rot = [0]
            dve.wait_ge(s_ixt, 32)

            def rotated(key, table, dst, w):
                i = rot[0]
                c0 = TT - w
                dve.wait_ge(s_rot, i + 1)
                src = slot(key)[:, 0:T] if w == T else ps_all(key)
                tab = lambda k: table[:, k, c0:TT] if w == T else halves(table[:, k, :])
                d = dst if w == T else halves(dst)
                other = square[i % 2][:, 0:T] if w == T else halves(square[i % 2][:])
                V.own(nc.vector.tensor_tensor(other, other, tab(1), ALU.mult))
                V.own(nc.vector.tensor_tensor(d, src, tab(0), ALU.mult))
                V.sync()
                V.sig(nc.vector.tensor_tensor(d, d, other, ALU.add), *evac_at(key))
                rot[0] += 1
            rotated(("ik",), ix_rot, ik[:], T)
            wait_result(dve, ("iw",))
            V.sig(nc.vector.tensor_scalar(iw[:].rearrange("p n c -> p (n c)"), slot(("iw",))[:, 0:NQ * 8], IDX_SCALE, None, ALU.mult),
                  *evac_at(("iw",)))
            for j in range(4):
                rotated(("iq", j), ix_rot, iq[:, j, :], T)
            V.own(nc.vector.memset(bias[:, :, 0:M], 0.0))
            V.own(nc.vector.tensor_copy(bias[:, 0, M:M + P], K("causal")[:, T - P:T]))
            for s in range(12):
                n, j = 1 + s // 4, s % 4
                w = (n + 1) * P
                key = ("is", n, j)
                wait_evac(dve, key)
                for a in range(2):
                    V.sync()
                    before = K("causal")[:, T - w:T] if (j, a) == (0, 0) else score[n - 1][:, 0:w]
                    ins = nc.vector.scalar_tensor_tensor(score[n - 1][:, 0:w], relu[s % 2][:, a, 0:w], iw[:, n, 2 * j + a:2 * j + a + 1],
                                                         before, ALU.mult, ALU.add)
                    V.own(ins) if a == 0 else V.sig(ins, s_relud, s + 1)
            rounds = [K_TOP // 8]

            def top(k):
                for _ in range(k):
                    rounds[0] -= 1
                    V.sync()
                    for n in range(1, NQ):
                        V.own(nc.vector.max(top8[:, n - 1, :], score[n - 1][:, 0:(n + 1) * P]))
                    V.sync()
                    for n in range(1, NQ):
                        w = (n + 1) * P
                        V.own(nc.vector.match_replace(score[n - 1][:, 0:w], top8[:, n - 1, :], score[n - 1][:, 0:w], TAKEN))
                if not rounds[0]:
                    V.sync()
                    for n in range(1, NQ):
                        w = (n + 1) * P
                        V.own(nc.vector.tensor_scalar(score[n - 1][:, 0:w], score[n - 1][:, 0:w], TAKEN, NEG, ALU.not_equal, ALU.mult))
                    V.sync()
                    for n in range(1, NQ):
                        w = (n + 1) * P
                        V.own(nc.vector.tensor_tensor(bias[:, n, M:M + w], score[n - 1][:, 0:w], K("causal")[:, T - w:T], ALU.add))

            def projected(key):
                if key[0] in ("aq", "ak"):
                    name, g, j = key
                    rotated(key, at_rot, (aq if name == "aq" else ak)[g % 2][:, j, :], T if name == "aq" else TT)
            for key, _ in projection_keys(0):
                projected(key)
                if key[0] in ("aq", "ak"):
                    top(2)
            top(rounds[0])
            V.sync()
            for s in range(ATT_STEPS + 3):
                if 1 <= s <= ATT_STEPS:
                    e = s - 1
                    n, i = e % NQ, e % 2
                    w = M + (n + 1) * P
                    dve.wait_ge(s_afa, e + 1)
                    V.own(nc.vector.reciprocal(asum[i][:], asum[i][:]))
                    V.sync()
                    V.sig(nc.vector.tensor_scalar(Ax[i][:, 0:w], Ax[i][:, 0:w], asum[i][:, 0:1], None, ALU.mult), s_afp, e + 1)
                if s < ATT_STEPS:
                    n, i = s % NQ, s % 2
                    w = M + (n + 1) * P
                    key = ("AS", s)
                    if s >= 2:
                        wait_result(dve, ("AP", s - 2))
                    wait_result(dve, key)
                    V.sig(nc.vector.tensor_tensor_reduce(Ax[i][:, 0:w], slot(key)[:, 0:w], bias[:, n, 0:w], 1.0, NEG,
                                                         ALU.add, ALU.max, amx[i][:, 0:1]), *evac_at(key))
                    V.sync()
                    V.sig(nc.vector.tensor_scalar(amx[i][:], amx[i][:], -ATT_SCALE, None, ALU.mult), s_af, s + 1)
                for key, _ in filled(2 * s - 1):
                    projected(key)
                if s >= 3:
                    e = s - 3
                    n, key = e % NQ, ("AV", e)
                    dve.wait_ge(s_athi, e + 1)
                    V.sig(nc.vector.tensor_tensor(att_lo[:, e // NQ, n * P:n * P + P], slot(key)[:, 0:P],
                                                  att_hi[:, e // NQ, n * P:n * P + P].bitcast(F32), ALU.subtract), *evac_at(key))
                for key, _ in filled(2 * s):
                    projected(key)
            dve.wait_ge(s_sigm, 1)
            for j in range(KD):
                key = ("ao", j)
                wait_result(dve, key)
                V.sig(nc.vector.tensor_tensor(ya[j], slot(key)[:, 0:T], ya[j], ALU.mult), *evac_at(key))
            dve.wait_ge(s_rtt, 16)
            for hd in range(RET_H):
                for a, (name, w) in enumerate((("rq", T), ("rk", TT))):
                    for j in range(2):
                        wait_evac(dve, (name, hd, j))
                    x1, x2 = square[0][:, 0:w], square[1][:, 0:w]
                    o1, o2 = rqk[:, 2 * a, 0:w], rqk[:, 2 * a + 1, 0:w]
                    cos, sin = rt_rot[:, 0, TT - w:TT], rt_rot[:, 1, TT - w:TT]
                    V.sync()
                    V.own(nc.vector.tensor_tensor(o1, x1, cos, ALU.mult))
                    V.own(nc.vector.tensor_tensor(o2, x2, cos, ALU.mult))
                    V.own(nc.vector.tensor_tensor(x2, x2, sin, ALU.mult))
                    V.own(nc.vector.tensor_tensor(x1, x1, sin, ALU.mult))
                    V.sync()
                    V.own(nc.vector.tensor_tensor(o1, o1, x2, ALU.subtract))
                    V.sig(nc.vector.tensor_tensor(o2, o2, x1, ALU.add), s_rotd, 2 * hd + a + 1)
                dve.wait_ge(s_dec, 16 * (hd + 1))
                for kt in range(NQ + 1):
                    key = ("rs", hd, kt)
                    wait_result(dve, key)
                    if kt < NQ:
                        w = T - kt * P
                        ins = nc.vector.tensor_tensor(rst[:, kt, kt * P:T], slot(key)[:, 0:w], dec[:, 0, 0:w], ALU.mult)
                    else:
                        ins = nc.vector.tensor_tensor(rstm[0:M, :], slot(key)[0:M, 0:T], dec[0:M, 1, :], ALU.mult)
                    V.sig(ins, *evac_at(key))
                    V.sync()
                    dve.sem_inc(s_rst, 1)

                for d in range(3):
                    wait_evac(dve, ("ry", hd, d))
                    wait_evac(dve, ("rg", hd, d))
                    V.own(nc.vector.tensor_tensor(rqk[:, d, 0:T], rqk[:, d, 0:T], rg[:, d, :], ALU.mult))
                V.sync()

                def ret_out(d):
                    def maker(dst, m):
                        r = made["rs"]
                        if d == 0:
                            dve.wait_ge(s_rs, r + 1)
                        src = rqk[:, d, 0:T]
                        if d == 3:
                            wait_evac(dve, ("rg", hd, 3))
                            V.own(nc.vector.tensor_tensor(src, src, rg[:, 3, :], ALU.mult))
                            V.sync()
                        V.sig(nc.vector.tensor_tensor(dst, src, rs[r % 2][:, 0:T], ALU.mult), s_xt, m + 1)
                    return maker
                split([ret_out(d) for d in range(4)], M, 0, y_hi, y_lo)
                V.sync()
                dve.sem_inc(s_rsd, 1)
                made["rs"] += 1
                for j in range(KD):
                    key = ("wr", hd, j)
                    wait_result(dve, key)
                    if hd == 0:
                        V.sig(nc.vector.tensor_copy(yr[:, j, :], slot(key)[:, 0:T]), *evac_at(key))
                    else:
                        V.sig(nc.vector.tensor_tensor(yr[:, j, :], yr[:, j, :], slot(key)[:, 0:T], ALU.add), *evac_at(key))
            def merge(j):
                def maker(dst, m):
                    wait_evac(dve, ("gr", j))
                    V.sync()
                    V.sig(nc.vector.tensor_tensor(yr[:, j, :], yr[:, j, :], square[j % 2][:, 0:T], ALU.mult), s_gate, j + 1)
                    V.sync()
                    V.sig(nc.vector.tensor_tensor(dst, yr[:, j, :], ya[j], ALU.add), s_xt, m + 1)
                return maker
            split([merge(j) for j in range(KD)], M, 0, merged_hi, merged_lo)
            for j in range(KD):
                add_to_h(("mx", j), M)
            ffn(2, M)
            r = made["rs"]
            dve.wait_ge(s_rs, r + 1)
            for k in range(KD):
                V.sig(nc.vector.scalar_tensor_tensor(h[:, k, TQ], h[:, k, TQ], sml("final_gain", k), rs[r % 2][:, 0:T],
                                                     ALU.mult, ALU.mult), s_y, k + 1)

        @block.tensor
        def _(pe):
            done = {"sq": 0}

            def begin(key):
                for last in FREE[key]:
                    wait_evac(pe, last)
                return slot(key)

            def mm(out, lhsT, rhs, start, stop):
                return nc.tensor.matmul(out, lhsT, rhs, start=start, stop=stop)

            def mm3(out, a, b, start, stop):
                mm(out, a[0], b[0], start, False)
                mm(out, a[1], b[0], False, False)
                return mm(out, a[0], b[1], False, stop)

            def sums(key, n, w, ones="ones"):
                ps = begin(key)
                for i in range(n):
                    q = done["sq"]
                    pe.wait_ge(s_sq, q + 1)
                    if w == T:
                        m = mm(ps[:, 0:T], K(ones), square[q % 2][:, 0:T], i == 0, i == n - 1)
                    else:
                        for a in range(2):
                            m = mm(ps[:, a * 512:a * 512 + HALF], K(ones), square[q % 2][:, a * HALF:a * HALF + HALF], i == 0, i == n - 1)
                    m.then_inc(s_sqd, 1)
                    done["sq"] += 1
                pe.wait_ge(s_sqd, done["sq"])
                pe.sem_inc(s_res, 1)

            def total(key, n, w):
                ps = begin(key)
                pe.wait_ge(s_acc, 2 * KD * n)
                if w == T:
                    m = mm(ps[:, 0:T], K("ones"), square[1][:, 0:T], True, True)
                else:
                    for a in range(2):
                        m = mm(ps[:, a * 512:a * 512 + HALF], K("ones"), square[1][:, a * HALF:a * HALF + HALF], True, True)
                m.then_inc(s_res, 1)

            def dense(key, parts, ktiles=KD, x=(x_hi, x_lo), per=8, made_before=None):
                ps = begin(key)
                b = BLOCK[key]
                k = 0
                for i in range(-(-ktiles // per)):
                    pe.wait_ge(s_lo, b + i + 1)
                    w = (w_hi[(b + i) % RING], w_lo[(b + i) % RING])
                    for j in range(min(per, ktiles - k)):
                        if made_before is not None:
                            pe.wait_ge(s_xlo, made_before + k + 1)
                        for o0, c0, c1 in parts:
                            m = mm3(ps[:, o0:o0 + c1 - c0], (w[0][:, j * P:j * P + P], w[1][:, j * P:j * P + P]),
                                    (x[0][:, k, c0:c1], x[1][:, k, c0:c1]), k == 0, k == ktiles - 1)
                        k += 1
                    m.then_inc(s_used, 1)

            SEQ = [(0, M, TT)]
            ALL = [(0, 0, HALF), (512, HALF, TT)]

            pe.wait_ge(s_const, 16)
            sums(("norm", 0), KD, T)
            pe.wait_ge(s_small, 48)
            for j in range(12):
                dense(("qkv", j), SEQ, made_before=0 if j == 0 else None)
            ps = begin(("ab",))
            b = BLOCK[("ab",)]
            pe.wait_ge(s_lo, b + 1)
            for n in range(NQ):
                tk = slice(M + n * P, M + n * P + P)
                for k in range(KD):
                    m = mm3(ps[:, n * 8:n * 8 + 8], (x_hi[:, k, tk], x_lo[:, k, tk]),
                            (w_hi[b % RING][:, k * P:k * P + 8], w_lo[b % RING][:, k * P:k * P + 8]), k == 0, k == KD - 1)
            m.then_inc(s_used, 1)
            sl = [begin(("dv", 0)), begin(("dv", 1))]
            b = BLOCK[("dv", 1)]
            for i in range(4):
                pe.wait_ge(s_lo, b + i + 1)
                w = (w_hi[(b + i) % RING], w_lo[(b + i) % RING])
                for kk in range(2):
                    k = 2 * i + kk
                    for n in range(NQ):
                        tk = slice(M + n * P, M + n * P + P)
                        m = mm3(sl[n // 2][:, (n % 2) * 512:(n % 2) * 512 + 512], (x_hi[:, k, tk], x_lo[:, k, tk]),
                                (w[0][:, kk * 512:kk * 512 + 512], w[1][:, kk * 512:kk * 512 + 512]), k == 0, k == KD - 1)
                m.then_inc(s_used, 1)
                for j in range(2):
                    sums(("hn", 2 * i + j), 1, T)
            pe.wait_ge(s_df, 1)
            ps = begin(("lam",))
            mm(ps[:, 0:2], K("ones")[0:64], lamt[0:64, 0:2], True, True).then_inc(s_res, 1)

            def four(key, f):
                ps = begin(key)
                for hd in range(4):
                    m = f(ps[:, hd * P:hd * P + P], hd)
                m.then_inc(s_res, 1)
            point = [0]

            def aside():
                p = point[0]
                point[0] += 1
                for t in range(p * PIECE, min((p + 1) * PIECE, 8 * len(ASIDE_DENSE))):
                    f, k = divmod(t, 8)
                    key = ASIDE_DENSE[f]
                    b = BLOCK[key]
                    if k == 0:
                        begin(key)
                        pe.wait_ge(s_lo, b + 1)
                    m = mm3(slot(key)[:, 0:T], (w_hi[b % RING][:, k * P:k * P + P], w_lo[b % RING][:, k * P:k * P + P]),
                            (x_hi[:, k, TQ], x_lo[:, k, TQ]), k == 0, k == KD - 1)
                    if k == KD - 1:
                        m.then_inc(s_used, 1)
                for i in norm_at(p, 1):
                    sums(("hn", 8 + i), 1, T, "ones64")
                if p < DF_START or (p - DF_START) % 2:
                    return
                s = df_at(p, 0)
                if s is not None:
                    j, n = s // NQ, s % NQ
                    ps = begin(("S", j, n))
                    for c in range(2):
                        r = slice(64 * c, 64 * c + 64)
                        m = mm(ps[:, c * 512:c * 512 + (n + 1) * P], dqk[r, j, n * P:n * P + P], dqk[r, 4 + j, 0:(n + 1) * P], True, True)
                    m.then_inc(s_res, 1)
                e = df_at(p, 2)
                if e is not None:
                    j, n, i = e // NQ, e % NQ, e % 2
                    pe.wait_ge(s_dfp, e + 1)
                    ps = begin(("PT", j, n))
                    for kt in range(n + 1):
                        m = nc.tensor.transpose(ps[:, kt * P:kt * P + P], Pm[i][:, kt * P:kt * P + P], K("ident"))
                    m.then_inc(s_res, 1)
                e = df_at(p, 3)
                if e is not None:
                    j, n, i = e // NQ, e % NQ, e % 2
                    wait_evac(pe, ("PT", j, n))
                    ps = begin(("PV", j, n))
                    for kt in range(n + 1):
                        m = mm(ps[:, 0:P], dv[:, kt, j * P:j * P + P], PTs[i][:, kt * P:kt * P + P], kt == 0, kt == n)
                    m.then_inc(s_res, 1)
            for n in range(NQ):
                tok = slice(n * P, n * P + P)
                DT, EG, qg, kb, AT, N, U, Tm, Ns, Y, kdec, kbg, Sd, u, wT, vnew, vb, gB, bB = work(n)
                pe.wait_ge(s_dn, dnv("gB", n))
                four(("gcb", n), lambda o, hd: mm(o, gB[:, hd, :], K("tri"), True, True))
                four(("beb", n), lambda o, hd: mm(o, bB[:, hd, :], K("ident"), True, True))
                ps = begin(("sm", n))
                for i, name in enumerate(("tri", "suffix", "chunk0", "chunk1")):
                    m = mm(ps[:, 4 * i:4 * i + 4], K(name), g[:, n, :], True, True)
                m.then_inc(s_res, 1)
                aside()
                pe.wait_ge(s_dn, dnv("qg", n))
                four(("N0", n), lambda o, hd: mm(o, qkv[:, 4 + hd, tok], kb[:, hd, :], True, True))
                four(("A0", n), lambda o, hd: mm(o, qkv[:, 4 + hd, tok], qkv[:, hd, tok], True, True))
                aside()
                pe.wait_ge(s_dn, dnv("U", n))
                four(("T1", n), lambda o, hd: nc.tensor.transpose(o, U[:, hd, :], K("ident")))
                four(("kt", n), lambda o, hd: nc.tensor.transpose(o, qkv[:, 4 + hd, tok], K("ident")))
                four(("vt", n), lambda o, hd: nc.tensor.transpose(o, qkv[:, 8 + hd, tok], K("ident")))
                aside()
                for l in range(5):
                    pe.wait_ge(s_dn, dnv(f"Ns{l}", n))
                    if l:
                        wait_evac(pe, ("dT", n, l - 1))
                    four(("Y", n, l), lambda o, hd: mm(o, Ns[l % 2][:, hd, :], Tm[:, hd, :], True, True))
                    aside()
                    wait_evac(pe, ("Y", n, l))
                    if l:
                        wait_evac(pe, ("dU", n, l - 1))
                    if l < 4:
                        four(("dT", n, l), lambda o, hd: mm(o, U[:, hd, :], Y[:, hd, :], True, True))
                    four(("dU", n, l), lambda o, hd: mm(o, Y[:, hd, :], U[:, hd, :], True, True))
                    aside()
                wait_evac(pe, ("dU", n, 4))
                wait_evac(pe, ("vt", n))
                four(("u", n), lambda o, hd: mm(o, U[:, hd, :], vb[:, hd, :], True, True))
                four(("wT", n), lambda o, hd: mm(o, kbg[:, hd, :], U[:, hd, :], True, True))
                aside()
                for c in range(2):
                    rr = slice(c * CH, c * CH + CH)
                    i = 2 * n + c
                    old = St[i % 2]
                    if i:
                        wait_evac(pe, ("dS", (i - 1) // 2, (i - 1) % 2))
                        wait_evac(pe, ("wT", n))
                        ps = begin(("wS", n, c))
                        for hd in range(4):
                            m = mm(ps[rr, hd * P:hd * P + P], wT[:, hd, rr], old[:, hd, :], True, True)
                        m.then_inc(s_res, 1)
                    aside()
                    if i:
                        wait_evac(pe, ("wS", n, c))
                    else:
                        wait_evac(pe, ("u", n))
                    vn = vnew if i else u
                    ps = begin(("o", n, c))
                    for hd in range(4):
                        if i:
                            mm(ps[:, hd * CH:hd * CH + CH], old[:, hd, :], qg[:, hd, rr], True, False)
                        m = mm(ps[:, hd * CH:hd * CH + CH], vn[rr, hd, :], AT[rr, hd, rr], i == 0, True)
                    m.then_inc(s_res, 1)
                    if i < 2 * NQ - 1:
                        four(("dS", n, c), lambda o, hd: mm(o, kdec[rr, hd, :], vn[rr, hd, :], True, True))
                    aside()
            while point[0] < LAST_POINT:
                aside()
            for i in range(8):
                sums(("ho", i), 1, T)
            for j in range(KD):
                dense(("wo", j), SEQ, made_before=8 if j == 0 else None)

            def ffn(i, parts):
                wide = len(parts) == 2
                total(("norm", 2 * i - 1), 2 * i - 1, TT if wide else T)
                b0 = BLOCK[("gate", i, 0)]
                x0 = xlo[0]
                xlo[0] += KD + KF
                with pe.Fori(0, KF // 2) as g:
                    for j in range(4):
                        key, b = (("gate", "up")[j % 2], i, j // 2), b0 + j
                        free, v = evac_at(key)
                        pe.wait_ge(free, g + (v - 1))
                        pe.wait_ge(s_lo, g * 4 + (b + 1))
                        for k in range(KD):
                            if j == 0:
                                pe.wait_ge(s_xlo, x0 + k + 1)
                            w = (w_hi[b % RING][:, k * P:k * P + P], w_lo[b % RING][:, k * P:k * P + P])
                            for o, a0, a1 in parts:
                                m = mm3(slot(key)[:, o:o + a1 - a0], w, (x_hi[:, k, a0:a1], x_lo[:, k, a0:a1]), k == 0, k == KD - 1)
                        m.then_inc(s_used, 1)
                pe.wait_ge(s_xlo, xlo[0])
                b1 = BLOCK[("down", i, 0)]
                with pe.Fori(0, 2) as g:
                    for j in range(4):
                        key = ("down", i, j)
                        free, v = evac_at(key)
                        pe.wait_ge(free, g + (v - 1))
                        for q in range(3):
                            b = b1 + 3 * j + q
                            pe.wait_ge(s_lo, g * 12 + (b + 1))
                            for kk in range(min(8, KF - 8 * q)):
                                k = 8 * q + kk
                                w = (w_hi[b % RING][:, kk * P:kk * P + P], w_lo[b % RING][:, kk * P:kk * P + P])
                                for o, a0, a1 in parts:
                                    m = mm3(slot(key)[:, o:o + a1 - a0], w, (f_hi[:, k, a0:a1], f_lo[:, k, a0:a1]), k == 0, k == KF - 1)
                            m.then_inc(s_used, 1)

            def wide(keys, meta):
                sl = [begin(k) for k in keys]
                b = BLOCK[keys[-1]]
                for i in range(4):
                    pe.wait_ge(s_lo, b + i + 1)
                    w = (w_hi[(b + i) % RING], w_lo[(b + i) % RING])
                    for kk in range(2):
                        k = 2 * i + kk
                        for n in range(NQ + meta):
                            tk = slice(M + n * P, M + n * P + P) if n < NQ else slice(0, M)
                            out = sl[n // 2][:, (n % 2) * 512:(n % 2) * 512 + 512] if n < NQ else sl[2][0:M, 0:512]
                            m = mm3(out, (x_hi[:, k, tk], x_lo[:, k, tk]),
                                    (w[0][:, kk * 512:kk * 512 + 512], w[1][:, kk * 512:kk * 512 + 512]), k == 0, k == KD - 1)
                    m.then_inc(s_used, 1)
            xlo = [16]
            ffn(1, ALL)
            total(("norm", 2), 2, TT)
            dense(("ik",), SEQ, made_before=xlo[0])
            xlo[0] += KD
            ps = begin(("iw",))
            b = BLOCK[("iw",)]
            pe.wait_ge(s_lo, b + 1)
            for n in range(NQ):
                tk = slice(M + n * P, M + n * P + P)
                for k in range(KD):
                    m = mm3(ps[:, n * 8:n * 8 + 8], (x_hi[:, k, tk], x_lo[:, k, tk]),
                            (w_hi[b % RING][:, k * P:k * P + 8], w_lo[b % RING][:, k * P:k * P + 8]), k == 0, k == KD - 1)
            m.then_inc(s_used, 1)
            for j in range(4):
                dense(("iq", j), SEQ)
            wait_evac(pe, ("ik",))
            for n in range(1, NQ):
                for j in range(4):
                    wait_evac(pe, ("iq", j))
                    ps = begin(("is", n, j))
                    for a in range(2):
                        r = slice(64 * a, 64 * a + 64)
                        m = mm(ps[:, a * 512:a * 512 + (n + 1) * P], iq[r, j, n * P:n * P + P], ik[r, 0:(n + 1) * P], True, True)
                    m.then_inc(s_res, 1)
            def unit(key, n, k, _):
                if key[0] != "av":
                    b = BLOCK[key]
                    if k == 0:
                        begin(key)
                        pe.wait_ge(s_lo, b + 1)
                    w = (w_hi[b % RING][:, k * P:k * P + P], w_lo[b % RING][:, k * P:k * P + P])
                    for o, c0, c1 in (ALL if key[0] == "ak" else SEQ):
                        m = mm3(slot(key)[:, o:o + c1 - c0], w, (x_hi[:, k, c0:c1], x_lo[:, k, c0:c1]), k == 0, k == KD - 1)
                    if k == KD - 1:
                        m.then_inc(s_used, 1)
                    return
                if k == 0 and n % NQ == 0:
                    begin(key)
                b = BLOCK[("av", key[1], 1)] + k // 4
                if n == 0:
                    pe.wait_ge(s_lo, b + 1)
                tk = slice(M + n * P, M + n * P + P) if n < NQ else slice(0, M)
                out = slot(key)[:, n * 256:n * 256 + 256] if n < NQ else slot(key)[0:M, 0:256]
                a = slice(k % 4 * 256, k % 4 * 256 + 256)
                m = mm3(out, (x_hi[:, k, tk], x_lo[:, k, tk]), (w_hi[b % RING][:, a], w_lo[b % RING][:, a]), k == 0, k == KD - 1)
                if n == NQ and k % 4 == 3:
                    m.then_inc(s_used, 1)
                elif (n, k) == (NQ - 1, KD - 1):
                    m.then_inc(s_res, 1)
            for u in projection_units(0):
                unit(*u)
            for j in range(4):
                dense(("ga", j), SEQ)
            for s in range(ATT_STEPS + 2):
                if s < ATT_STEPS:
                    pair, j, n = s // PAIR_STEPS, s // NQ % 2, s % NQ
                    if n == 0:
                        wait_evac(pe, ("aq", pair, j))
                        wait_evac(pe, ("ak", pair, j))
                    w = M + (n + 1) * P
                    ps = begin(("AS", s))
                    for a0, a1 in ((0, min(w, 512)), (512, w)):
                        if a1 > a0:
                            m = mm(ps[:, a0:a1], aq[pair % 2][:, j, n * P:n * P + P], ak[pair % 2][:, j, a0:a1], True, True)
                    m.then_inc(s_res, 1)
                for u in FILL.get(2 * s, []):
                    unit(*u)
                if 1 <= s <= ATT_STEPS:
                    e = s - 1
                    n, i = e % NQ, e % 2
                    pe.wait_ge(s_afp, e + 1)
                    ps = begin(("AP", e))
                    nc.tensor.transpose(ps[0:M, 0:P], Ax[i][:, 0:M], K("ident"))
                    for kt in range(n + 1):
                        m = nc.tensor.transpose(ps[:, (kt + 1) * P:(kt + 2) * P], Ax[i][:, M + kt * P:M + kt * P + P], K("ident"))
                    m.then_inc(s_res, 1)
                for u in FILL.get(2 * s + 1, []):
                    unit(*u)
                if s >= 2:
                    e = s - 2
                    pair, j, n, i = e // PAIR_STEPS, e // NQ % 2, e % NQ, e % 2
                    if e % PAIR_STEPS == 0:
                        wait_evac(pe, ("av", pair, 0))
                        wait_evac(pe, ("av", pair, 1))
                    wait_evac(pe, ("AP", e))
                    ps = begin(("AV", e))
                    mm(ps[:, 0:P], avm[pair % 2][0:M, j * P:j * P + P], At[i][0:M, 0:P], True, False)
                    for kt in range(n + 1):
                        m = mm(ps[:, 0:P], av[pair % 2][:, kt, j * P:j * P + P], At[i][:, (kt + 1) * P:(kt + 2) * P], False, kt == n)
                    m.then_inc(s_res, 1)
            wait_evac(pe, ("AV", ATT_STEPS - 1))
            for j in range(KD):
                dense(("ao", j), [(0, 0, T)], ATT_H, (att_hi, att_lo))
            for hd in range(RET_H):
                for j in range(2):
                    dense(("rq", hd, j), SEQ)
                for j in range(2):
                    dense(("rk", hd, j), ALL)
                wide([("rv", hd, i) for i in range(3)], 1)
                dense(("rg", hd, 0), SEQ)
                pe.wait_ge(s_rotd, 2 * hd + 2)
                for kt in range(NQ + 1):
                    ps = begin(("rs", hd, kt))
                    keys = slice(M + kt * P, M + kt * P + P) if kt < NQ else slice(0, M)
                    q0 = kt * P if kt < NQ else 0
                    out = ps[:, 0:T - q0] if kt < NQ else ps[0:M, 0:T]
                    for d in range(2):
                        m = mm(out, rqk[:, 2 + d, keys], rqk[:, d, q0:T], d == 0, d == 1)
                    m.then_inc(s_res, 1)
                dense(("rg", hd, 1), SEQ)
                for i in range(3):
                    wait_evac(pe, ("rv", hd, i))
                pe.wait_ge(s_rst, 5 * hd + 5)
                for d in range(4):
                    ps = begin(("ry", hd, d))
                    mm(ps[:, 0:T], rvm[0:M, d * P:d * P + P], rstm[0:M, :], True, False)
                    for kt in range(NQ):
                        m = mm(ps[:, kt * P:T], rv[:, kt, d * P:d * P + P], rst[:, kt, kt * P:T], False, kt == NQ - 1)
                    m.then_inc(s_res, 1)
                dense(("rg", hd, 2), SEQ)
                sums(("rn", hd), 4, T)
                dense(("rg", hd, 3), SEQ)
                for j in range(KD):
                    key = ("wr", hd, j)
                    ps = begin(key)
                    b = BLOCK[key]
                    pe.wait_ge(s_lo, b + 1)
                    w = (w_hi[b % RING], w_lo[b % RING])
                    for k in range(4):
                        pe.wait_ge(s_xlo, xlo[0] + k + 1)
                        a = (j % 2) * 512 + k * P
                        m = mm3(ps[:, 0:T], (w[0][:, a:a + P], w[1][:, a:a + P]), (y_hi[:, k, :], y_lo[:, k, :]), k == 0, k == 3)
                    m.then_inc(s_used if j % 2 else s_res, 1)
                xlo[0] += 4
            for j in range(KD):
                dense(("gr", j), SEQ)
            for j in range(KD):
                dense(("mx", j), [(0, 0, T)], x=(merged_hi, merged_lo), made_before=xlo[0] if j == 0 else None)
            xlo[0] += KD
            ffn(2, SEQ)
            total(("norm", 4), 4, T)

        @block.gpsimd
        def _(pool):
            with pool.Fori(0, BLOCKS_PADDED // RING) as i:
                for j in range(RING):
                    pool.wait_ge(s_hi, i * RING + (j + 1))
                    nc.gpsimd.tensor_tensor(w_lo[j][:], w_raw[j][:], w_hi[j][:].bitcast(F32),
                                            ALU.subtract).then_inc(s_lo, 1)
            if dump is not None:
                for o in owners:
                    pool.wait_ge(*o.last)
                src = {"h": h, "qkv": qkv, "dqk": dqk, "g": g, "beta": beta, "x_hi": x_hi}[dump]
                pool.dma_start(dump_dram, src[:].bitcast(F32) if dump == "x_hi" else src[:]).then_inc(s_dump, 16)
                pool.wait_ge(s_dump, 16)


def tiles_of(w, cols):
    k, n = w.shape
    return w


def stream(inp):
    z = np.zeros
    w_in, w_out = inp["w_in"][0], inp["w_out"][0]
    blocks = []

    def cols(w):
        k = w.shape[0]
        w = w.reshape(k // P, P, w.shape[1]).transpose(1, 0, 2)
        blocks.append(np.ascontiguousarray(w.reshape(P, -1)))

    def wide(w):
        w = w.reshape(4, 2, P, 512).transpose(0, 2, 1, 3).reshape(4, P, 1024)
        blocks.extend(np.ascontiguousarray(w))
    o = np.cumsum([0, 512, 512, 512, 512, 4, 4, 512, 512, 512, 512])
    for at in (o[0], o[1], o[2]):
        for j in range(4):
            cols(w_in[:, at + j * P:at + j * P + P])
    gates = z((D, P), np.float32)
    gates[:, 0:8] = w_in[:, o[4]:o[6]]
    cols(gates)
    wide(w_in[:, o[8]:o[9]])
    for at in (o[3], o[9], o[6], o[7]):
        for j in range(4):
            cols(w_in[:, at + j * P:at + j * P + P])
    for j in range(8):
        cols(w_out[:, j * P:j * P + P])
    fit = lambda w: np.concatenate([w, z((w.shape[0], P - w.shape[1]), np.float32)], 1)

    def ffn(i):
        gate, up, down = (inp[f"ffn{i}_w_{n}_2"][0] for n in ("gate", "up", "down"))
        for f in range(KF):
            cols(gate[:, f * P:f * P + P])
            cols(up[:, f * P:f * P + P])
        for d in range(KD):
            w = np.concatenate([down[:, d * P:d * P + P], z((24 * P - D_FF, P), np.float32)])
            for q in range(3):
                cols(w[q * 1024:q * 1024 + 1024])
    ffn(1)
    w2 = inp["w_in_2"][0]
    names = ("rq", "rk", "rv", "rg", "aq", "ak", "av", "iq", "ik", "iw", "gr", "ga")
    sizes = (1024, 1024, 2048, 2048, 1024, 1024, 1024, 512, 64, 8, 1024, 1024)
    start = dict(zip(names, np.cumsum([0, *sizes])))
    part = lambda name, c, n: w2[:, start[name] + c:start[name] + c + n]
    cols(np.concatenate([part("ik", 0, 64)] * 2, 1))
    cols(fit(part("iw", 0, 8)))
    for j in range(4):
        cols(part("iq", j * P, P))
    for g in range(ATT_H // 2 + 1):
        if g < ATT_H // 2:
            for j in range(2):
                for name in ("ak", "aq"):
                    cols(part(name, g * 256 + j * P, P))
            w = part("av", g * 256, 256)
            blocks.extend(np.ascontiguousarray(w.reshape(2, 4, P, 256).transpose(0, 2, 1, 3).reshape(2, P, 1024)))
        if g in (0, ATT_H // 2):
            for j in range(4):
                cols(part("ga", (4 if g else 0) * P + j * P, P))
    for j in range(KD):
        cols(inp["w_att_out_2"][0][:, j * P:j * P + P])
    for hd in range(RET_H):
        for name in ("rq", "rk"):
            for j in range(2):
                cols(part(name, hd * 256 + j * P, P))
        wide(part("rv", hd * 512, 512))
        for j in range(4):
            cols(part("rg", hd * 512 + j * P, P))
        w = inp["w_ret_out_2"][0][hd * 512:hd * 512 + 512]
        for j in range(0, KD, 2):
            blocks.append(np.ascontiguousarray(
                w.reshape(4, P, KD, P)[:, :, j:j + 2].transpose(1, 2, 0, 3).reshape(P, 1024)))
    for j in range(KD):
        cols(part("gr", j * P, P))
    for j in range(KD):
        cols(inp["w_mix_out_2"][0][:, j * P:j * P + P])
    ffn(2)
    assert len(blocks) == BLOCKS, (len(blocks), BLOCKS)
    while len(blocks) < BLOCKS_PADDED:
        blocks.append(z((P, 1024), np.float32))
    return np.stack(blocks).reshape(BLOCKS_PADDED // RING, RING, P, 1024)


def small_inputs(inp):
    a = np.zeros((P, N_SMALL), np.float32)

    def put(name, v):
        v = np.asarray(v)
        a[:v.shape[0], SMALL[name][0]:SMALL[name][0] + v.shape[1]] = v
    col = lambda v: v.reshape(-1, P).T
    put("norm_gain", col(inp["norm_gain"][0]))
    put("conv", inp["conv_w"][0].reshape(4, 12, P).transpose(2, 1, 0).reshape(P, 48))
    put("dn_gain", col(inp["dn_out_gain"][0]))
    put("q_gain", np.concatenate([inp["q_gain"][0]] * 2)[:, None])
    put("k_gain", np.concatenate([inp["k_gain"][0]] * 2)[:, None])
    put("df_gain", col(inp["df_out_gain"][0]))
    put("a_log", np.broadcast_to(inp["a_log"][0], (P, 4)))
    put("dt_bias", np.broadcast_to(inp["dt_bias"][0], (P, 4)))
    for n, m in (("lq1", "lambda_q1"), ("lk1", "lambda_k1"), ("lq2", "lambda_q2"), ("lk2", "lambda_k2")):
        put(n, inp[m][0][:, None])
    put("f1_gain", col(inp["ffn1_norm_2"][0]))
    put("mix_gain", col(inp["mix_norm_2"][0]))
    put("f2_gain", col(inp["ffn2_norm_2"][0]))
    put("final_gain", col(inp["final_norm_2"]))
    return a


def kernel(_dump=None, **inputs):
    import concourse.bacc as bacc
    from concourse.bass_utils import run_bass_kernel_spmd as run

    inp = {k: np.asarray(v) for k, v in inputs.items()}
    feature_major = lambda a: np.ascontiguousarray(a.T.reshape(KD, P, -1).transpose(1, 0, 2))
    arrays = {
        "weights": stream(inp),
        "x_t": feature_major(inp["x"][0]),
        "meta_t": feature_major(inp["meta_tokens_2"]),
        "consts": constants(),
        "small_in": small_inputs(inp),
        "rotations": rotations(),
        "decays": retention_decay(),
    }
    nc = bacc.Bacc("TRN2", target_bir_lowering=False, num_devices=1)
    args = [nc.dram_tensor(n, a.shape, F32, kind="ExternalInput").ap() for n, a in arrays.items()]
    out = nc.dram_tensor("out", (P, KD, T), F32, kind="ExternalOutput").ap()
    dd = None
    if _dump:
        dd = nc.dram_tensor("dumped", _dump[1], F32, kind="ExternalOutput").ap()
    build(nc, *args, out, _dump and _dump[0], dd)
    r = run(nc, [arrays], core_ids=[0])
    y = r.results[0]["out"]
    return np.ascontiguousarray(y.transpose(1, 0, 2).reshape(D, T).T)[None]
```

```python
from contextlib import ExitStack

import numpy as np
import concourse.bass as bass
from concourse import mybir

F32 = mybir.dt.float32
F32R = mybir.dt.float32r
ALU = mybir.AluOpType
ACT = mybir.ActivationFunctionType
AX = mybir.AxisListType

P = 128
D = 1024
KD = D // P
T = 512
M = 16
TT = M + T
HALF = TT // 2
TQ = slice(M, TT)
NQ = T // P
EPS = 1e-6
LN_EXP = "natural_log_exp_and_others"
NEG = -1.0e30
DN_WORK = "decay qg attn n inv_t inv join join_b y kdec kbg u".split()

DN_H = 4
LAMBDA_INIT = 0.8 - 0.6 * 1.0
DF_H = 4
DF_STEPS = DF_H * NQ
CH = 64
D_FF = 2816
KF = D_FF // P
RET_H = 4
RET_DK = 256
ROPE_THETA = 10000.0
ATT_SCALE = 128 ** -0.5
IDX_SCALE = (64 ** -0.5) * (8 ** -0.5)
TAKEN = -3.0e38
ATT_H = 8
K_TOP = 128
SLOTS = 4
RING = 4



def results():
    r = []
    add = lambda key, blocks=0: r.append((key, blocks))
    add(("norm", 0))
    for j in range(12):
        add(("qkv", j), 1)
        for i in norms_after(j):
            add(("hn", i))
    add(("ab",), 1)
    add(("ab_t",))
    for i in norms_after(12):
        add(("hn", i))
    add(("dv", 0))
    add(("dv", 1), 4)
    add(("lam",))
    point = 0

    def aside():
        nonlocal point
        for key in aside_results(point):
            add(key, 1 if key in ASIDE_DENSE else 0)
        point += 1
    for n in range(NQ):
        for k in ("gcb", "beb", "sm"):
            add((k, n))
        aside()
        for k in ("N0", "A0"):
            add((k, n))
        aside()
        for k in ("T1", "kt", "vt"):
            add((k, n))
        aside()
        for l in range(5):
            add(("Y", n, l))
            aside()
            if l < 4:
                add(("dT", n, l))
            add(("dU", n, l))
            aside()
        for k in ("u", "wT"):
            add((k, n))
        aside()
        for c in range(2):
            if (n, c) != (0, 0):
                add(("wS", n, c))
            aside()
            add(("o", n, c))
            if (n, c) != (NQ - 1, 1):
                add(("dS", n, c))
            aside()
    assert point == POINTS * NQ
    while point < LAST_POINT:
        aside()
    for i in HEADS_OUT:
        if i not in HO_POINT:
            add(("ho", i))
    for j in range(KD):
        add(("wo", j), 1)
    ffn_results(add, 1)
    add(("norm", 2))
    add(("ik",), 1)
    add(("iw",), 1)
    add(("iw_t",))
    for j in range(4):
        add(("iq", j), 1)
    for s in range(IX_STEPS):
        add(("is", 1 + s // 4, s % 4))
        if s in IX_BESIDE:
            add(*projection_keys(0)[IX_BESIDE.index(s)])
    for key, blocks in projection_keys(0)[len(IX_BESIDE):]:
        add(key, blocks)
    for j in range(4):
        add(("ga", j), 1)
    for s in range(ATT_STEPS + 2):
        if s < ATT_STEPS:
            add(("AS", s))
        for key, blocks in filled(2 * s):
            add(key, blocks)
        if 1 <= s <= ATT_STEPS:
            add(("AP", s - 1))
        for key, blocks in filled(2 * s + 1):
            add(key, blocks)
        if s >= 2:
            add(("AV", s - 2))
    for j in range(KD):
        add(("ao", j), 1)
    for hd in range(RET_H):
        for j in range(1 if hd else 0, 2):
            add(("rq", hd, j), 1)
        for j in range(2):
            add(("rk", hd, j), 1)
        add(("rv", hd, 0))
        add(("rv", hd, 1))
        add(("rv", hd, 2), 4)
        add(("rg", hd, 0), 1)
        for kt in range(NQ + 1):
            add(("rs", hd, kt))
        add(("rg", hd, 1), 1)
        for d in range(4):
            add(("ry", hd, d))
        add(("rg", hd, 2), 1)
        add(("rn", hd))
        add(("rg", hd, 3), 1)
        if hd + 1 < RET_H:
            add(("rq", hd + 1, 0), 1)
        for j in range(KD):
            add(("wr", hd, j), j % 2)
    for j in range(KD):
        add(("gr", j), 1)
    for j in range(KD):
        add(("mx", j), 1)
    ffn_results(add, 2)
    add(("norm", 4))
    return r


def ffn_results(add, i):
    add(("norm", 2 * i - 1))
    for f in range(KF):
        add(("gate", i, f), 1)
        add(("up", i, f), 1)
    for d in range(KD):
        add(("down", i, d), 3)


def norms_after(j):
    return (2 * (j - 9), 2 * (j - 9) + 1) if j >= 9 else ()


POINTS = 18
ASIDE_DENSE = [("dqk", j) for j in range(8)] + [("dz", j) for j in range(4)] + [("z", j) for j in range(4)]
DF_START = 2 * POINTS
SHARE = [3, 3, 2] + [1] * 15
EARLY = 84
LATE_POINTS = 30
LAST_POINT = DF_START + 2 * (DF_STEPS - 1) + 8


def dense_points():
    points, products = [], 8 * len(ASIDE_DENSE)
    early = [SHARE[p % POINTS] for p in range(DF_START)]
    late = [SHARE[p % POINTS] for p in range(LATE_POINTS)]
    for t in range(products):
        share, first, part = (early, 0, t / EARLY) if t < EARLY else (late, DF_START, (t - EARLY) / (products - EARLY))
        p = first + next(i for i in range(len(share)) if sum(share[:i + 1]) > part * sum(share))
        if points and t % 8 == 0:
            p = max(p, points[-1] + 1)
        points.append(max([p] + points[-1:]))
    return points


def dense_done(f):
    return DENSE_POINTS[8 * f + 7]


DENSE_POINTS = dense_points()
assert dense_done(12) >= DF_START and dense_done(7) + 5 < DF_START


HO_POINT = {4 + j: DF_START + 8 * j + 14 for j in range(3)}
GATE_POINT = DF_START + 33
HEADS_OUT = [4, 5, 6, 0, 1, 2, 3, 7]


def norm_at(p, stage):
    return [i for i in range(8) if dense_done(ASIDE_DENSE.index(("dqk", i))) + 2 + stage == p]


def df_at(p, late):
    s, odd = divmod(p - DF_START, 2)
    s -= late
    return s if 0 <= s < DF_STEPS else None


def aside_results(p):
    keys = [key for f, key in enumerate(ASIDE_DENSE) if dense_done(f) == p]
    keys += [("hn", 8 + i) for i in norm_at(p, 1)]
    keys += [("ho", i) for i, first in HO_POINT.items() if first + 1 == p]
    if p >= DF_START and (p - DF_START) % 2 == 0:
        for name, late in (("S", 0), ("PT", 2), ("PV", 3)):
            s = df_at(p, late)
            if s is not None:
                keys.append((name, s // NQ, s % NQ))
    return keys


IX_BESIDE = [0, 2]
IX_STEPS = (NQ - 1) * 4
ATT_STEPS = ATT_H * NQ
PAIR_STEPS = 2 * NQ


def projection_keys(g):
    if g == ATT_H // 2:
        return [(("ga", 4 + j), 1) for j in range(4)]
    return [((name, g, j), 1) for j in range(2) for name in ("ak", "aq")] + [(("av", g, 0), 0), (("av", g, 1), 2)]


def projection_units(g):
    units = []
    for key, _ in projection_keys(g):
        if key[0] == "av":
            units += [(key, n, k, 1) for n in (range(NQ) if key[2] == 0 else [NQ]) for k in range(KD)]
        else:
            units += [(key, None, k, 2) for k in range(KD)]
    return units


def fill_places():
    units, complete = {}, {}
    for g in range(ATT_H // 2):
        todo = projection_units(g + 1)
        cost, places, before = sum(u[3] for u in todo), 2 * PAIR_STEPS, 0
        for u in todo:
            at = 2 * PAIR_STEPS * g + before * places // cost
            units.setdefault(at, []).append(u)
            before += u[3]
            if u is todo[-1] or todo[todo.index(u) + 1][0] != u[0]:
                complete.setdefault(at, []).append(u[0])
    return units, complete


FILL, FILLED = fill_places()


def filled(at):
    return [(key, dict(projection_keys(key[1] if key[0] != "ga" else ATT_H // 2))[key]) for key in FILLED.get(at, [])]


RESULTS = results()
ROTATED = [k for k, _ in RESULTS if k[0] in ("ik", "iq", "aq", "ak")]
PLACE = {}
FREE = {}
_bank, _count, _main, _delta, _first = {}, {}, 1, 0, 0
for _key, _ in RESULTS:
    if _key[0] in ("gcb", "beb", "sm", "N0", "A0", "T1", "Y", "dT", "dU", "kt", "vt", "u", "wT", "wS", "o", "dS") or \
            _key[0] == "hn" and _key[1] < 8 or _key[0] == "ho" and _key[1] in HO_POINT:
        _p = (5 + _delta % 3, 1)
        _delta += 1
    elif _key in ASIDE_DENSE:
        _p = (4 if _key[0] in ("dz", "z") else 2 * (ASIDE_DENSE.index(_key) % 2), 1)
    elif _key[0] == "hn":
        _p = (3 - 2 * (_key[1] % 2), 1)
    elif _key[0] in ("qkv", "ab", "ab_t"):
        _p = (_first % 4, 1)
        _first += 1
    elif _key[0] in ("S", "dv"):
        _p = (2 * _key[1] if _key[0] == "dv" else 0, 2)
    elif _key[0] in ("aq", "ak", "av", "AS", "AP", "AV") or _key[0] == "ga" and _key[1] >= 4:
        _p = {"aq": (2, 1), "ak": (0, 2), "AV": (3, 1), "AS": (4, 2), "AP": (6, 2),
              "av": ((0, 2), (2, 1))[_key[-1] % 2], "ga": ((0, 2), (2, 1))[_key[-1] % 2]}[_key[0]]
    elif _key[0] == "is":
        _p = (4 + 2 * (_key[2] % 2), 2)
    elif _key[0] in ("PT", "PV"):
        _p = (2 + (_key[0] == "PV"), 1)
    else:
        _p = (2 * (_main % SLOTS), 2)
        _main += 1
    _count[_p] = _count.get(_p, 0) + 1
    PLACE[_key] = (*_p, _count[_p])
    FREE[_key] = sorted({_bank[b] for b in range(_p[0], _p[0] + _p[1]) if b in _bank}, key=str)
    for b in range(_p[0], _p[0] + _p[1]):
        _bank[b] = _key
BLOCK = {}
READY = {}
_b = _g = 0
for _key, _n in RESULTS:
    BLOCK[_key] = _b
    _b += _n
    if _n:
        READY[_key] = ("used", _b)
    elif _key[0] in ("dv", "rv"):
        READY[_key] = ("used", _b + 4)
    else:
        _g += 1
        READY[_key] = ("result", _g)
BLOCKS = _b
BLOCKS_PADDED = -(-BLOCKS // RING) * RING

CONST = {}


def constants():
    i = np.arange(P)
    s, c = i[:, None], i[None, :]
    same = (s // CH) == (c // CH)
    parts = {
        "ident": s == c,
        "ones": s == s + 0 * c,
        "ones64": (s // 64) == (c // 64),
        "tri": same & (s <= c),
        "suffix": same & (s > c),
        "chunk0": (s < CH) & (c == c),
        "chunk1": (s >= CH) & (c == c),
    }
    for l in range(6):
        w = 2 ** l
        parts[f"join{l}"] = (s // (2 * w) == c // (2 * w)) & (s % (2 * w) < w) & (c % (2 * w) >= w)
    causal = np.zeros((P, T), np.float32)
    causal[:, T - P:] = np.where(c > s, np.float32(NEG), np.float32(0))
    parts = {"ident": parts.pop("ident"), "ones": parts.pop("ones"), "causal": causal, **parts}
    out, at = [], 0
    for name, m in parts.items():
        CONST[name] = (at, at + m.shape[1])
        at += m.shape[1]
        out.append(np.broadcast_to(m, (P, m.shape[1])).astype(np.float32))
    return np.ascontiguousarray(np.concatenate(out, 1))


N_CONST = constants().shape[1]
CAUSAL = CONST["causal"][0]
N_KEPT = CONST["causal"][1]


def rotations():
    pos = np.arange(TT, dtype=np.float32)

    def table(d, copies, signed):
        inv = np.float32(ROPE_THETA) ** (-np.arange(0, d, 2, dtype=np.float32) / np.float32(d))
        angle = (pos[:, None] * inv[None, :].astype(np.float32)).astype(np.float32).T
        cos, sin = np.cos(angle), np.sin(angle)
        cos = np.concatenate([cos] * copies)
        sin = np.concatenate([sin * (-1 if signed and k % 2 == 0 else 1) for k in range(copies)])
        return [cos, sin]
    t = table(128, 2, True) + table(64, 4, True) + table(256, 1, False)
    return np.ascontiguousarray(np.stack(t).transpose(1, 0, 2).astype(np.float32))


def retention_decay():
    out = np.zeros((P, RET_H, TT), np.float64)
    k, q = np.arange(P)[:, None], np.arange(TT)[None, :]
    for hd in range(RET_H):
        log_g = float(np.log1p(-np.float32(2.0 ** (-5.0 - hd))))
        out[:, hd] = np.where(q >= k, np.exp(log_g * np.maximum(q - k, 0)), 0.0)
    return (out * RET_DK ** -0.5).astype(np.float32)

SMALL = {}
_at = 0
for _name, _w in (("norm_gain", 8), ("conv", 48), ("dn_gain", 1), ("q_gain", 1), ("k_gain", 1), ("df_gain", 1),
                  ("a_log", 4), ("dt_bias", 4), ("lq1", 1), ("lk1", 1), ("lq2", 1), ("lk2", 1),
                  ("f1_gain", 8), ("mix_gain", 8), ("f2_gain", 8), ("final_gain", 8)):
    SMALL[_name] = (_at, _at + _w)
    _at += _w
N_SMALL = _at


class Own:

    def __init__(self, engine, sem):
        self.engine, self.sem, self.count, self.last = engine, sem, 0, None

    def own(self, ins):
        self.count += 1
        ins.then_inc(self.sem, 1)
        self.last = (self.sem, self.count)

    def sig(self, ins, sem, value):
        ins.then_inc(sem, 1)
        self.last = (sem, value)

    def sync(self):
        self.engine.wait_ge(*self.last)


def build(nc, w_dram, x_dram, meta_dram, const_dram, small_dram, rot_dram, dec_dram, out_dram):
    with ExitStack() as ctx:
        def sb(name, shape, dt=F32, scope=ctx):
            return scope.enter_context(nc.sbuf_tensor(name, shape, dt))

        def sem(name):
            return ctx.enter_context(nc.semaphore(name))

        w_raw = [sb(f"w_raw{i}", [P, 1024]) for i in range(RING)]
        w_hi = [sb(f"w_hi{i}", [P, 1024], F32R) for i in range(RING)]
        w_lo = [sb(f"w_lo{i}", [P, 1024], F32R) for i in range(RING)]
        h = sb("h", [P, KD, TT])
        const = sb("const", [P, N_KEPT])
        small = sb("small", [P, N_SMALL])
        eps = sb("eps", [P, 1])
        square = [sb(f"square{i}", [P, TT]) for i in range(2)]
        rs = [sb(f"rs{i}", [P, TT]) for i in range(2)]
        xt = [sb(f"xt{i}", [P, TT]) for i in range(2)]
        psum = [ctx.enter_context(nc.psum_tensor(f"slot{i}", [P, 1024], F32)) for i in range(SLOTS)]

        x_hi = sb("x_hi", [P, KD, TT], F32R)
        x_lo = sb("x_lo", [P, KD, TT], F32R)

        with ExitStack() as scope:
            fb = lambda name, shape, dt=F32, scope=scope: sb(name, shape, dt, scope)
            qkv = fb("qkv", [P, 12, T])
            dsz = fb("dsz", [P, 4, T])
            dqk = fb("dqk", [P, 8, T])
            dv = fb("dv", [P, NQ, T])
            with ExitStack() as after:
                mixed_hi = fb("mixed_hi", [P, KD, T], F32R, after)
                mixed_lo = fb("mixed_lo", [P, KD, T], F32R, after)
            state = fb("state", [P, 4, P])
            work = [fb(f"dn_{name}", [P, 4, P]) for name in DN_WORK[:-2]]
            work += [x[:, 0:T].rearrange("p (h c) -> p h c", h=4) for x in xt]
            Sx = [[fb(f"score{i}{c}", [P, T]) for c in range(2)] for i in range(2)]
            Pm = [Sx[i][0] for i in range(2)]
            PTs = fb("prob_t", [P, T])
            sz = qkv[:, 4:12, 0:2 * P].rearrange("p (a j) t -> p a j t", a=2)
            mx = [fb(f"mx{i}", [P, 2]) for i in range(2)]
            sums_ = [fb(f"sum{i}", [P, 2]) for i in range(2)]
            ab = fb("ab", [P, NQ, 8])
            tA = fb("tA", [P, NQ, 4])
            tB = fb("tB", [P, NQ, 4])
            beta = fb("beta", [P, NQ, 4])
            g = fb("g", [P, NQ, 4])
            nea = fb("nea", [P, 4])
            sm = fb("sm", [P, 16])
            esm = fb("esm", [P, 16])
            cb = fb("cb", [P, 4])
            lamt = fb("lamt", [P, 8])
            const1 = fb("const1", [P, N_CONST - N_KEPT])

        with ExitStack() as scope:
            f_hi = sb("f_hi", [P, KF, TT], F32R, scope)
            f_lo = sb("f_lo", [P, KF, TT], F32R, scope)

        with ExitStack() as mix:
            mb = lambda name, shape, dt=F32, scope=mix: sb(name, shape, dt, scope)
            with ExitStack() as scope:
                aq = [mb(f"aq{i}", [P, 2, T], F32, scope) for i in range(1)]
                av = [mb(f"av{i}", [P, NQ, 2 * P], F32, scope) for i in range(1)]
            ya_late = mb("ya_late", [P, 4, T])
            ya_early = mb("ya_early", [P, 4, T])
            ya = [(ya_early if j < 4 else ya_late)[:, j % 4, :] for j in range(KD)]
            with ExitStack() as att:
                aq += [mb("aq1", [P, 2, T], F32, att)]
                av += [mb("av1", [P, NQ, 2 * P], F32, att)]
                ak = [mb(f"ak{i}", [P, 2, TT], F32, att) for i in range(2)]
                avm = [mb(f"av_meta{i}", [P, 2 * P], F32, att) for i in range(2)]
                bias = mb("bias", [P, NQ, TT], F32, att)
                at_rot = mb("at_rot", [P, 2, TT], F32, att)
                with ExitStack() as scope:
                    ix_rot = mb("ix_rot", [P, 2, TT], F32, scope)
                    iq = mb("iq", [P, 4, T], F32, scope)
                    ik = mb("ik", [P, T], F32, scope)
                    relu = [mb(f"relu{i}", [P, 2, T], F32, scope) for i in range(2)]
                    iw = mb("iw", [P, NQ, 8], F32, scope)
                with ExitStack() as scope:
                    att_hi = mb("att_hi", [P, ATT_H, T], F32R, scope)
                    att_lo = mb("att_lo", [P, ATT_H, T], F32R, scope)
                    Ax = [mb(f"att_score{i}", [P, TT], F32, scope) for i in range(2)]
                    At = [mb(f"att_prob_t{i}", [P, 5 * P], F32, scope) for i in range(2)]
                    amx = [mb(f"att_mx{i}", [P, 1], F32, scope) for i in range(2)]
                    asum = [mb(f"att_sum{i}", [P, 1], F32, scope) for i in range(2)]
                    score = [mb(f"ix_score{i}", [P, T], F32, scope) for i in range(3)]
                    top8 = mb("top8", [P, 3, 8], F32, scope)
            yr = mb("yr", [P, KD, T])
            with ExitStack() as scope:
                merged_hi = mb("merged_hi", [P, KD, T], F32R, scope)
                merged_lo = mb("merged_lo", [P, KD, T], F32R, scope)
            rqk = mb("rqk", [P, 4, TT])
            rv = mb("rv", [P, NQ, T])
            rvm = mb("rv_last", [P, T])
            rg = mb("rg", [P, 4, T])
            rst = mb("ret_score_t", [P, NQ, T])
            rstm = mb("ret_score_last", [P, M])
            y_hi = mb("y_hi", [P, 4, T], F32R)
            y_lo = mb("y_lo", [P, 4, T], F32R)
            rt_rot = mb("rt_rot", [P, 2, TT])
            dec = mb("dec", [P, TT])

        s_small = sem("small_loaded")
        s_const = sem("const_loaded")
        s_gain = sem("gains_loaded")
        s_x = [sem(f"x_loaded{i}") for i in range(4)]
        s_raw = [sem(f"w_raw_loaded{i}") for i in range(RING)]
        s_hi = sem("w_hi_made")
        s_lo = sem("w_lo_made")
        s_used = sem("w_block_used")
        s_res = sem("result_ready")
        s_evac = {p: sem(f"evac_bank{p[0]}_{p[1]}") for p in sorted({(a, b) for a, b, _ in PLACE.values()})}
        s_eps = sem("eps_set")
        s_sq = sem("square_made")
        s_sqd = sem("square_used")
        s_acc = sem("squares_added")
        s_fsilu = sem("ffn_silu_made")
        s_rs = sem("rs_made")
        s_rsd = sem("rs_used")
        s_xt = sem("xt_made")
        s_xhi = sem("x_hi_made")
        s_xlo = sem("x_lo_made")
        s_v = sem("vector_order")
        s_a = sem("scalar_order")
        s_silu = sem("silu_made")
        s_g = sem("g_beta")
        s_dn = sem("delta_vector")
        s_da = sem("delta_scalar")
        s_df = sem("diff_vector")
        s_dfp = sem("diff_prob")
        s_dfa = sem("diff_scalar")
        s_rot = sem("rotated_copy")
        s_ixt = sem("indexer_tables")
        s_relud = sem("relu_used")
        s_af = sem("att_vector")
        s_afp = sem("att_prob")
        s_afa = sem("att_scalar")
        s_athi = sem("att_hi_made")
        s_gate = sem("gate_used")
        s_sigm = sem("att_gate_made")
        s_dec = sem("decay_loaded")
        s_rst = sem("ret_score_decayed")
        s_y = sem("y_made")
        s_rotd = sem("ret_rotated")
        s_rtt = sem("ret_rotation_loaded")
        s_out = sem("out_stored")

        def halves(ap):
            return ap.rearrange("p (a c) -> p a c", a=2)

        def ps_all(key):
            return halves(slot(key)[:])[:, :, 0:HALF]

        def evac_in(key, g):
            s_, v = evac_at(key)
            return s_, v + g

        def K(name):
            a, b = CONST[name]
            return const[:, a:b] if b <= N_KEPT else const1[:, a - N_KEPT:b - N_KEPT]

        def sml(name, j=0, w=1):
            a = SMALL[name][0] + j
            return small[:, a:a + w]

        def wait_result(eng, key):
            kind, value = READY[key]
            eng.wait_ge(s_used if kind == "used" else s_res, value)

        def evac_at(key):
            bank, n, count = PLACE[key]
            return s_evac[bank, n], count

        def wait_evac(eng, key):
            eng.wait_ge(*evac_at(key))

        def slot(key):
            bank, n, _ = PLACE[key]
            return psum[bank // 2][:, bank % 2 * 512:(bank % 2 + n) * 512]

        DT, qg, AT, N, U, Tm, Ns_a, Ns_b, Y, kdec, kbg, u = work
        EG, kb, Ns, Sd, wT, vnew, vb, gB, bB = qg, Ns_a, (Ns_a, Ns_b), kbg, Tm, u, DT, Y, Ns_a

        def heads(ap):
            return ap.rearrange("p (h c) -> p h c", h=4)

        DNV = ["gB", "dt", "qg", "U", "Ns0", "Ns1", "Ns2", "Ns3", "Ns4"]
        dnv = lambda name, n: n * len(DNV) + DNV.index(name) + 1

        block = ctx.enter_context(nc.Block())

        @block.sync
        def _(sp):
            sp.wait_ge(s_x[1], 16)
            for j in range(RING):
                sp.dma_start(w_raw[j][:], w_dram[0, j]).then_inc(s_raw[j], 16)
            with sp.Fori(1, BLOCKS_PADDED // RING) as i:
                for j in range(RING):
                    sp.wait_ge(s_lo, i * RING + (j + 1 - RING))
                    sp.dma_start(w_raw[j][:], w_dram[i, j]).then_inc(s_raw[j], 16)

        @block.scalar
        def _(act):
            A = Own(act, s_a)
            made = {"w": 0, "sq": 0, "rs": 0, "x": 0, "table": None}

            def w_split(upto):
                while made["w"] < min(upto + 1, BLOCKS_PADDED):
                    b = made["w"]
                    act.wait_ge(s_raw[b % RING], 16 * (b // RING + 1))
                    if b >= RING:
                        act.wait_ge(s_used, b - RING + 1)
                    nc.scalar.activation(w_hi[b % RING][:], w_raw[b % RING][:], ACT.Copy).then_inc(s_hi, 1)
                    made["w"] += 1

            def ahead(key, blocks=1):
                w_split(BLOCK[key] + blocks - 1 + RING - 1)

            def squares(srcs):
                for src in srcs:
                    q = made["sq"]
                    if q >= 2:
                        act.wait_ge(s_sqd, q - 1)
                    w = src.shape[-1]
                    nc.scalar.activation(square[q % 2][:, 0:w], src, ACT.Square).then_inc(s_sq, 1)
                    made["sq"] += 1

            def rsqrt(key, scale, w):
                r = made["rs"]
                if r >= 2:
                    act.wait_ge(s_rsd, r - 1)
                wait_result(act, key)
                if w == T:
                    src, dst = slot(key)[:, 0:T], rs[r % 2][:, 0:T]
                else:
                    src = slot(key)[:].rearrange("p (a c) -> p a c", a=2)[:, :, 0:HALF]
                    dst = rs[r % 2][:].rearrange("p (a c) -> p a c", a=2)
                if made["table"] != LN_EXP:
                    nc.scalar.preload_act_table_set(LN_EXP)
                    made["table"] = LN_EXP
                A.sig(nc.scalar.activation(dst, src, ACT.Ln, bias=eps[:, 0:1], scale=scale), *evac_at(key))
                A.sync()
                A.sig(nc.scalar.activation(dst, dst, ACT.Exp, scale=-0.5), s_rs, r + 1)
                made["rs"] += 1

            def x_high(n, k0=0, c0=0, dst=x_hi):
                for k in range(k0, k0 + n):
                    m = made["x"]
                    act.wait_ge(s_xt, m + 1)
                    o = dst[:, k, c0:TT] if dst is x_hi else dst[:, k, :]
                    A.sig(nc.scalar.activation(o, xt[m % 2][:, c0:TT], ACT.Copy), s_xhi, m + 1)
                    made["x"] += 1

            def copy_out(key, dst, func=ACT.Copy, w=T):
                wait_result(act, key)
                src = slot(key)[:, 0:w] if w != TT else ps_all(key)
                A.sig(nc.scalar.activation(halves(dst) if w == TT else dst, src, func), *evac_at(key))

            def ffn(i, c0):
                width = TT if c0 == 0 else T
                rsqrt(("norm", 2 * i - 1), 1.0 / D, width)
                b0, m0 = BLOCK[("gate", i, 0)], made["x"]
                w_split(b0 + RING - 2)
                act.wait_ge(s_sqd, made["sq"])

                def w_next(b, g, per):
                    b += RING - 1
                    act.wait_ge(s_raw[b % RING], g * (16 * per // RING) + 16 * (b // RING + 1))
                    act.wait_ge(s_used, g * per + (b - RING + 1))
                    nc.scalar.activation(w_hi[b % RING][:], w_raw[b % RING][:], ACT.Copy).then_inc(s_hi, 1)
                made["table"] = None
                with act.Fori(0, KF // 2) as g:
                    for j in range(2):
                        gk = ("gate", i, j)
                        w_next(b0 + 2 * j, g, 4)
                        s_, v = evac_in(gk, g)
                        act.wait_ge(s_, v)
                        nc.scalar.activation(square[j][:, 0:width], square[j][:, 0:width], ACT.Silu).then_inc(s_fsilu, 1)
                        w_next(b0 + 2 * j + 1, g, 4)
                        act.wait_ge(s_xt, g * 2 + (m0 + j + 1))
                        nc.scalar.activation(f_hi[:, g * 2 + j, c0:TT], xt[j][:, c0:TT], ACT.Copy).then_inc(s_xhi, 1)
                made["x"] += KF
                made["w"] += 2 * KF
                b1 = BLOCK[("down", i, 0)]
                assert made["w"] == b1 + RING - 1
                if i == 1:
                    with act.Fori(0, 2) as g:
                        for j in range(12):
                            w_next(b1 + j, g, 12)
                    made["w"] += 24
                else:
                    w_split(BLOCKS_PADDED - 1)
                act.wait_ge(s_xhi, made["x"])
                wait_evac(act, ("down", i, 7))
                wait_evac(act, ("down", i, 6))

            for i in range(4):
                act.dma_start(h[:, 2 * i:2 * i + 2, TQ], x_dram[:, 2 * i:2 * i + 2]).then_inc(s_x[i], 16)
                if i == 0:
                    act.dma_start(const[:, 0:CAUSAL], const_dram[:, 0:CAUSAL]).then_inc(s_const, 16)
                    act.dma_start(small[:], small_dram).then_inc(s_gain, 16)
            act.dma_start(const[:, CAUSAL:N_KEPT], const_dram[:, CAUSAL:N_KEPT]).then_inc(s_small, 16)
            act.dma_start(const1[:], const_dram[:, N_KEPT:N_CONST]).then_inc(s_small, 16)
            act.dma_start(h[:, :, 0:M], meta_dram).then_inc(s_small, 16)
            for i in range(4):
                act.wait_ge(s_x[i], 16)
                squares([h[:, k, TQ] for k in (2 * i, 2 * i + 1)])
            w_split(1)
            act.wait_ge(s_eps, 1)
            rsqrt(("norm", 0), 1.0 / D, T)
            x_high(2, c0=M)
            w_split(RING - 2)
            x_high(KD - 2, 2, M)
            made["table"] = None
            srcs = [qkv[:, j, :] for j in range(8)]
            for j in range(8):
                key = ("qkv", j)
                ahead(key)
                wait_evac(act, key)
                A.sig(nc.scalar.activation(qkv[:, j, :], qkv[:, j, :], ACT.Silu), s_silu, j + 1)
            ahead(("qkv", 8))
            A.sync()
            squares(srcs[0:2])
            for j in range(9, 13):
                ahead(("qkv", j) if j < 12 else ("ab",))
                for i in norms_after(j):
                    rsqrt(("hn", i), 1.0, T)
                    squares(srcs[i + 2:i + 3])
            w_split(BLOCK[("dv", 1)] + RING - 2)
            act.wait_ge(s_g, 1)
            A.own(nc.scalar.activation(tA[:], tA[:], ACT.Exp, scale=-1.0))
            A.own(nc.scalar.activation(beta[:], ab[:, :, 0:4], ACT.Exp, scale=-1.0))
            A.sync()
            A.own(nc.scalar.activation(tA[:], tA[:], ACT.Ln, bias=1.0))
            A.sig(nc.scalar.activation(nea[:], sml("a_log", 0, 4), ACT.Exp), s_da, 1)
            made["table"] = None
            for j in range(8, 12):
                A.own(nc.scalar.activation(qkv[:, j, :], qkv[:, j, :], ACT.Silu))
                w_split(BLOCK[("dv", 1)] + RING - 2 + j - 7)
            for i in range(2):
                wait_result(act, ("dv", i))
                A.sig(nc.scalar.activation(dv[:, 2 * i:2 * i + 2, :].rearrange("p a c -> p (a c)"), slot(("dv", i))[:, :], ACT.Copy), *evac_at(("dv", i)))
            w_split(BLOCK[("dv", 1)] + 3 + RING - 1)
            act.wait_ge(s_df, 1)
            wait_result(act, ("lam",))
            A.sig(nc.scalar.activation(lamt[:, 2:4], slot(("lam",))[:, 0:2], ACT.Exp), *evac_at(("lam",)))
            da = [1]

            def dsig(ins):
                da[0] += 1
                A.sig(ins, s_da, da[0])
            point = [0]

            def aside():
                p = point[0]
                point[0] += 1
                for f, key in enumerate(ASIDE_DENSE):
                    if dense_done(f) + 1 == p:
                        wait_result(act, key)
                        name, j = key
                        src, dst = slot(key)[:, 0:T], (dsz if name == "dz" else dqk)[:, j % 8, :]
                        if name == "z":
                            src, dst = src.rearrange("p (a t) -> p a t", a=2), sz[:, :, j, :]
                        A.sig(nc.scalar.activation(dst, src, ACT.Copy), *evac_at(key))
                        w_split(BLOCK[key] + RING)
                for i in norm_at(p, 0):
                    A.sync()
                    squares([dqk[:, i, :]])
                for i in norm_at(p, 2):
                    rsqrt(("hn", 8 + i), 1.0 / 64, T)
                for i, first in HO_POINT.items():
                    if p == first:
                        wait_evac(act, ("PV", i - 4, NQ - 1))
                        squares([dqk[:, i - 4, :]])
                    elif p == first + 2:
                        rsqrt(("ho", i), 1.0 / P, T)
                if p == GATE_POINT:
                    A.sync()
                    made["table"] = None
                    for j in range(4):
                        A.own(nc.scalar.activation(dsz[:, j, :], dsz[:, j, :], ACT.Silu))
                        A.own(nc.scalar.activation(sz[:, :, j, :], sz[:, :, j, :], ACT.Silu))
                    A.sync()
                    act.sem_inc(s_silu, 1)
                if p < DF_START or (p - DF_START) % 2 == 0:
                    return
                s = df_at(p, 0)
                if s is not None:
                    n, i = s % NQ, s % 2
                    w = (n + 1) * P
                    act.wait_ge(s_df, 2 + s)
                    for c in range(2):
                        A.sig(nc.scalar.activation(Sx[i][c][:, 0:w], Sx[i][c][:, 0:w], ACT.Exp, bias=mx[i][:, c:c + 1],
                                                   accum_out=sums_[i][:, c:c + 1]), s_dfa, 2 * s + c + 1)
                e = df_at(p, 2)
                if e is not None:
                    w = (e % NQ + 1) * P
                    key = ("PT", e // NQ, e % NQ)
                    if e:
                        wait_result(act, ("PV", (e - 1) // NQ, (e - 1) % NQ))
                    wait_result(act, key)
                    A.sig(nc.scalar.activation(PTs[:, 0:w], slot(key)[:, 0:w], ACT.Copy), *evac_at(key))
            for n in range(NQ):
                act.wait_ge(s_dn, dnv("dt", n))
                dsig(nc.scalar.activation(DT[:], DT[:], ACT.Exp))
                A.sig(nc.scalar.activation(EG[:].rearrange("p h c -> p (h c)"), slot(("gcb", n))[:, 0:T], ACT.Exp), *evac_at(("gcb", n)))
                wait_evac(act, ("sm", n))
                dsig(nc.scalar.activation(esm[:], sm[:], ACT.Exp))
                for _ in range(3):
                    aside()
                for l in range(5):
                    wait_result(act, ("Y", n, l))
                    A.sig(nc.scalar.activation(Y[:].rearrange("p h c -> p (h c)"), slot(("Y", n, l))[:, 0:T], ACT.Copy), *evac_at(("Y", n, l)))
                    aside()
                    aside()
                wait_result(act, ("u", n))
                A.sig(nc.scalar.activation(u[:].rearrange("p h c -> p (h c)"), slot(("u", n))[:, 0:T], ACT.Copy), *evac_at(("u", n)))
                aside()
                for c in range(2):
                    aside()
                    wait_result(act, ("o", n, c))
                    A.sig(nc.scalar.activation(qkv[:, 0:4, n * P + c * CH:n * P + c * CH + CH],
                                         slot(("o", n, c))[:, 0:4 * CH].rearrange("p (h c) -> p h c", h=4), ACT.Copy), *evac_at(("o", n, c)))
                    aside()
            while point[0] < LAST_POINT:
                aside()
            A.sync()
            late = [i for i in HEADS_OUT if i not in HO_POINT]
            head = lambda i: qkv[:, i, :] if i < 4 else dqk[:, i - 4, :]
            squares([head(late[0])])
            for i in HO_POINT:
                x_high(1, i, M, mixed_hi)
            for a, i in enumerate(late):
                if a + 1 < len(late):
                    if late[a + 1] >= 4:
                        wait_evac(act, ("PV", DF_H - 1, NQ - 1))
                    squares([head(late[a + 1])])
                rsqrt(("ho", i), 1.0 / P, T)
                if a:
                    x_high(1, late[a - 1], M, mixed_hi)
            x_high(1, late[-1], M, mixed_hi)
            for j in range(KD):
                ahead(("wo", j))
                if j:
                    x_high(1, j - 1)
            x_high(1, KD - 1)
            ffn(1, 0)
            act.dma_start(at_rot[:], rot_dram[:, 0:2]).then_inc(s_ixt, 16)
            act.dma_start(ix_rot[:], rot_dram[:, 2:4]).then_inc(s_ixt, 16)
            rsqrt(("norm", 2), 1.0 / D, TT)
            x_high(KD)
            rot = [0]

            def rotate(key, half, w):
                i = rot[0]
                wait_result(act, key)
                if i >= 2:
                    wait_evac(act, ROTATED[i - 2])
                else:
                    act.wait_ge(s_sqd, made["sq"])
                for p in range(0, P, 2 * half):
                    for a, b in ((p, p + half), (p + half, p)):
                        if w == T:
                            ins = nc.scalar.activation(square[i % 2][a:a + half, 0:T], slot(key)[b:b + half, 0:T], ACT.Copy)
                        else:
                            ins = nc.scalar.activation(halves(square[i % 2][:])[a:a + half], ps_all(key)[b:b + half], ACT.Copy)
                        A.own(ins) if (p, a) != (P - 2 * half, P - half) else A.sig(ins, s_rot, i + 1)
                rot[0] += 1
            ahead(("ik",))
            rotate(("ik",), 32, T)
            ahead(("iw",))
            for j in range(4):
                ahead(("iq", j))
                rotate(("iq", j), 32, T)
            def projected(key, blocks):
                name, g = key[0], key[1]
                if name in ("aq", "ak"):
                    rotate(key, 64, T if name == "aq" else TT)
                elif key == ("av", g, 0):
                    copy_out(key, av[g % 2][:].rearrange("p a c -> p (a c)"), w=2 * T)
                elif key == ("av", g, 1):
                    wait_result(act, key)
                    A.sig(nc.scalar.activation(avm[g % 2][0:M, :], slot(key)[0:M, 0:2 * P], ACT.Copy), *evac_at(key))
                else:
                    copy_out(key, ya[g])
                if blocks:
                    w_split(BLOCK[key] + blocks - 1 + RING)
            for s in range(IX_STEPS):
                key = ("is", 1 + s // 4, s % 4)
                w = (1 + s // 4 + 1) * P
                if s >= 2:
                    act.wait_ge(s_relud, s - 1)
                wait_result(act, key)
                A.sig(nc.scalar.activation(relu[s % 2][:, :, 0:w], slot(key)[:].rearrange("p (a c) -> p a c", a=2)[:, :, 0:w],
                                           ACT.Relu), *evac_at(key))
                if s in IX_BESIDE:
                    projected(*projection_keys(0)[IX_BESIDE.index(s)])
            for key, blocks in projection_keys(0)[len(IX_BESIDE):]:
                projected(key, blocks)
            for j in range(4):
                copy_out(("ga", j), ya[j], ACT.Sigmoid)
                w_split(BLOCK[("ga", j)] + RING)
            for s in range(ATT_STEPS + 3):
                if s >= 3:
                    e = s - 3
                    n, key = e % NQ, ("AV", e)
                    wait_result(act, key)
                    A.sig(nc.scalar.activation(att_hi[:, e // NQ, n * P:n * P + P], slot(key)[:, 0:P], ACT.Copy), s_athi, e + 1)
                if s < ATT_STEPS:
                    n, i = s % NQ, s % 2
                    w = M + (n + 1) * P
                    act.wait_ge(s_af, s + 1)
                    A.sig(nc.scalar.activation(Ax[i][:, 0:w], Ax[i][:, 0:w], ACT.Exp, bias=amx[i][:, 0:1], scale=ATT_SCALE,
                                               accum_out=asum[i][:, 0:1]), s_afa, s + 1)
                for key, blocks in filled(2 * s - 1):
                    projected(key, blocks)
                if 1 <= s <= ATT_STEPS:
                    e = s - 1
                    n, i = e % NQ, e % 2
                    if e >= 2:
                        wait_result(act, ("AV", e - 2))
                    key = ("AP", e)
                    wait_result(act, key)
                    A.own(nc.scalar.activation(At[i][0:M, 0:P], slot(key)[0:M, 0:P], ACT.Copy))
                    A.sig(nc.scalar.activation(At[i][:, P:P + (n + 1) * P], slot(key)[:, P:P + (n + 1) * P], ACT.Copy), *evac_at(key))
                for key, blocks in filled(2 * s):
                    projected(key, blocks)
            A.sync()
            for j in range(4, KD):
                A.own(nc.scalar.activation(ya[j], ya[j], ACT.Sigmoid))
            A.sync()
            act.sem_inc(s_sigm, 1)
            for j in range(KD):
                ahead(("ao", j))
            def sigmoid(key, i):
                if i >= 2:
                    act.wait_ge(s_gate, i - 1)
                wait_result(act, key)
                A.sig(nc.scalar.activation(square[i % 2][:, 0:T], slot(key)[:, 0:T], ACT.Sigmoid), *evac_at(key))
            wait_evac(act, ("ao", KD - 1))
            act.dma_start(rt_rot[:], rot_dram[:, 4:6]).then_inc(s_rtt, 16)
            for hd in range(RET_H):
                if hd:
                    act.wait_ge(s_rst, 5 * hd)
                act.dma_start(dec[:], dec_dram[:, hd]).then_inc(s_dec, 16)
                for j in range(1 if hd else 0, 4):
                    key = ("rq", hd, j) if j < 2 else ("rk", hd, j - 2)
                    ahead(key)
                    if j % 2 == 0 and (hd or j):
                        act.wait_ge(s_rotd, (2 * hd + j // 2))
                    dst = square[j % 2][:, 0:T] if j < 2 else square[j % 2][:]
                    copy_out(key, dst, w=T if j < 2 else TT)
                w_split(BLOCK[("rv", hd, 2)] + 3 + 2)
                for i in range(2):
                    wait_result(act, ("rv", hd, i))
                    A.sig(nc.scalar.activation(rv[:, 2 * i:2 * i + 2, :].rearrange("p a c -> p (a c)"),
                                               slot(("rv", hd, i))[:, :], ACT.Copy), *evac_at(("rv", hd, i)))
                A.sig(nc.scalar.activation(rvm[0:M, :], slot(("rv", hd, 2))[0:M, 0:T], ACT.Copy), *evac_at(("rv", hd, 2)))
                for j in range(2):
                    ahead(("rg", hd, j))
                    made["table"] = None
                    copy_out(("rg", hd, j), rg[:, j, :], ACT.Silu)
                ahead(("rg", hd, 2))
                act.wait_ge(s_rst, 5 * hd + 5)
                for d in range(4):
                    copy_out(("ry", hd, d), rqk[:, d, 0:T])
                copy_out(("rg", hd, 2), rg[:, 2, :], ACT.Silu)
                ahead(("rg", hd, 3))
                rsqrt(("rn", hd), 1.0 / T, T)
                x_high(3, 0, M, y_hi)
                made["table"] = None
                copy_out(("rg", hd, 3), rg[:, 3, :], ACT.Silu)
                w_split(BLOCK[("rg", hd, 3)] + 1 + 3)
                x_high(1, 3, M, y_hi)
                if hd + 1 < RET_H:
                    copy_out(("rq", hd + 1, 0), square[0][:, 0:T])
                for j in range(KD):
                    ahead(("wr", hd, j))
            for j in range(KD):
                ahead(("gr", j))
                sigmoid(("gr", j), j)
                if j:
                    x_high(1, j - 1, M, merged_hi)
            x_high(1, KD - 1, M, merged_hi)
            for j in range(KD):
                ahead(("mx", j))
                if j:
                    x_high(1, j - 1, M)
            x_high(1, KD - 1, M)
            ffn(2, M)
            rsqrt(("norm", 4), 1.0 / D, T)
            for k in range(0, KD, 2):
                act.wait_ge(s_y, k + 2)
                act.dma_start(out_dram[:, k:k + 2], h[:, k:k + 2, TQ]).then_inc(s_out, 16)
            act.wait_ge(s_out, 16 * KD // 2)

        @block.vector
        def _(dve):
            V = Own(dve, s_v)
            made = {"rs": 0, "x": 0, "acc": 0}

            def split(makers, c0=0, k0=0, hi=x_hi, lo=x_lo, ks=None):
                d0 = c0 if hi is x_hi else 0
                ks = ks or range(k0, k0 + len(makers))

                def low(m, k):
                    dve.wait_ge(s_xhi, m + 1)
                    V.sig(nc.vector.tensor_tensor(lo[:, k, d0:], xt[m % 2][:, c0:TT],
                                                  hi[:, k, d0:].bitcast(F32), ALU.subtract), s_xlo, m + 1)
                for i, maker in enumerate(makers):
                    m = made["x"]
                    if i >= 2:
                        V.sync()
                    maker(xt[m % 2][:, c0:TT], m)
                    made["x"] += 1
                    if i:
                        low(m - 1, ks[i - 1])
                low(made["x"] - 1, ks[-1])

            def model_norm(gain, c0):
                r = made["rs"]
                dve.wait_ge(s_rs, r + 1)
                split([lambda dst, m, k=k: V.sig(nc.vector.scalar_tensor_tensor(
                    dst, h[:, k, c0:TT], sml(gain, k), rs[r % 2][:, 0:TT - c0], ALU.mult, ALU.mult), s_xt, m + 1)
                    for k in range(KD)], c0)
                V.sync()
                dve.sem_inc(s_rsd, 1)
                made["rs"] += 1

            def few(name):
                wait_result(dve, (name,))
                V.sync()
                V.sig(nc.vector.tensor_copy(xt[0][0:8, 0:T], slot((name,))[0:8, 0:T]), *evac_at((name,)))

            V.sig(nc.vector.memset(eps[:], EPS), s_eps, 1)
            dve.wait_ge(s_gain, 16)
            for i in range(4):
                dve.wait_ge(s_x[i], 16)
            model_norm("norm_gain", M)
            dve.wait_ge(s_small, 48)
            def head_norm(i):
                r = made["rs"]
                dve.wait_ge(s_rs, r + 1)
                if i < 8:
                    t, gain, const_s = qkv[:, i, :], (P ** -0.5 if i < 4 else 1.0), None
                    V.sig(nc.vector.scalar_tensor_tensor(t, t, gain, rs[r % 2][:, 0:T], ALU.mult, ALU.mult), s_rsd, r + 1)
                else:
                    t = dqk[:, i - 8, :]
                    gain = sml("q_gain" if i < 12 else "k_gain")
                    V.sig(nc.vector.scalar_tensor_tensor(t, t, gain, rs[r % 2][:, 0:T], ALU.mult, ALU.mult), s_rsd, r + 1)
                    if i < 12:
                        V.sync()
                        V.own(nc.vector.tensor_scalar(t, t, 64 ** -0.5, None, ALU.mult))
                made["rs"] += 1
            V.own(nc.vector.tensor_tensor(lamt[0:64, 0:1], sml("lq1")[0:64], sml("lk1")[0:64], ALU.mult))
            V.sig(nc.vector.tensor_tensor(lamt[0:64, 1:2], sml("lq2")[0:64], sml("lk2")[0:64], ALU.mult), s_df, 1)
            for j in range(12):
                key = ("qkv", j)
                wait_result(dve, key)
                ps = slot(key)
                cw = lambda i: sml("conv", 4 * j + i)
                V.own(nc.vector.tensor_scalar(qkv[:, j, :], ps[:, 0:T], cw(3), None, ALU.mult))
                for i in (1, 2, 3):
                    V.sync()
                    ins = nc.vector.scalar_tensor_tensor(qkv[:, j, i:T], ps[:, 0:T - i], cw(3 - i), qkv[:, j, i:T],
                                                         ALU.mult, ALU.add)
                    if i < 3:
                        V.own(ins)
                    else:
                        V.sig(ins, *evac_at(key))
                for i in norms_after(j):
                    head_norm(i)
            few("ab")
            key = ("ab_t",)
            wait_result(dve, key)
            V.sig(nc.vector.tensor_copy(ab[:].rearrange("p n c -> p (n c)"), slot(key)[:, 0:NQ * 8]), *evac_at(key))
            V.sync()
            dtb = sml("dt_bias", 0, 4).unsqueeze(1).broadcast_to([P, NQ, 4])
            V.own(nc.vector.tensor_tensor(g[:], ab[:, :, 4:8], dtb, ALU.add))
            V.sync()
            V.own(nc.vector.tensor_scalar(tA[:], g[:], -1.0, None, ALU.mult))
            V.sync()
            V.own(nc.vector.tensor_tensor(tA[:], tA[:], g[:], ALU.max))
            V.sync()
            V.sig(nc.vector.tensor_scalar(tB[:], g[:], 0.0, None, ALU.max), s_g, 1)
            for i in norms_after(12):
                head_norm(i)
            dve.wait_ge(s_da, 1)
            V.own(nc.vector.tensor_tensor(tB[:], tB[:], tA[:], ALU.add))
            V.own(nc.vector.tensor_scalar(beta[:], beta[:], 1.0, None, ALU.add))
            V.sync()
            V.own(nc.vector.reciprocal(beta[:], beta[:]))
            V.own(nc.vector.scalar_tensor_tensor(g[:], tB[:], -1.0, nea[:].unsqueeze(1).broadcast_to([P, NQ, 4]), ALU.mult, ALU.mult))
            V.sync()
            dn = [0]

            def dsig(ins, name, n):
                dn[0] += 1
                assert dn[0] == dnv(name, n), (name, n)
                V.sig(ins, s_dn, dn[0])

            def per_token(ap):
                return ap.unsqueeze(2).broadcast_to([P, 4, P])

            def per_head(name):
                return K(name).unsqueeze(1).broadcast_to([P, 4, P])
            point = [0]

            def head_scaled(i, dst):
                r = made["rs"]
                dve.wait_ge(s_rs, r + 1)
                V.sig(nc.vector.scalar_tensor_tensor(dst, qkv[:, i, :] if i < 4 else dqk[:, i - 4, :], sml("dn_gain" if i < 4 else "df_gain"),
                                                     rs[r % 2][:, 0:T], ALU.mult, ALU.mult), s_rsd, r + 1)
                made["rs"] += 1

            def aside():
                p = point[0]
                point[0] += 1
                for i in norm_at(p, 3):
                    head_norm(8 + i)
                for i, first in HO_POINT.items():
                    if p == first + 3:
                        head_scaled(i, dqk[:, i - 4, :])
                if p < DF_START or (p - DF_START) % 2 == 0:
                    return
                e = df_at(p, 1)
                if e is not None:
                    j, n, i = e // NQ, e % NQ, e % 2
                    w = (n + 1) * P
                    dve.wait_ge(s_dfa, 2 * e + 2)
                    V.own(nc.vector.reciprocal(sums_[i][:], sums_[i][:]))
                    V.sync()
                    V.own(nc.vector.tensor_scalar(sums_[i][:, 1:2], sums_[i][:, 1:2], lamt[:, 5:6], None, ALU.mult))
                    V.sync()
                    V.own(nc.vector.tensor_scalar(Sx[i][1][:, 0:w], Sx[i][1][:, 0:w], sums_[i][:, 1:2], None, ALU.mult))
                    V.sync()
                    V.sig(nc.vector.scalar_tensor_tensor(Pm[i][:, 0:w], Sx[i][0][:, 0:w], sums_[i][:, 0:1], Sx[i][1][:, 0:w],
                                                         ALU.mult, ALU.add), s_dfp, e + 1)
                s = df_at(p, 0)
                if s is not None:
                    j, n, i = s // NQ, s % NQ, s % 2
                    w = (n + 1) * P
                    key = ("S", j, n)
                    if s >= 2:
                        wait_result(dve, ("PT", (s - 2) // NQ, (s - 2) % NQ))
                    wait_result(dve, key)
                    for c in range(2):
                        ins = nc.vector.tensor_tensor_reduce(Sx[i][c][:, 0:w], slot(key)[:, c * 512:c * 512 + w],
                                                             K("causal")[:, T - w:T], 1.0, NEG, ALU.add, ALU.max, mx[i][:, c:c + 1])
                        V.own(ins) if c == 0 else V.sig(ins, *evac_at(key))
                    V.sync()
                    V.sig(nc.vector.tensor_scalar(mx[i][:], mx[i][:], -1.0, None, ALU.mult), s_df, 2 + s)
                e = df_at(p, 3)
                if e is not None:
                    j, n = e // NQ, e % NQ
                    key = ("PV", j, n)
                    wait_result(dve, key)
                    V.sig(nc.vector.tensor_copy(dqk[:, j, n * P:n * P + P], slot(key)[:, 0:P]), *evac_at(key))
            for n in range(NQ):
                tok = slice(n * P, n * P + P)
                V.sync()
                if n:
                    wait_result(dve, ("beb", n - 1))
                if n == 1:
                    wait_evac(dve, ("lam",))
                    V.own(nc.vector.scalar_tensor_tensor(lamt[:, 4:5], lamt[:, 2:3], LAMBDA_INIT, lamt[:, 3:4], ALU.add, ALU.subtract))
                    V.sync()
                    V.own(nc.vector.tensor_scalar(lamt[:, 5:6], lamt[:, 4:5], -1.0, None, ALU.mult))
                V.own(nc.vector.tensor_copy(bB[:], per_token(beta[:, n, :])))
                dsig(nc.vector.tensor_copy(gB[:], per_token(g[:, n, :])), "gB", n)
                wait_result(dve, ("sm", n))
                V.sig(nc.vector.tensor_copy(sm[:], slot(("sm", n))[:, 0:16]), *evac_at(("sm", n)))
                V.sync()
                for hd in range(4):
                    ins = nc.vector.tensor_scalar(DT[:, hd, :], slot(("gcb", n))[:, hd * P:hd * P + P], sm[:, hd:hd + 1], 0.0,
                                                  ALU.subtract, ALU.min)
                    if hd < 3:
                        V.own(ins)
                    else:
                        dsig(ins, "dt", n)
                V.sig(nc.vector.tensor_tensor(kb[:], qkv[:, 4:8, tok], heads(slot(("beb", n))[:, 0:T]), ALU.mult), *evac_at(("beb", n)))
                wait_evac(dve, ("gcb", n))
                V.own(nc.vector.tensor_tensor(DT[:], DT[:], per_head("tri"), ALU.mult))
                dsig(nc.vector.tensor_tensor(qg[:], qkv[:, 0:4, tok], EG[:], ALU.mult), "qg", n)
                aside()
                aside()
                wait_result(dve, ("N0", n))
                V.sync()
                V.sig(nc.vector.tensor_tensor(N[:], heads(slot(("N0", n))[:, 0:T]), DT[:], ALU.mult), *evac_at(("N0", n)))
                V.sync()
                V.own(nc.vector.tensor_tensor(U[:], N[:], per_head("join0"), ALU.mult))
                V.sync()
                dsig(nc.vector.scalar_tensor_tensor(U[:], U[:], -1.0, per_head("ident"), ALU.mult, ALU.add), "U", n)
                wait_result(dve, ("A0", n))
                V.sig(nc.vector.tensor_tensor(AT[:], heads(slot(("A0", n))[:, 0:T]), DT[:], ALU.mult), *evac_at(("A0", n)))
                wait_result(dve, ("T1", n))
                V.sig(nc.vector.tensor_copy(Tm[:].rearrange("p h c -> p (h c)"), slot(("T1", n))[:, 0:T]), *evac_at(("T1", n)))
                V.sync()
                aside()
                dsig(nc.vector.tensor_tensor(Ns[0][:], N[:], per_head("join1"), ALU.mult), "Ns0", n)
                for l in range(5):
                    if l < 4:
                        dsig(nc.vector.tensor_tensor(Ns[(l + 1) % 2][:], N[:], per_head(f"join{l + 2}"), ALU.mult), f"Ns{l + 1}", n)
                    if l == 0:
                        dve.wait_ge(s_da, 1 + 2 * n + 2)
                        V.own(nc.vector.tensor_tensor(cb[:], esm[:, 0:4], beta[:, n, :], ALU.mult))
                        wait_result(dve, ("kt", n))
                        V.sync()
                        V.own(nc.vector.tensor_tensor(kdec[:], heads(slot(("kt", n))[:, 0:T]), per_token(esm[:, 4:8]), ALU.mult))
                        V.sig(nc.vector.tensor_tensor(kbg[:], heads(slot(("kt", n))[:, 0:T]), per_token(cb[:]), ALU.mult), *evac_at(("kt", n)))
                        wait_result(dve, ("vt", n))
                        V.sig(nc.vector.tensor_tensor(vb[:], heads(slot(("vt", n))[:, 0:T]), per_token(beta[:, n, :]), ALU.mult), *evac_at(("vt", n)))
                    aside()
                    aside()
                    if l < 4:
                        wait_result(dve, ("dT", n, l))
                        V.sig(nc.vector.tensor_tensor(Tm[:], Tm[:], heads(slot(("dT", n, l))[:, 0:T]), ALU.subtract), *evac_at(("dT", n, l)))
                    wait_result(dve, ("dU", n, l))
                    V.sig(nc.vector.tensor_tensor(U[:], U[:], heads(slot(("dU", n, l))[:, 0:T]), ALU.subtract), *evac_at(("dU", n, l)))
                    V.sync()
                wait_result(dve, ("wT", n))
                V.sig(nc.vector.tensor_copy(wT[:].rearrange("p h c -> p (h c)"), slot(("wT", n))[:, 0:T]), *evac_at(("wT", n)))
                aside()
                wait_evac(dve, ("u", n))
                for c in range(2):
                    rr = slice(c * CH, c * CH + CH)
                    i = 2 * n + c
                    if i:
                        wait_result(dve, ("wS", n, c))
                        V.sig(nc.vector.tensor_tensor(vnew[rr], u[rr], heads(slot(("wS", n, c))[rr, 0:T]), ALU.subtract), *evac_at(("wS", n, c)))
                    aside()
                    if i == 2 * NQ - 1:
                        aside()
                        continue
                    if i:
                        V.own(nc.vector.tensor_tensor(Sd[:], state[:], per_token(esm[:, 8 + 4 * c:12 + 4 * c]), ALU.mult))
                        V.sync()
                    wait_result(dve, ("dS", n, c))
                    if i:
                        V.sig(nc.vector.tensor_tensor(state[:], Sd[:], heads(slot(("dS", n, c))[:, 0:T]), ALU.add), *evac_at(("dS", n, c)))
                    else:
                        V.sig(nc.vector.tensor_copy(state[:].rearrange("p h c -> p (h c)"), slot(("dS", n, c))[:, 0:T]), *evac_at(("dS", n, c)))
                    V.sync()
                    aside()
            while point[0] < LAST_POINT:
                aside()
            dve.wait_ge(s_silu, 8 + 1)

            def head_out(i):
                def maker(dst, m):
                    src = dqk[:, i - 4, :] if i in HO_POINT else dst
                    if i not in HO_POINT:
                        head_scaled(i, dst)
                        V.sync()
                    z = sz[:, :, i, :] if i < 4 else dsz[:, i - 4, :]
                    if i < 4:
                        src, dst = (x.rearrange("p (a t) -> p a t", a=2) for x in (src, dst))
                    V.sig(nc.vector.scalar_tensor_tensor(dst, src, 1.0 if i < 4 else 1.0 - LAMBDA_INIT, z, ALU.mult, ALU.mult), s_xt, m + 1)
                return maker
            split([head_out(i) for i in HEADS_OUT], M, 0, mixed_hi, mixed_lo, HEADS_OUT)

            def x_low(j, c0):
                m = made["x"] - 1
                dve.wait_ge(s_xhi, m + 1)
                V.sig(nc.vector.tensor_tensor(x_lo[:, j, c0:TT], xt[m % 2][:, c0:TT], x_hi[:, j, c0:TT].bitcast(F32), ALU.subtract), s_xlo, m + 1)

            def add_to_h(key, c0, gain):
                j = key[-1]
                if j:
                    x_low(j - 1, c0)
                else:
                    V.own(nc.vector.memset(square[1][:], 0.0))
                wait_result(dve, key)
                V.sig(nc.vector.tensor_tensor(h[:, j, TQ], h[:, j, TQ], slot(key)[:, 0:T], ALU.add), *evac_at(key))
                V.sync()
                w = TT - c0
                V.sig(nc.vector.tensor_tensor(square[0][:, 0:w], h[:, j, c0:TT], h[:, j, c0:TT], ALU.mult), s_acc, made["acc"] + 1)
                V.sync()
                V.sig(nc.vector.tensor_tensor(square[1][:, 0:w], square[1][:, 0:w], square[0][:, 0:w], ALU.add), s_acc, made["acc"] + 2)
                made["acc"] += 2
                m = made["x"]
                V.sig(nc.vector.tensor_scalar(xt[m % 2][:, c0:TT], h[:, j, c0:TT], sml(gain, j), None, ALU.mult), s_xt, m + 1)
                made["x"] += 1
                if j == KD - 1:
                    x_low(j, c0)
            for j in range(KD):
                add_to_h(("wo", j), 0, "f1_gain")

            def ffn(i, c0):
                V.sync()
                r = made["rs"]
                dve.wait_ge(s_rs, r + 1)
                norm = rs[r % 2][:, 0:TT - c0]
                b0, m0 = BLOCK[("gate", i, 0)], made["x"]
                wide, f0 = c0 == 0, (i - 1) * KF
                with dve.Fori(0, KF // 2) as g:
                    for j in range(2):
                        gate, up = ("gate", i, j), ("up", i, j)
                        q, o, psg, psu = square[j][:, 0:TT - c0], xt[j][:, c0:TT], slot(gate)[:, 0:T], slot(up)[:, 0:T]
                        qq, oo, nn = q, o, norm
                        if wide:
                            qq, oo, nn, psg, psu = halves(q), halves(o), halves(norm), ps_all(gate), ps_all(up)
                        dve.wait_ge(s_used, g * 4 + (b0 + 2 * j + 1))
                        nc.vector.tensor_tensor(qq, psg, nn, ALU.mult).then_inc(evac_in(gate, g)[0], 1)
                        dve.wait_ge(s_used, g * 4 + (b0 + 2 * j + 2))
                        dve.wait_ge(s_xlo, g * 2 + (m0 + j))
                        nc.vector.tensor_tensor(oo, psu, nn, ALU.mult).then_inc(evac_in(up, g)[0], 1)
                        dve.wait_ge(*evac_in(up, g))
                        dve.wait_ge(s_fsilu, g * 2 + (f0 + j + 1))
                        nc.vector.tensor_tensor(o, o, q, ALU.mult).then_inc(s_xt, 1)
                        dve.wait_ge(s_xhi, g * 2 + (m0 + j + 1))
                        nc.vector.tensor_tensor(f_lo[:, g * 2 + j, c0:TT], xt[j][:, c0:TT],
                                                f_hi[:, g * 2 + j, c0:TT].bitcast(F32), ALU.subtract).then_inc(s_xlo, 1)
                made["x"] += KF
                b1, a0, w = BLOCK[("down", i, 0)], made["acc"], TT - c0
                V.last = (s_xlo, made["x"])
                V.sync()
                dve.sem_inc(s_rsd, 1)
                made["rs"] += 1
                V.own(nc.vector.memset(square[1][:], 0.0))
                V.sync()
                with dve.Fori(0, 2) as g:
                    for j in range(4):
                        key = ("down", i, j)
                        dve.wait_ge(s_used, g * 12 + (b1 + 3 * j + 3))
                        hh = h[:, g * 4 + j, c0:TT]
                        src = slot(key)[:, 0:T]
                        if wide:
                            hh, src = halves(hh), ps_all(key)
                        s_, v = evac_in(key, g)
                        nc.vector.scalar_tensor_tensor(hh, src, 0.5, hh, ALU.mult, ALU.add).then_inc(s_, 1)
                        dve.wait_ge(s_, v)
                        hh = h[:, g * 4 + j, c0:TT]
                        nc.vector.tensor_tensor(square[0][:, 0:w], hh, hh, ALU.mult).then_inc(s_acc, 1)
                        dve.wait_ge(s_acc, g * 8 + (a0 + 2 * j + 1))
                        nc.vector.tensor_tensor(square[1][:, 0:w], square[1][:, 0:w], square[0][:, 0:w],
                                                ALU.add).then_inc(s_acc, 1)
                        dve.wait_ge(s_acc, g * 8 + (a0 + 2 * j + 2))
                made["acc"] += 16
                V.last = (s_acc, made["acc"])
                V.sync()
            ffn(1, 0)
            model_norm("mix_gain", 0)
            rot = [0]
            dve.wait_ge(s_ixt, 32)

            def rotated(key, table, dst, w):
                i = rot[0]
                c0 = TT - w
                dve.wait_ge(s_rot, i + 1)
                src = slot(key)[:, 0:T] if w == T else ps_all(key)
                tab = lambda k: table[:, k, c0:TT] if w == T else halves(table[:, k, :])
                d = dst if w == T else halves(dst)
                other = square[i % 2][:, 0:T] if w == T else halves(square[i % 2][:])
                V.own(nc.vector.tensor_tensor(other, other, tab(1), ALU.mult))
                V.own(nc.vector.tensor_tensor(d, src, tab(0), ALU.mult))
                V.sync()
                V.sig(nc.vector.tensor_tensor(d, d, other, ALU.add), *evac_at(key))
                rot[0] += 1
            rotated(("ik",), ix_rot, ik[:], T)
            few("iw")
            wait_result(dve, ("iw_t",))
            V.sig(nc.vector.tensor_scalar(iw[:].rearrange("p n c -> p (n c)"), slot(("iw_t",))[:, 0:NQ * 8], IDX_SCALE, None, ALU.mult),
                  *evac_at(("iw_t",)))
            for j in range(4):
                rotated(("iq", j), ix_rot, iq[:, j, :], T)
            V.own(nc.vector.memset(bias[:, :, 0:M], 0.0))
            V.own(nc.vector.tensor_copy(bias[:, 0, M:M + P], K("causal")[:, T - P:T]))
            def projected(key):
                if key[0] in ("aq", "ak"):
                    name, g, j = key
                    rotated(key, at_rot, (aq if name == "aq" else ak)[g % 2][:, j, :], T if name == "aq" else TT)
            for s in range(IX_STEPS):
                n, j = 1 + s // 4, s % 4
                w = (n + 1) * P
                key = ("is", n, j)
                wait_evac(dve, key)
                for a in range(2):
                    V.sync()
                    before = K("causal")[:, T - w:T] if (j, a) == (0, 0) else score[n - 1][:, 0:w]
                    ins = nc.vector.scalar_tensor_tensor(score[n - 1][:, 0:w], relu[s % 2][:, a, 0:w], iw[:, n, 2 * j + a:2 * j + a + 1],
                                                         before, ALU.mult, ALU.add)
                    V.own(ins) if a == 0 else V.sig(ins, s_relud, s + 1)
                if s in IX_BESIDE:
                    projected(projection_keys(0)[IX_BESIDE.index(s)][0])
            rounds = [K_TOP // 8]

            def top(k):
                for _ in range(k):
                    rounds[0] -= 1
                    V.sync()
                    for n in range(1, NQ):
                        V.own(nc.vector.max(top8[:, n - 1, :], score[n - 1][:, 0:(n + 1) * P]))
                    V.sync()
                    for n in range(1, NQ):
                        w = (n + 1) * P
                        V.own(nc.vector.match_replace(score[n - 1][:, 0:w], top8[:, n - 1, :], score[n - 1][:, 0:w], TAKEN))
                if not rounds[0]:
                    V.sync()
                    for n in range(1, NQ):
                        w = (n + 1) * P
                        V.own(nc.vector.tensor_scalar(score[n - 1][:, 0:w], score[n - 1][:, 0:w], TAKEN, NEG, ALU.not_equal, ALU.mult))
                    V.sync()
                    for n in range(1, NQ):
                        w = (n + 1) * P
                        V.own(nc.vector.tensor_tensor(bias[:, n, M:M + w], score[n - 1][:, 0:w], K("causal")[:, T - w:T], ALU.add))

            for key, _ in projection_keys(0)[len(IX_BESIDE):]:
                top(3)
                projected(key)
            top(rounds[0])
            V.sync()
            for s in range(ATT_STEPS + 3):
                if 1 <= s <= ATT_STEPS:
                    e = s - 1
                    n, i = e % NQ, e % 2
                    w = M + (n + 1) * P
                    dve.wait_ge(s_afa, e + 1)
                    V.own(nc.vector.reciprocal(asum[i][:], asum[i][:]))
                    V.sync()
                    V.sig(nc.vector.tensor_scalar(Ax[i][:, 0:w], Ax[i][:, 0:w], asum[i][:, 0:1], None, ALU.mult), s_afp, e + 1)
                if s < ATT_STEPS:
                    n, i = s % NQ, s % 2
                    w = M + (n + 1) * P
                    key = ("AS", s)
                    if s >= 2:
                        wait_result(dve, ("AP", s - 2))
                    wait_result(dve, key)
                    V.sig(nc.vector.tensor_tensor_reduce(Ax[i][:, 0:w], slot(key)[:, 0:w], bias[:, n, 0:w], 1.0, NEG,
                                                         ALU.add, ALU.max, amx[i][:, 0:1]), *evac_at(key))
                    V.sync()
                    V.sig(nc.vector.tensor_scalar(amx[i][:], amx[i][:], -ATT_SCALE, None, ALU.mult), s_af, s + 1)
                for key, _ in filled(2 * s - 1):
                    projected(key)
                if s >= 3:
                    e = s - 3
                    n, key = e % NQ, ("AV", e)
                    dve.wait_ge(s_athi, e + 1)
                    V.sig(nc.vector.tensor_tensor(att_lo[:, e // NQ, n * P:n * P + P], slot(key)[:, 0:P],
                                                  att_hi[:, e // NQ, n * P:n * P + P].bitcast(F32), ALU.subtract), *evac_at(key))
                for key, _ in filled(2 * s):
                    projected(key)
            dve.wait_ge(s_sigm, 1)
            for j in range(KD):
                key = ("ao", j)
                wait_result(dve, key)
                V.sig(nc.vector.tensor_tensor(ya[j], slot(key)[:, 0:T], ya[j], ALU.mult), *evac_at(key))
            dve.wait_ge(s_rtt, 16)
            for hd in range(RET_H):
                for a, (name, w) in enumerate((("rq", T), ("rk", TT))):
                    for j in range(2):
                        wait_evac(dve, (name, hd, j))
                    x1, x2 = square[0][:, 0:w], square[1][:, 0:w]
                    o1, o2 = rqk[:, 2 * a, 0:w], rqk[:, 2 * a + 1, 0:w]
                    cos, sin = rt_rot[:, 0, TT - w:TT], rt_rot[:, 1, TT - w:TT]
                    V.sync()
                    V.own(nc.vector.tensor_tensor(o1, x1, cos, ALU.mult))
                    V.own(nc.vector.tensor_tensor(o2, x2, cos, ALU.mult))
                    V.own(nc.vector.tensor_tensor(x2, x2, sin, ALU.mult))
                    V.own(nc.vector.tensor_tensor(x1, x1, sin, ALU.mult))
                    V.sync()
                    V.own(nc.vector.tensor_tensor(o1, o1, x2, ALU.subtract))
                    V.sig(nc.vector.tensor_tensor(o2, o2, x1, ALU.add), s_rotd, 2 * hd + a + 1)
                dve.wait_ge(s_dec, 16 * (hd + 1))
                for kt in range(NQ + 1):
                    key = ("rs", hd, kt)
                    wait_result(dve, key)
                    q0 = max(kt * P - M, 0)
                    w, d0 = T - q0, (0 if kt else M)
                    if kt < NQ:
                        ins = nc.vector.tensor_tensor(rst[:, kt, q0:T], slot(key)[:, 0:w], dec[:, d0:d0 + w], ALU.mult)
                    else:
                        ins = nc.vector.tensor_tensor(rstm[0:M, 0:w], slot(key)[0:M, 0:w], dec[0:M, 0:w], ALU.mult)
                    V.sig(ins, *evac_at(key))
                    V.sync()
                    dve.sem_inc(s_rst, 1)

                V.own(nc.vector.memset(square[1][:, 0:T], 0.0))
                for d in range(4):
                    wait_evac(dve, ("ry", hd, d))
                    V.sync()
                    V.sig(nc.vector.tensor_tensor(square[0][:, 0:T], rqk[:, d, 0:T], rqk[:, d, 0:T], ALU.mult), s_acc, made["acc"] + 1)
                    V.sync()
                    V.sig(nc.vector.tensor_tensor(square[1][:, 0:T], square[1][:, 0:T], square[0][:, 0:T], ALU.add), s_acc, made["acc"] + 2)
                    made["acc"] += 2
                for d in range(3):
                    wait_evac(dve, ("rg", hd, d))
                    V.own(nc.vector.tensor_tensor(rqk[:, d, 0:T], rqk[:, d, 0:T], rg[:, d, :], ALU.mult))
                V.sync()

                def ret_out(d):
                    def maker(dst, m):
                        r = made["rs"]
                        if d == 0:
                            dve.wait_ge(s_rs, r + 1)
                        src = rqk[:, d, 0:T]
                        if d == 3:
                            wait_evac(dve, ("rg", hd, 3))
                            V.own(nc.vector.tensor_tensor(src, src, rg[:, 3, :], ALU.mult))
                            V.sync()
                        V.sig(nc.vector.tensor_tensor(dst, src, rs[r % 2][:, 0:T], ALU.mult), s_xt, m + 1)
                    return maker
                split([ret_out(d) for d in range(4)], M, 0, y_hi, y_lo)
                V.sync()
                dve.sem_inc(s_rsd, 1)
                made["rs"] += 1
                for j in range(KD):
                    key = ("wr", hd, j)
                    wait_result(dve, key)
                    if hd == 0:
                        V.sig(nc.vector.tensor_copy(yr[:, j, :], slot(key)[:, 0:T]), *evac_at(key))
                    else:
                        V.sig(nc.vector.tensor_tensor(yr[:, j, :], yr[:, j, :], slot(key)[:, 0:T], ALU.add), *evac_at(key))
            def merge(j):
                def maker(dst, m):
                    wait_evac(dve, ("gr", j))
                    V.sync()
                    V.sig(nc.vector.tensor_tensor(yr[:, j, :], yr[:, j, :], square[j % 2][:, 0:T], ALU.mult), s_gate, j + 1)
                    V.sync()
                    V.sig(nc.vector.tensor_tensor(dst, yr[:, j, :], ya[j], ALU.add), s_xt, m + 1)
                return maker
            split([merge(j) for j in range(KD)], M, 0, merged_hi, merged_lo)
            for j in range(KD):
                add_to_h(("mx", j), M, "f2_gain")
            ffn(2, M)
            r = made["rs"]
            dve.wait_ge(s_rs, r + 1)
            for k in range(KD):
                V.sig(nc.vector.scalar_tensor_tensor(h[:, k, TQ], h[:, k, TQ], sml("final_gain", k), rs[r % 2][:, 0:T],
                                                     ALU.mult, ALU.mult), s_y, k + 1)

        @block.tensor
        def _(pe):
            done = {"sq": 0, "acc": 0}

            def begin(key):
                for last in FREE[key]:
                    wait_evac(pe, last)
                return slot(key)

            def mm(out, lhsT, rhs, start, stop):
                return nc.tensor.matmul(out, lhsT, rhs, start=start, stop=stop)

            def mm3(out, a, b, start, stop):
                mm(out, a[0], b[0], start, False)
                mm(out, a[1], b[0], False, False)
                return mm(out, a[0], b[1], False, stop)

            def sums(key, n, w, ones="ones"):
                ps = begin(key)
                for i in range(n):
                    q = done["sq"]
                    pe.wait_ge(s_sq, q + 1)
                    if w == T:
                        m = mm(ps[:, 0:T], K(ones), square[q % 2][:, 0:T], i == 0, i == n - 1)
                    else:
                        for a in range(2):
                            m = mm(ps[:, a * 512:a * 512 + HALF], K(ones), square[q % 2][:, a * HALF:a * HALF + HALF], i == 0, i == n - 1)
                    m.then_inc(s_sqd, 1)
                    done["sq"] += 1
                pe.wait_ge(s_sqd, done["sq"])
                pe.sem_inc(s_res, 1)

            def total(key, n, w):
                ps = begin(key)
                done["acc"] += 2 * n
                pe.wait_ge(s_acc, done["acc"])
                if w == T:
                    m = mm(ps[:, 0:T], K("ones"), square[1][:, 0:T], True, True)
                else:
                    for a in range(2):
                        m = mm(ps[:, a * 512:a * 512 + HALF], K("ones"), square[1][:, a * HALF:a * HALF + HALF], True, True)
                m.then_inc(s_res, 1)

            def dense(key, parts, x=(x_hi, x_lo), made_before=None, order=range(KD)):
                ps = begin(key)
                b = BLOCK[key]
                pe.wait_ge(s_lo, b + 1)
                w = (w_hi[b % RING], w_lo[b % RING])
                for i, k in enumerate(order):
                    if made_before is not None:
                        pe.wait_ge(s_xlo, made_before + i + 1)
                    for o0, c0, c1 in parts:
                        m = mm3(ps[:, o0:o0 + c1 - c0], (w[0][:, k * P:k * P + P], w[1][:, k * P:k * P + P]),
                                (x[0][:, k, c0:c1], x[1][:, k, c0:c1]), i == 0, i == KD - 1)
                m.then_inc(s_used, 1)

            SEQ = [(0, M, TT)]
            ALL = [(0, 0, HALF), (512, HALF, TT)]

            pe.wait_ge(s_const, 16)
            sums(("norm", 0), KD, T)
            pe.wait_ge(s_small, 48)
            for j in range(12):
                dense(("qkv", j), SEQ, made_before=0 if j == 0 else None)
                for i in norms_after(j):
                    sums(("hn", i), 1, T)
            def few(name):
                dense((name,), SEQ)
                wait_evac(pe, (name,))
                ps = begin((name + "_t",))
                for n in range(NQ):
                    m = nc.tensor.transpose(ps[:, n * 8:n * 8 + 8], xt[0][0:8, n * P:n * P + P], const[0:8, 0:8])
                m.then_inc(s_res, 1)
            few("ab")
            for i in norms_after(12):
                sums(("hn", i), 1, T)
            sl = [begin(("dv", 0)), begin(("dv", 1))]
            b = BLOCK[("dv", 1)]
            for i in range(4):
                pe.wait_ge(s_lo, b + i + 1)
                w = (w_hi[(b + i) % RING], w_lo[(b + i) % RING])
                for kk in range(2):
                    k = 2 * i + kk
                    for n in range(NQ):
                        tk = slice(M + n * P, M + n * P + P)
                        m = mm3(sl[n // 2][:, (n % 2) * 512:(n % 2) * 512 + 512], (x_hi[:, k, tk], x_lo[:, k, tk]),
                                (w[0][:, kk * 512:kk * 512 + 512], w[1][:, kk * 512:kk * 512 + 512]), k == 0, k == KD - 1)
                m.then_inc(s_used, 1)
            pe.wait_ge(s_df, 1)
            ps = begin(("lam",))
            mm(ps[:, 0:2], K("ones")[0:64], lamt[0:64, 0:2], True, True).then_inc(s_res, 1)

            def four(key, f):
                ps = begin(key)
                for hd in range(4):
                    m = f(ps[:, hd * P:hd * P + P], hd)
                m.then_inc(s_res, 1)
            point = [0]

            def aside():
                p = point[0]
                point[0] += 1
                for t in [t for t in range(8 * len(ASIDE_DENSE)) if DENSE_POINTS[t] == p]:
                    f, k = divmod(t, 8)
                    key = ASIDE_DENSE[f]
                    b = BLOCK[key]
                    if k == 0:
                        begin(key)
                        pe.wait_ge(s_lo, b + 1)
                    m = mm3(slot(key)[:, 0:T], (w_hi[b % RING][:, k * P:k * P + P], w_lo[b % RING][:, k * P:k * P + P]),
                            (x_hi[:, k, TQ], x_lo[:, k, TQ]), k == 0, k == KD - 1)
                    if k == KD - 1:
                        m.then_inc(s_used, 1)
                for i in norm_at(p, 1):
                    sums(("hn", 8 + i), 1, T, "ones64")
                for i, first in HO_POINT.items():
                    if p == first + 1:
                        sums(("ho", i), 1, T)
                if p < DF_START or (p - DF_START) % 2:
                    return
                s = df_at(p, 0)
                if s is not None:
                    j, n = s // NQ, s % NQ
                    ps = begin(("S", j, n))
                    for c in range(2):
                        r = slice(64 * c, 64 * c + 64)
                        m = mm(ps[:, c * 512:c * 512 + (n + 1) * P], dqk[r, j, n * P:n * P + P], dqk[r, 4 + j, 0:(n + 1) * P], True, True)
                    m.then_inc(s_res, 1)
                e = df_at(p, 2)
                if e is not None:
                    j, n, i = e // NQ, e % NQ, e % 2
                    pe.wait_ge(s_dfp, e + 1)
                    ps = begin(("PT", j, n))
                    for kt in range(n + 1):
                        m = nc.tensor.transpose(ps[:, kt * P:kt * P + P], Pm[i][:, kt * P:kt * P + P], K("ident"))
                    m.then_inc(s_res, 1)
                e = df_at(p, 3)
                if e is not None:
                    j, n, i = e // NQ, e % NQ, e % 2
                    wait_evac(pe, ("PT", j, n))
                    ps = begin(("PV", j, n))
                    for kt in range(n + 1):
                        m = mm(ps[:, 0:P], dv[:, kt, j * P:j * P + P], PTs[:, kt * P:kt * P + P], kt == 0, kt == n)
                    m.then_inc(s_res, 1)
            for n in range(NQ):
                tok = slice(n * P, n * P + P)
                pe.wait_ge(s_dn, dnv("gB", n))
                four(("gcb", n), lambda o, hd: mm(o, gB[:, hd, :], K("tri"), True, True))
                four(("beb", n), lambda o, hd: mm(o, bB[:, hd, :], K("ident"), True, True))
                ps = begin(("sm", n))
                for i, name in enumerate(("tri", "suffix", "chunk0", "chunk1")):
                    m = mm(ps[:, 4 * i:4 * i + 4], K(name), g[:, n, :], True, True)
                m.then_inc(s_res, 1)
                aside()
                pe.wait_ge(s_dn, dnv("qg", n))
                four(("N0", n), lambda o, hd: mm(o, qkv[:, 4 + hd, tok], kb[:, hd, :], True, True))
                four(("A0", n), lambda o, hd: mm(o, qkv[:, 4 + hd, tok], qkv[:, hd, tok], True, True))
                aside()
                pe.wait_ge(s_dn, dnv("U", n))
                four(("T1", n), lambda o, hd: nc.tensor.transpose(o, U[:, hd, :], K("ident")))
                four(("kt", n), lambda o, hd: nc.tensor.transpose(o, qkv[:, 4 + hd, tok], K("ident")))
                four(("vt", n), lambda o, hd: nc.tensor.transpose(o, qkv[:, 8 + hd, tok], K("ident")))
                aside()
                for l in range(5):
                    pe.wait_ge(s_dn, dnv(f"Ns{l}", n))
                    if l:
                        wait_evac(pe, ("dT", n, l - 1))
                    four(("Y", n, l), lambda o, hd: mm(o, Ns[l % 2][:, hd, :], Tm[:, hd, :], True, True))
                    aside()
                    wait_evac(pe, ("Y", n, l))
                    if l:
                        wait_evac(pe, ("dU", n, l - 1))
                    if l < 4:
                        four(("dT", n, l), lambda o, hd: mm(o, U[:, hd, :], Y[:, hd, :], True, True))
                    four(("dU", n, l), lambda o, hd: mm(o, Y[:, hd, :], U[:, hd, :], True, True))
                    aside()
                wait_evac(pe, ("dU", n, 4))
                wait_evac(pe, ("vt", n))
                four(("u", n), lambda o, hd: mm(o, U[:, hd, :], vb[:, hd, :], True, True))
                four(("wT", n), lambda o, hd: mm(o, kbg[:, hd, :], U[:, hd, :], True, True))
                aside()
                for c in range(2):
                    rr = slice(c * CH, c * CH + CH)
                    i = 2 * n + c
                    if i:
                        wait_evac(pe, ("dS", (i - 1) // 2, (i - 1) % 2))
                        wait_evac(pe, ("wT", n))
                        ps = begin(("wS", n, c))
                        for hd in range(4):
                            m = mm(ps[rr, hd * P:hd * P + P], wT[:, hd, rr], state[:, hd, :], True, True)
                        m.then_inc(s_res, 1)
                    aside()
                    if i:
                        wait_evac(pe, ("wS", n, c))
                    else:
                        wait_evac(pe, ("u", n))
                    vn = vnew if i else u
                    ps = begin(("o", n, c))
                    for hd in range(4):
                        if i:
                            mm(ps[:, hd * CH:hd * CH + CH], state[:, hd, :], qg[:, hd, rr], True, False)
                        m = mm(ps[:, hd * CH:hd * CH + CH], vn[rr, hd, :], AT[rr, hd, rr], i == 0, True)
                    m.then_inc(s_res, 1)
                    if i < 2 * NQ - 1:
                        four(("dS", n, c), lambda o, hd: mm(o, kdec[rr, hd, :], vn[rr, hd, :], True, True))
                    aside()
            while point[0] < LAST_POINT:
                aside()
            for i in HEADS_OUT:
                if i not in HO_POINT:
                    sums(("ho", i), 1, T)
            for j in range(KD):
                dense(("wo", j), [(0, 0, T)], made_before=8 if j == 0 else None, order=HEADS_OUT, x=(mixed_hi, mixed_lo))

            def ffn(i, parts):
                wide = len(parts) == 2
                total(("norm", 2 * i - 1), KD, TT if wide else T)
                b0 = BLOCK[("gate", i, 0)]
                x0 = xlo[0]
                xlo[0] += KD + KF
                with pe.Fori(0, KF // 2) as g:
                    for j in range(4):
                        key, b = (("gate", "up")[j % 2], i, j // 2), b0 + j
                        free, v = evac_at(key)
                        pe.wait_ge(free, g + (v - 1))
                        pe.wait_ge(s_lo, g * 4 + (b + 1))
                        for k in range(KD):
                            if j == 0:
                                pe.wait_ge(s_xlo, x0 + k + 1)
                            w = (w_hi[b % RING][:, k * P:k * P + P], w_lo[b % RING][:, k * P:k * P + P])
                            for o, a0, a1 in parts:
                                m = mm3(slot(key)[:, o:o + a1 - a0], w, (x_hi[:, k, a0:a1], x_lo[:, k, a0:a1]), k == 0, k == KD - 1)
                        m.then_inc(s_used, 1)
                pe.wait_ge(s_xlo, xlo[0] - 2)
                b1 = BLOCK[("down", i, 0)]
                with pe.Fori(0, 2) as g:
                    for j in range(4):
                        key = ("down", i, j)
                        free, v = evac_at(key)
                        pe.wait_ge(free, g + (v - 1))
                        for q in range(3):
                            b = b1 + 3 * j + q
                            pe.wait_ge(s_lo, g * 12 + (b + 1))
                            for kk in range(min(8, KF - 8 * q)):
                                k = 8 * q + kk
                                if j == 0 and k >= KF - 2:
                                    pe.wait_ge(s_xlo, xlo[0] - (KF - 1 - k))
                                w = (w_hi[b % RING][:, kk * P:kk * P + P], w_lo[b % RING][:, kk * P:kk * P + P])
                                for o, a0, a1 in parts:
                                    m = mm3(slot(key)[:, o:o + a1 - a0], w, (f_hi[:, k, a0:a1], f_lo[:, k, a0:a1]), k == 0, k == KF - 1)
                            m.then_inc(s_used, 1)

            def wide(keys, meta):
                sl = [begin(k) for k in keys]
                b = BLOCK[keys[-1]]
                for i in range(4):
                    pe.wait_ge(s_lo, b + i + 1)
                    w = (w_hi[(b + i) % RING], w_lo[(b + i) % RING])
                    for kk in range(2):
                        k = 2 * i + kk
                        for n in range(NQ + meta):
                            tk = slice(n * P, min(n * P + P, TT))
                            out = sl[n // 2][:, (n % 2) * 512:(n % 2) * 512 + 512] if n < NQ else sl[2][0:M, 0:512]
                            m = mm3(out, (x_hi[:, k, tk], x_lo[:, k, tk]),
                                    (w[0][:, kk * 512:kk * 512 + 512], w[1][:, kk * 512:kk * 512 + 512]), k == 0, k == KD - 1)
                    m.then_inc(s_used, 1)
            xlo = [16]
            ffn(1, ALL)
            total(("norm", 2), KD, TT)
            dense(("ik",), SEQ, made_before=xlo[0])
            xlo[0] += KD
            few("iw")
            for j in range(4):
                dense(("iq", j), SEQ)
            wait_evac(pe, ("ik",))
            def unit(key, n, k, _):
                if key[0] != "av":
                    b = BLOCK[key]
                    if k == 0:
                        begin(key)
                        pe.wait_ge(s_lo, b + 1)
                    w = (w_hi[b % RING][:, k * P:k * P + P], w_lo[b % RING][:, k * P:k * P + P])
                    for o, c0, c1 in (ALL if key[0] == "ak" else SEQ):
                        m = mm3(slot(key)[:, o:o + c1 - c0], w, (x_hi[:, k, c0:c1], x_lo[:, k, c0:c1]), k == 0, k == KD - 1)
                    if k == KD - 1:
                        m.then_inc(s_used, 1)
                    return
                if k == 0 and n % NQ == 0:
                    begin(key)
                b = BLOCK[("av", key[1], 1)] + k // 4
                if n == 0:
                    pe.wait_ge(s_lo, b + 1)
                tk = slice(M + n * P, M + n * P + P) if n < NQ else slice(0, M)
                out = slot(key)[:, n * 256:n * 256 + 256] if n < NQ else slot(key)[0:M, 0:256]
                a = slice(k % 4 * 256, k % 4 * 256 + 256)
                m = mm3(out, (x_hi[:, k, tk], x_lo[:, k, tk]), (w_hi[b % RING][:, a], w_lo[b % RING][:, a]), k == 0, k == KD - 1)
                if n == NQ and k % 4 == 3:
                    m.then_inc(s_used, 1)
                elif (n, k) == (NQ - 1, KD - 1):
                    m.then_inc(s_res, 1)
            for s in range(IX_STEPS):
                n, j = 1 + s // 4, s % 4
                wait_evac(pe, ("iq", j))
                ps = begin(("is", n, j))
                for a in range(2):
                    r = slice(64 * a, 64 * a + 64)
                    m = mm(ps[:, a * 512:a * 512 + (n + 1) * P], iq[r, j, n * P:n * P + P], ik[r, 0:(n + 1) * P], True, True)
                m.then_inc(s_res, 1)
                if s in IX_BESIDE:
                    for piece in projection_units(0):
                        if piece[0] == projection_keys(0)[IX_BESIDE.index(s)][0]:
                            unit(*piece)
            for piece in projection_units(0):
                if piece[0] not in [key for key, _ in projection_keys(0)[:len(IX_BESIDE)]]:
                    unit(*piece)
            for j in range(4):
                dense(("ga", j), SEQ)
            for s in range(ATT_STEPS + 2):
                if s < ATT_STEPS:
                    pair, j, n = s // PAIR_STEPS, s // NQ % 2, s % NQ
                    if n == 0:
                        wait_evac(pe, ("aq", pair, j))
                        wait_evac(pe, ("ak", pair, j))
                    w = M + (n + 1) * P
                    ps = begin(("AS", s))
                    for a0, a1 in ((0, min(w, 512)), (512, w)):
                        if a1 > a0:
                            m = mm(ps[:, a0:a1], aq[pair % 2][:, j, n * P:n * P + P], ak[pair % 2][:, j, a0:a1], True, True)
                    m.then_inc(s_res, 1)
                for piece in FILL.get(2 * s, []):
                    unit(*piece)
                if 1 <= s <= ATT_STEPS:
                    e = s - 1
                    n, i = e % NQ, e % 2
                    pe.wait_ge(s_afp, e + 1)
                    ps = begin(("AP", e))
                    nc.tensor.transpose(ps[0:M, 0:P], Ax[i][:, 0:M], K("ident"))
                    for kt in range(n + 1):
                        m = nc.tensor.transpose(ps[:, (kt + 1) * P:(kt + 2) * P], Ax[i][:, M + kt * P:M + kt * P + P], K("ident"))
                    m.then_inc(s_res, 1)
                for piece in FILL.get(2 * s + 1, []):
                    unit(*piece)
                if s >= 2:
                    e = s - 2
                    pair, j, n, i = e // PAIR_STEPS, e // NQ % 2, e % NQ, e % 2
                    if e % PAIR_STEPS == 0:
                        wait_evac(pe, ("av", pair, 0))
                        wait_evac(pe, ("av", pair, 1))
                    wait_evac(pe, ("AP", e))
                    ps = begin(("AV", e))
                    mm(ps[:, 0:P], avm[pair % 2][0:M, j * P:j * P + P], At[i][0:M, 0:P], True, False)
                    for kt in range(n + 1):
                        m = mm(ps[:, 0:P], av[pair % 2][:, kt, j * P:j * P + P], At[i][:, (kt + 1) * P:(kt + 2) * P], False, kt == n)
                    m.then_inc(s_res, 1)
            wait_evac(pe, ("AV", ATT_STEPS - 1))
            for j in range(KD):
                dense(("ao", j), [(0, 0, T)], (att_hi, att_lo))
            for hd in range(RET_H):
                for j in range(1 if hd else 0, 2):
                    dense(("rq", hd, j), SEQ)
                for j in range(2):
                    dense(("rk", hd, j), ALL)
                wide([("rv", hd, i) for i in range(3)], 1)
                dense(("rg", hd, 0), SEQ)
                pe.wait_ge(s_rotd, 2 * hd + 2)
                for kt in range(NQ + 1):
                    ps = begin(("rs", hd, kt))
                    keys = slice(kt * P, min(kt * P + P, TT))
                    q0 = max(kt * P - M, 0)
                    out = ps[0:keys.stop - keys.start, 0:T - q0]
                    for d in range(2):
                        m = mm(out, rqk[:, 2 + d, keys], rqk[:, d, q0:T], d == 0, d == 1)
                    m.then_inc(s_res, 1)
                dense(("rg", hd, 1), SEQ)
                for i in range(3):
                    wait_evac(pe, ("rv", hd, i))
                pe.wait_ge(s_rst, 5 * hd + 5)
                for d in range(4):
                    ps = begin(("ry", hd, d))
                    for kt in range(NQ):
                        q0 = max(kt * P - M, 0)
                        mm(ps[:, q0:T], rv[:, kt, d * P:d * P + P], rst[:, kt, q0:T], kt == 0, False)
                    m = mm(ps[:, T - M:T], rvm[0:M, d * P:d * P + P], rstm[0:M, 0:M], False, True)
                    m.then_inc(s_res, 1)
                dense(("rg", hd, 2), SEQ)
                total(("rn", hd), 4, T)
                dense(("rg", hd, 3), SEQ)
                if hd + 1 < RET_H:
                    dense(("rq", hd + 1, 0), SEQ)
                for j in range(KD):
                    key = ("wr", hd, j)
                    ps = begin(key)
                    b = BLOCK[key]
                    pe.wait_ge(s_lo, b + 1)
                    w = (w_hi[b % RING], w_lo[b % RING])
                    for k in range(4):
                        pe.wait_ge(s_xlo, xlo[0] + k + 1)
                        a = (j % 2) * 512 + k * P
                        m = mm3(ps[:, 0:T], (w[0][:, a:a + P], w[1][:, a:a + P]), (y_hi[:, k, :], y_lo[:, k, :]), k == 0, k == 3)
                    m.then_inc(s_used if j % 2 else s_res, 1)
                xlo[0] += 4
            for j in range(KD):
                dense(("gr", j), SEQ)
            for j in range(KD):
                dense(("mx", j), [(0, 0, T)], x=(merged_hi, merged_lo), made_before=xlo[0] if j == 0 else None)
            xlo[0] += KD
            ffn(2, SEQ)
            total(("norm", 4), KD, T)

        @block.gpsimd
        def _(pool):
            with pool.Fori(0, BLOCKS_PADDED // RING) as i:
                for j in range(RING):
                    pool.wait_ge(s_hi, i * RING + (j + 1))
                    nc.gpsimd.tensor_tensor(w_lo[j][:], w_raw[j][:], w_hi[j][:].bitcast(F32),
                                            ALU.subtract).then_inc(s_lo, 1)


def stream(inp):
    z = np.zeros
    w_in, w_out = inp["w_in"][0], inp["w_out"][0]
    blocks = []

    def cols(w):
        k = w.shape[0]
        w = w.reshape(k // P, P, w.shape[1]).transpose(1, 0, 2)
        blocks.append(np.ascontiguousarray(w.reshape(P, -1)))

    def wide(w):
        w = w.reshape(4, 2, P, 512).transpose(0, 2, 1, 3).reshape(4, P, 1024)
        blocks.extend(np.ascontiguousarray(w))
    o = np.cumsum([0, 512, 512, 512, 512, 4, 4, 512, 512, 512, 512])
    for at in (o[0], o[1], o[2]):
        for j in range(4):
            cols(w_in[:, at + j * P:at + j * P + P])
    gates = z((D, P), np.float32)
    gates[:, 0:8] = w_in[:, o[4]:o[6]]
    cols(gates)
    wide(w_in[:, o[8]:o[9]])
    for at in (o[6], o[7], o[9], o[3]):
        for j in range(4):
            cols(w_in[:, at + j * P:at + j * P + P])
    for j in range(8):
        cols(w_out[:, j * P:j * P + P])
    fit = lambda w: np.concatenate([w, z((w.shape[0], P - w.shape[1]), np.float32)], 1)

    def ffn(i):
        gate, up, down = (inp[f"ffn{i}_w_{n}_2"][0] for n in ("gate", "up", "down"))
        for f in range(KF):
            cols(gate[:, f * P:f * P + P])
            cols(up[:, f * P:f * P + P])
        for d in range(KD):
            w = np.concatenate([down[:, d * P:d * P + P], z((24 * P - D_FF, P), np.float32)])
            for q in range(3):
                cols(w[q * 1024:q * 1024 + 1024])
    ffn(1)
    w2 = inp["w_in_2"][0]
    names = ("rq", "rk", "rv", "rg", "aq", "ak", "av", "iq", "ik", "iw", "gr", "ga")
    sizes = (1024, 1024, 2048, 2048, 1024, 1024, 1024, 512, 64, 8, 1024, 1024)
    start = dict(zip(names, np.cumsum([0, *sizes])))
    part = lambda name, c, n: w2[:, start[name] + c:start[name] + c + n]
    cols(np.concatenate([part("ik", 0, 64)] * 2, 1))
    cols(fit(part("iw", 0, 8)))
    for j in range(4):
        cols(part("iq", j * P, P))
    for g in range(ATT_H // 2 + 1):
        if g < ATT_H // 2:
            for j in range(2):
                for name in ("ak", "aq"):
                    cols(part(name, g * 256 + j * P, P))
            w = part("av", g * 256, 256)
            blocks.extend(np.ascontiguousarray(w.reshape(2, 4, P, 256).transpose(0, 2, 1, 3).reshape(2, P, 1024)))
        if g in (0, ATT_H // 2):
            for j in range(4):
                cols(part("ga", (4 if g else 0) * P + j * P, P))
    for j in range(KD):
        cols(inp["w_att_out_2"][0][:, j * P:j * P + P])
    for hd in range(RET_H):
        for name, j in (("rq", 0), ("rq", 1), ("rk", 0), ("rk", 1)):
            if not (hd and (name, j) == ("rq", 0)):
                cols(part(name, hd * 256 + j * P, P))
        wide(part("rv", hd * 512, 512))
        for j in range(4):
            cols(part("rg", hd * 512 + j * P, P))
        if hd + 1 < RET_H:
            cols(part("rq", (hd + 1) * 256, P))
        w = inp["w_ret_out_2"][0][hd * 512:hd * 512 + 512]
        for j in range(0, KD, 2):
            blocks.append(np.ascontiguousarray(
                w.reshape(4, P, KD, P)[:, :, j:j + 2].transpose(1, 2, 0, 3).reshape(P, 1024)))
    for j in range(KD):
        cols(part("gr", j * P, P))
    for j in range(KD):
        cols(inp["w_mix_out_2"][0][:, j * P:j * P + P])
    ffn(2)
    assert len(blocks) == BLOCKS, (len(blocks), BLOCKS)
    while len(blocks) < BLOCKS_PADDED:
        blocks.append(z((P, 1024), np.float32))
    return np.stack(blocks).reshape(BLOCKS_PADDED // RING, RING, P, 1024)


def small_inputs(inp):
    a = np.zeros((P, N_SMALL), np.float32)

    def put(name, v):
        v = np.asarray(v)
        a[:v.shape[0], SMALL[name][0]:SMALL[name][0] + v.shape[1]] = v
    col = lambda v: v.reshape(-1, P).T
    put("norm_gain", col(inp["norm_gain"][0]))
    put("conv", inp["conv_w"][0].reshape(4, 12, P).transpose(2, 1, 0).reshape(P, 48))
    put("dn_gain", col(inp["dn_out_gain"][0]))
    put("q_gain", np.concatenate([inp["q_gain"][0]] * 2)[:, None])
    put("k_gain", np.concatenate([inp["k_gain"][0]] * 2)[:, None])
    put("df_gain", col(inp["df_out_gain"][0]))
    put("a_log", np.broadcast_to(inp["a_log"][0], (P, 4)))
    put("dt_bias", np.broadcast_to(inp["dt_bias"][0], (P, 4)))
    for n, m in (("lq1", "lambda_q1"), ("lk1", "lambda_k1"), ("lq2", "lambda_q2"), ("lk2", "lambda_k2")):
        put(n, inp[m][0][:, None])
    put("f1_gain", col(inp["ffn1_norm_2"][0]))
    put("mix_gain", col(inp["mix_norm_2"][0]))
    put("f2_gain", col(inp["ffn2_norm_2"][0]))
    put("final_gain", col(inp["final_norm_2"]))
    return a


def kernel(**inputs):
    import concourse.bacc as bacc
    from concourse.bass_utils import run_bass_kernel_spmd as run

    inp = {k: np.asarray(v) for k, v in inputs.items()}
    feature_major = lambda a: np.ascontiguousarray(a.T.reshape(KD, P, -1).transpose(1, 0, 2))
    arrays = {
        "weights": stream(inp),
        "x_t": feature_major(inp["x"][0]),
        "meta_t": feature_major(inp["meta_tokens_2"]),
        "consts": constants(),
        "small_in": small_inputs(inp),
        "rotations": rotations(),
        "decays": retention_decay(),
    }
    nc = bacc.Bacc("TRN2", target_bir_lowering=False, num_devices=1)
    args = [nc.dram_tensor(n, a.shape, F32, kind="ExternalInput").ap() for n, a in arrays.items()]
    out = nc.dram_tensor("out", (P, KD, T), F32, kind="ExternalOutput").ap()
    build(nc, *args, out)
    r = run(nc, [arrays], core_ids=[0])
    y = r.results[0]["out"]
    return np.ascontiguousarray(y.transpose(1, 0, 2).reshape(D, T).T)[None]
```
